# Optimizing a Trainium2 kernel written in Bass

```python
import math
import jax, jax.numpy as jnp
from jax import lax
import numpy as np

D_MODEL = 1024
BATCH = 1
SEQ = 512
DEPTH = 2
DEC_BATCH = 8
DEC_SEQ = 8
PAST_LEN = 2048
PAGE_SIZE = 128

N_META = 16
MLA_HEADS = 8
MLA_Q_RANK = 256
MLA_KV_RANK = 128
MLA_NOPE = 64
MLA_ROPE = 32
MLA_V = 64
MLA_SCALE = (MLA_NOPE + MLA_ROPE) ** -0.5
ROPE_THETA = 10000.0
Q_BLOCK = 128
GLA_HEADS = 4
GLA_DK = 32
GLA_DV = 64
GLA_GATE_RANK = 16
GLA_TAU = 16.0
ML_HEADS = 4
ML_DH = 64
ML_WIDTH = ML_HEADS * ML_DH
CONV_W = 4
CHUNK = 64
MIX_WIDTH = MLA_HEADS * MLA_V + GLA_HEADS * GLA_DV + ML_WIDTH
N_EXPERTS = 16
N_GROUPS = 4
E_PER_GROUP = N_EXPERTS // N_GROUPS
TOP_K = 2
D_EXPERT = 256
ALPHA = (2 * DEPTH) ** 0.25
BETA = (8 * DEPTH) ** -0.25
LN_EPS = 1e-5
RMS_EPS = 1e-6
IN_SIZES = (MLA_Q_RANK, MLA_KV_RANK, MLA_ROPE,
            GLA_HEADS * GLA_DK, GLA_HEADS * GLA_DK, GLA_HEADS * GLA_DV, GLA_GATE_RANK, GLA_HEADS * GLA_DV,
            ML_WIDTH, ML_WIDTH, ML_HEADS, ML_HEADS, ML_WIDTH)
D_IN = sum(IN_SIZES)

kernel_name = 'hybrid_mla_gla_mlstm_moe_step'

def layer_norm(x, g, b):
    xf = x.astype(jnp.float32)
    mu = jnp.mean(xf, -1, keepdims=True)
    var = jnp.mean(jnp.square(xf - mu), -1, keepdims=True)
    return ((xf - mu) * lax.rsqrt(var + LN_EPS) * g + b).astype(x.dtype)

def rms_norm(x, g):
    xf = x.astype(jnp.float32)
    return (xf * lax.rsqrt(jnp.mean(xf * xf, -1, keepdims=True) + RMS_EPS) * g).astype(x.dtype)

def head_norm(x):
    xf = x.astype(jnp.float32)
    mu = jnp.mean(xf, -1, keepdims=True)
    var = jnp.mean(jnp.square(xf - mu), -1, keepdims=True)
    return (xf - mu) * lax.rsqrt(var + LN_EPS)

def rope(x, pos):
    half = x.shape[-1] // 2
    inv = ROPE_THETA ** (-jnp.arange(half, dtype=jnp.float32) / half)
    ang = pos.astype(jnp.float32)[:, None] * inv
    ang = ang.reshape(ang.shape[:1] + (1,) * (x.ndim - 3) + (half,))
    cos, sin = jnp.cos(ang), jnp.sin(ang)
    xf = x.astype(jnp.float32)
    x1, x2 = xf[..., :half], xf[..., half:]
    return jnp.concatenate([x1 * cos - x2 * sin, x2 * cos + x1 * sin], -1).astype(x.dtype)

def mla_scores(q_lat, q_rope, c, kr):
    s = jnp.einsum('bqhr,bkr->bhqk', q_lat, c) + jnp.einsum('bqhe,bke->bhqk', q_rope, kr)
    return s.astype(jnp.float32) * MLA_SCALE

def mla_prompt_attend(q_lat, q_rope, c, kr):
    B, L = c.shape[:2]
    nb = -(-L // Q_BLOCK)
    pad = nb * Q_BLOCK - L

    def blocks(a):
        a = jnp.pad(a, ((0, 0), (0, pad), (0, 0), (0, 0)))
        return jnp.moveaxis(a.reshape((B, nb, Q_BLOCK) + a.shape[2:]), 1, 0)

    kpos = jnp.arange(L)

    def one_block(args):
        ql, qr, i = args
        s = mla_scores(ql, qr, c, kr)
        qpos = i * Q_BLOCK + jnp.arange(Q_BLOCK)
        s = jnp.where(kpos[None, :] <= qpos[:, None], s, -jnp.inf)
        p = jax.nn.softmax(s, axis=-1).astype(c.dtype)
        return jnp.einsum('bhqk,bkr->bqhr', p, c)

    o = lax.map(one_block, (blocks(q_lat), blocks(q_rope), jnp.arange(nb)))
    o = jnp.moveaxis(o, 0, 1).reshape(B, nb * Q_BLOCK, MLA_HEADS, MLA_KV_RANK)
    return o[:, :L]

def mla_sample_attend(q_lat, q_rope, c_new, kr_new, c_past, kr_past):
    T = c_new.shape[1]
    s_past = mla_scores(q_lat, q_rope, c_past, kr_past)
    s_new = mla_scores(q_lat, q_rope, c_new, kr_new)
    s_new = jnp.where(jnp.tril(jnp.ones((T, T), bool)), s_new, -jnp.inf)
    m = jnp.maximum(s_past.max(-1, keepdims=True), s_new.max(-1, keepdims=True))
    e_past = jnp.exp(s_past - m)
    e_new = jnp.exp(s_new - m)
    z = e_past.sum(-1, keepdims=True) + e_new.sum(-1, keepdims=True)
    return (jnp.einsum('bhqk,bkr->bqhr', (e_past / z).astype(c_past.dtype), c_past)
            + jnp.einsum('bhqk,bkr->bqhr', (e_new / z).astype(c_new.dtype), c_new))

def gla_chunk(S, q, k, v, la):
    C = q.shape[1]
    b = jnp.cumsum(la, axis=1)
    causal = jnp.tril(jnp.ones((C, C), bool))[None, :, :, None, None]
    diff = jnp.where(causal, b[:, :, None] - b[:, None, :], -jnp.inf)
    A = jnp.einsum('bthk,bshk,btshk->bhts', q, k, jnp.exp(diff))
    intra = jnp.einsum('bhts,bshv->bthv', A, v)
    inter = jnp.einsum('bthk,bhkv->bthv', q * jnp.exp(b), S)
    bl = b[:, -1]
    S = jnp.exp(bl)[..., None] * S + jnp.einsum('bshk,bshv->bhkv', k * jnp.exp(bl[:, None] - b), v)
    return S, intra + inter

def mlstm_chunk(state, q, k, v, ig, lf):
    Cs, ns, ms = state
    C = q.shape[1]
    F = jnp.cumsum(lf, axis=1)
    a = F + ms[:, None]
    causal = jnp.tril(jnp.ones((C, C), bool))[None, :, :, None]
    d = jnp.where(causal, F[:, :, None] - F[:, None, :] + ig[:, None], -jnp.inf)
    m = jnp.maximum(a, d.max(axis=2))
    wp = jnp.exp(a - m)
    W = jnp.exp(d - m[:, :, None])
    qk = jnp.einsum('bthd,bshd->btsh', q, k) * W
    num = wp[..., None] * jnp.einsum('bthk,bhkv->bthv', q, Cs) + jnp.einsum('btsh,bshv->bthv', qk, v)
    den = wp * jnp.einsum('bthk,bhk->bth', q, ns) + qk.sum(2)
    h = num / jnp.maximum(jnp.abs(den), jnp.exp(-m))[..., None]
    m_last = m[:, -1]
    wl = jnp.exp(F[:, -1] + ms - m_last)
    ws = jnp.exp(F[:, -1][:, None] - F + ig - m_last[:, None])
    Cs = wl[..., None, None] * Cs + jnp.einsum('bsh,bshk,bshv->bhkv', ws, k, v)
    ns = wl[..., None] * ns + jnp.einsum('bsh,bshk->bhk', ws, k)
    return (Cs, ns, m_last), h

def _scan_chunks(chunk_fn, state, inputs, c):
    B, T = inputs[0].shape[:2]
    n = T // c
    xs = [jnp.moveaxis(a.reshape((B, n, c) + a.shape[2:]), 1, 0) for a in inputs]
    state, ys = lax.scan(lambda s, xi: chunk_fn(s, *xi), state, xs)
    ys = jnp.moveaxis(ys, 0, 1)
    return state, ys.reshape((B, T) + ys.shape[3:])

def run_chunks(chunk_fn, state, inputs, lead, chunk):
    outs = []
    if lead:
        state, y = _scan_chunks(chunk_fn, state, [a[:, :lead] for a in inputs], lead)
        outs.append(y)
        inputs = [a[:, lead:] for a in inputs]
    state, y = _scan_chunks(chunk_fn, state, inputs, chunk)
    outs.append(y)
    return state, jnp.concatenate(outs, axis=1)

def mixer_block(h, pos, lead, chunk, lw, past):
    (w_in, mla_q_norm, mla_w_uq, mla_kv_norm, mla_w_ukv, gla_w_a, gla_b_a, gla_norm,
     ml_conv_w, ml_conv_b, ml_w_q, ml_w_k, ml_b_i, ml_b_f, ml_norm, ml_skip, w_out) = lw
    B, T, _ = h.shape
    f32 = jnp.float32
    (cq, ckv, kr, gq, gk, gv, ga, gr, mu, mv, mi, mf, mo) = jnp.split(
        h @ w_in, np.cumsum(IN_SIZES)[:-1].tolist(), axis=-1)

    q = (rms_norm(cq, mla_q_norm) @ mla_w_uq).reshape(B, T, MLA_HEADS, MLA_NOPE + MLA_ROPE)
    q_nope, q_rope = q[..., :MLA_NOPE], rope(q[..., MLA_NOPE:], pos)
    c_kv = rms_norm(ckv, mla_kv_norm)
    k_rope = rope(kr, pos)
    w_ukv = mla_w_ukv.reshape(MLA_KV_RANK, MLA_HEADS, MLA_NOPE + MLA_V)
    q_lat = jnp.einsum('bthn,rhn->bthr', q_nope, w_ukv[..., :MLA_NOPE])
    if past is None:
        o_lat = mla_prompt_attend(q_lat, q_rope, c_kv, k_rope)
    else:
        o_lat = mla_sample_attend(q_lat, q_rope, c_kv, k_rope, past[0], past[1])
    o_mla = jnp.einsum('bthr,rhv->bthv', o_lat, w_ukv[..., MLA_NOPE:]).reshape(B, T, -1)

    la = (jax.nn.log_sigmoid((ga @ gla_w_a + gla_b_a).astype(f32)) / GLA_TAU).reshape(B, T, GLA_HEADS, GLA_DK)
    gla_in = (gq.reshape(B, T, GLA_HEADS, GLA_DK).astype(f32) * GLA_DK ** -0.5,
              gk.reshape(B, T, GLA_HEADS, GLA_DK).astype(f32),
              gv.reshape(B, T, GLA_HEADS, GLA_DV).astype(f32), la)
    S0 = jnp.zeros((B, GLA_HEADS, GLA_DK, GLA_DV), f32) if past is None else past[2].astype(f32)
    S_new, o = run_chunks(gla_chunk, S0, gla_in, lead, chunk)
    o_gla = (rms_norm(o, gla_norm) * jax.nn.silu(gr.reshape(B, T, GLA_HEADS, GLA_DV).astype(f32)))
    o_gla = o_gla.reshape(B, T, -1).astype(h.dtype)

    buf = jnp.zeros((B, CONV_W - 1, ML_WIDTH), mu.dtype) if past is None else past[6].astype(mu.dtype)
    up = jnp.concatenate([buf, mu], axis=1)
    uc = ml_conv_b
    for i in range(CONV_W):
        uc = uc + up[:, i:i + T] * ml_conv_w[i]
    uc = jax.nn.silu(uc)
    uch = uc.reshape(B, T, ML_HEADS, ML_DH)
    mq = jnp.einsum('bthd,hde->bthe', uch, ml_w_q).astype(f32)
    mk = (jnp.einsum('bthd,hde->bthe', uch, ml_w_k) * ML_DH ** -0.5).astype(f32)
    mvv = mv.reshape(B, T, ML_HEADS, ML_DH).astype(f32)
    ig = (mi + ml_b_i).astype(f32)
    lf = jax.nn.log_sigmoid((mf + ml_b_f).astype(f32))
    if past is None:
        st0 = (jnp.zeros((B, ML_HEADS, ML_DH, ML_DH), f32), jnp.zeros((B, ML_HEADS, ML_DH), f32),
               jnp.zeros((B, ML_HEADS), f32))
    else:
        st0 = (past[3].astype(f32), past[4].astype(f32), past[5].astype(f32))
    (Cs, ns, ms), hc = run_chunks(mlstm_chunk, st0, (mq, mk, mvv, ig, lf), lead, chunk)
    hc = hc * jax.nn.sigmoid(mo.astype(f32)).reshape(B, T, ML_HEADS, ML_DH)
    o_ml = (head_norm(hc) * ml_norm.reshape(ML_HEADS, ML_DH)).reshape(B, T, -1) + ml_skip * uc

    y = jnp.concatenate([o_mla, o_gla, o_ml.astype(h.dtype)], axis=-1) @ w_out
    return y, (c_kv, k_rope, S_new, Cs, ns, ms, up[:, -(CONV_W - 1):])

def moe(x, router_w, router_bias, w_gate, w_up, w_down):
    B, T, D = x.shape
    xt = x.reshape(-1, D)
    scores = jax.nn.sigmoid((xt @ router_w).astype(jnp.float32))
    sel = (scores + router_bias.astype(jnp.float32)).reshape(-1, N_GROUPS, E_PER_GROUP)
    g = jnp.argmax(lax.top_k(sel, TOP_K)[0].sum(-1), axis=-1)
    gmask = jnp.arange(N_GROUPS)[None, :] == g[:, None]
    masked = jnp.where(gmask[:, :, None], sel, -jnp.inf).reshape(-1, N_EXPERTS)
    _, idx = lax.top_k(masked, TOP_K)
    gate = jnp.take_along_axis(scores, idx, axis=-1)
    gate = gate / gate.sum(-1, keepdims=True)
    w = (jax.nn.one_hot(idx, N_EXPERTS, dtype=jnp.float32) * gate[..., None]).sum(1)
    hg = jnp.einsum('nd,edf->nef', xt, w_gate)
    hu = jnp.einsum('nd,edf->nef', xt, w_up)
    hh = jax.nn.silu(hg) * hu * w[:, :, None].astype(x.dtype)
    return jnp.einsum('nef,efd->nd', hh, w_down).reshape(B, T, D)

def trunk(x, pos, lead, chunk, past_fn, layer_w, norm_w, moe_w, router):
    ln1_g, ln1_b, ln2_g, ln2_b = norm_w
    states = []
    for l in range(DEPTH):
        past = None if past_fn is None else past_fn(l)
        y, st = mixer_block(x, pos, lead, chunk, tuple(a[l] for a in layer_w), past)
        x = layer_norm(ALPHA * x + y, ln1_g[l], ln1_b[l])
        x = layer_norm(ALPHA * x + moe(x, router[0], router[1], *(a[l] for a in moe_w)), ln2_g[l], ln2_b[l])
        states.append(st)
    return x, tuple(jnp.stack(s) for s in zip(*states))

def setup_inputs(seed: int = 0) -> dict:
    key = jax.random.key(seed)
    ks = list(jax.random.split(key, 48))

    def nrm(shape, scale=1.0):
        return jax.random.normal(ks.pop(), shape, jnp.float32) * scale

    n_pages = PAST_LEN // PAGE_SIZE
    n_pool = (DEC_BATCH * n_pages * 5) // 4
    page_table = jax.random.permutation(ks.pop(), n_pool)[:DEC_BATCH * n_pages]
    page_table = page_table.reshape(DEC_BATCH, n_pages).astype(jnp.int32)
    return {
        'x_prompt': nrm((BATCH, SEQ, D_MODEL)),
        'x_sample': nrm((DEC_BATCH, DEC_SEQ, D_MODEL)),
        'cache_kv_latent': nrm((DEPTH, n_pool, PAGE_SIZE, MLA_KV_RANK)),
        'cache_k_rope': nrm((DEPTH, n_pool, PAGE_SIZE, MLA_ROPE)),
        'state_gla': nrm((DEPTH, DEC_BATCH, GLA_HEADS, GLA_DK, GLA_DV)),
        'state_mlstm_C': nrm((DEPTH, DEC_BATCH, ML_HEADS, ML_DH, ML_DH)),
        'state_mlstm_n': nrm((DEPTH, DEC_BATCH, ML_HEADS, ML_DH)),
        'state_mlstm_m': nrm((DEPTH, DEC_BATCH, ML_HEADS)),
        'state_mlstm_conv': nrm((DEPTH, DEC_BATCH, CONV_W - 1, ML_WIDTH)),
        'page_table': page_table,
        'meta_tokens': nrm((N_META, D_MODEL)),
        'ln_in_g': 1.0 + nrm((D_MODEL,), 0.02),
        'ln_in_b': nrm((D_MODEL,), 0.02),
        'w_in': nrm((DEPTH, D_MODEL, D_IN), D_MODEL ** -0.5),
        'mla_q_norm': 1.0 + nrm((DEPTH, MLA_Q_RANK), 0.02),
        'mla_w_uq': nrm((DEPTH, MLA_Q_RANK, MLA_HEADS * (MLA_NOPE + MLA_ROPE)), MLA_Q_RANK ** -0.5),
        'mla_kv_norm': 1.0 + nrm((DEPTH, MLA_KV_RANK), 0.02),
        'mla_w_ukv': nrm((DEPTH, MLA_KV_RANK, MLA_HEADS * (MLA_NOPE + MLA_V)), MLA_KV_RANK ** -0.5),
        'gla_w_a': nrm((DEPTH, GLA_GATE_RANK, GLA_HEADS * GLA_DK), GLA_GATE_RANK ** -0.5),
        'gla_b_a': nrm((DEPTH, GLA_HEADS * GLA_DK), 0.1),
        'gla_norm': 1.0 + nrm((DEPTH, GLA_DV), 0.02),
        'ml_conv_w': nrm((DEPTH, CONV_W, ML_WIDTH), CONV_W ** -0.5),
        'ml_conv_b': nrm((DEPTH, ML_WIDTH), 0.02),
        'ml_w_q': nrm((DEPTH, ML_HEADS, ML_DH, ML_DH), ML_DH ** -0.5),
        'ml_w_k': nrm((DEPTH, ML_HEADS, ML_DH, ML_DH), ML_DH ** -0.5),
        'ml_b_i': nrm((DEPTH, ML_HEADS), 0.1),
        'ml_b_f': jnp.linspace(3.0, 6.0, ML_HEADS, dtype=jnp.float32)[None] + nrm((DEPTH, ML_HEADS), 0.1),
        'ml_norm': 1.0 + nrm((DEPTH, ML_WIDTH), 0.02),
        'ml_skip': 1.0 + nrm((DEPTH, ML_WIDTH), 0.02),
        'w_out': nrm((DEPTH, MIX_WIDTH, D_MODEL), MIX_WIDTH ** -0.5 * BETA),
        'ln1_g': 1.0 + nrm((DEPTH, D_MODEL), 0.02),
        'ln1_b': nrm((DEPTH, D_MODEL), 0.02),
        'ln2_g': 1.0 + nrm((DEPTH, D_MODEL), 0.02),
        'ln2_b': nrm((DEPTH, D_MODEL), 0.02),
        'router_w': nrm((D_MODEL, N_EXPERTS), D_MODEL ** -0.5),
        'router_bias': nrm((N_EXPERTS,), 0.01),
        'moe_w_gate': nrm((DEPTH, N_EXPERTS, D_MODEL, D_EXPERT), D_MODEL ** -0.5),
        'moe_w_up': nrm((DEPTH, N_EXPERTS, D_MODEL, D_EXPERT), D_MODEL ** -0.5),
        'moe_w_down': nrm((DEPTH, N_EXPERTS, D_EXPERT, D_MODEL), D_EXPERT ** -0.5 * BETA),
    }

def reference(x_prompt, x_sample, cache_kv_latent, cache_k_rope, state_gla, state_mlstm_C, state_mlstm_n,
              state_mlstm_m, state_mlstm_conv, page_table, meta_tokens, ln_in_g, ln_in_b, w_in, mla_q_norm,
              mla_w_uq, mla_kv_norm, mla_w_ukv, gla_w_a, gla_b_a, gla_norm, ml_conv_w, ml_conv_b, ml_w_q, ml_w_k,
              ml_b_i, ml_b_f, ml_norm, ml_skip, w_out, ln1_g, ln1_b, ln2_g, ln2_b, router_w, router_bias,
              moe_w_gate, moe_w_up, moe_w_down):
    layer_w = (w_in, mla_q_norm, mla_w_uq, mla_kv_norm, mla_w_ukv, gla_w_a, gla_b_a, gla_norm,
               ml_conv_w, ml_conv_b, ml_w_q, ml_w_k, ml_b_i, ml_b_f, ml_norm, ml_skip, w_out)
    norm_w = (ln1_g, ln1_b, ln2_g, ln2_b)
    moe_w = (moe_w_gate, moe_w_up, moe_w_down)
    router = (router_w, router_bias)

    B, S, D = x_prompt.shape
    meta = jnp.broadcast_to(meta_tokens[None].astype(x_prompt.dtype), (B, N_META, D))
    xp = layer_norm(jnp.concatenate([meta, x_prompt], axis=1), ln_in_g, ln_in_b)
    pos_p = jnp.arange(S + N_META)
    hp, (p_kv, p_kr, p_gla, p_C, p_n, p_m, p_conv) = trunk(
        xp, pos_p, N_META, CHUNK, None, layer_w, norm_w, moe_w, router)
    y_prompt = hp[:, N_META:]

    n_seq, T = x_sample.shape[:2]

    def sample_past(l):
        c_past = cache_kv_latent[l, page_table].reshape(n_seq, -1, MLA_KV_RANK)
        kr_past = cache_k_rope[l, page_table].reshape(n_seq, -1, MLA_ROPE)
        return (c_past, kr_past, state_gla[l], state_mlstm_C[l], state_mlstm_n[l], state_mlstm_m[l],
                state_mlstm_conv[l])

    xs = layer_norm(x_sample, ln_in_g, ln_in_b)
    pos_s = PAST_LEN + jnp.arange(T)
    y_sample, (s_kv, s_kr, s_gla, s_C, s_n, s_m, s_conv) = trunk(
        xs, pos_s, 0, T, sample_past, layer_w, norm_w, moe_w, router)

    return (y_prompt, y_sample, p_kv, p_kr, p_gla, p_C, p_n, p_m, p_conv,
            s_kv, s_kr, s_gla, s_C, s_n, s_m, s_conv)


_drawn_inputs = setup_inputs


def setup_inputs(seed=0):
    import zlib

    import numpy as np

    out = dict(_drawn_inputs(seed))
    spreads = {}
    factors = {'cache_k_rope': 8.0, 'mla_q_norm': 4.797, 'gla_norm': 3.768, 'ml_skip': 4.673}
    for name, (base, spread) in spreads.items():
        noise = np.random.default_rng([zlib.crc32(name.encode()), seed]).standard_normal(out[name].shape)
        drawn = base * np.exp(spread * noise) if base else spread * noise
        out[name] = __import__('jax').numpy.asarray(drawn.astype(out[name].dtype))
    for name, factor in factors.items():
        out[name] = (out[name] * factor).astype(out[name].dtype)
    return out
```

```python
from contextlib import ExitStack

import numpy as np
import concourse.bass as bass
from concourse import mybir

F32 = mybir.dt.float32
I32 = mybir.dt.int32
ALU = mybir.AluOpType
ACT = mybir.ActivationFunctionType
AX = mybir.AxisListType

P = 128
D = 1024
KD = D // P
DEPTH = 2
N_META, SEQ = 16, 512
TP = N_META + SEQ
NSEQ, TS = 8, 8
T = TP + NSEQ * TS
HALF = T // 2
TT = -(-T // P)
LAST = T - (TT - 1) * P
H = 8
LAT, ROPE, NOPE, MV = 128, 32, 64, 64
PAST, PAGE = 2048, 128
NPAGES = PAST // PAGE
POOL = NSEQ * NPAGES * 5 // 4
KEYS_ROW = 16
ROWS_PAGE = PAGE // KEYS_ROW
SCALE = float((NOPE + ROPE) ** -0.5)
GK, GV, GH = 32, 64, 4
GR = 16
TAU = 16.0
MH, DH = 4, 64
CONV = 4
C = 66
NCH = TP // C
NS = NSEQ * TS
E = 16
F = 256
ALPHA = float((2 * DEPTH) ** 0.25)
LN_EPS, RMS_EPS = 1e-5, 1e-6
NEG = -1.0e30
QT = 16
NQ = TP // QT
SH = [slice(0, HALF), slice(HALF, T)]
COL = dict(cq=0, ckv=256, kr=384, gq=416, gk=544, gv=672, ga=928, gr=944, mu=1200, mv=1456, mi=1712, mo=1720)
CHUNKS = [("cq", 0), ("cq", 1), ("ckv", 0), ("gq", 0), ("gk", 0), ("mu", 0), ("mu", 1), ("gv", 0), ("gv", 1),
          ("gr", 0), ("gr", 1), ("mv", 0), ("mv", 1), ("mo", 0), ("mo", 1)]
NSLOT = 4
SMALL = 104
VEC = [("q_norm", 2), ("kv_norm", 1), ("b_a", 1), ("gla_norm", 1), ("conv_w", 8), ("conv_b", 2), ("ml_norm", 2),
       ("ml_skip", 2), ("ln1_g", 8), ("ln1_b", 8), ("ln2_g", 8), ("ln2_b", 8)]
VROW, _n = {}, 0
for _k, _w in VEC:
    VROW[_k] = _n
    _n += DEPTH * _w
VROW["ln_in_g"] = _n
VROW["ln_in_b"] = _n + KD
NVEC = _n + 2 * KD
VW = dict(VEC)


def shape_constants():
    f = np.float32
    p = np.arange(P)
    out, at, n = [], {}, 0

    def put(name, a):
        nonlocal n
        a = np.asarray(a, f).reshape(a.shape[0], -1)
        full = np.zeros((P, a.shape[1]), f)
        full[:a.shape[0]] = a
        at[name] = (n, a.shape[1])
        n += a.shape[1]
        out.append(full)

    put("ident", np.eye(P))
    put("ones", np.ones((P, P)))
    put("block", (p[:, None] // 64 == p[None, :] // 64))
    k = np.arange(QT)
    put("mask_q", np.where(p[:, None] >= 8 * k[None, :], 0.0, NEG))
    put("mask_n", np.where((p[:, None] >= 8 * k[None, :]) & (p[:, None] // 64 == k[None, :] // 8), 0.0, NEG))
    s = np.arange(C)
    ok = s[:, None] <= s[None, :]
    put("tri", np.repeat(ok[:, None, :], 4, 1))
    put("trineg", np.where(np.repeat(ok[:, None, :], 4, 1), 0.0, NEG))
    s = np.arange(NS)
    ok = (s[:, None] <= s[None, :]) & (s[:, None] // TS == s[None, :] // TS)
    put("tri_s", np.repeat(ok[:, None, :], 4, 1))
    put("trineg_s", np.where(np.repeat(ok[:, None, :], 4, 1), 0.0, NEG))
    put("seqmask", s[:, None] // TS == np.arange(NSEQ)[None, :])
    put("rowsel", np.repeat(np.eye(4)[:, :, None], C, 2))
    put("negid", -np.eye(4))
    put("pairsel", (np.arange(4)[:, None, None] == 2 * np.arange(2)[None, :, None] + p[None, None, :] // 64))
    put("expsel", np.repeat(np.eye(E)[:, :, None], P, 2))
    put("epsln", np.full((P, 1), LN_EPS))
    put("epsrms", np.full((P, 1), RMS_EPS))
    put("one", np.ones((P, 1)))
    put("rank16", np.repeat(E - np.arange(E)[None, :], P, 0))
    put("rank4", np.repeat(4 - np.arange(4)[None, :], P, 0))
    put("rowrem", np.stack([p % ROWS_PAGE + l * POOL * ROWS_PAGE for l in range(DEPTH)], 1))
    reset = np.ones((P, T))
    reset[:, 0:TP:C] = 0
    reset[:, TP::TS] = 0
    put("reset", reset)
    half = ROPE // 2
    inv = (f(10000.0) ** (-np.arange(half, dtype=f) / f(half))).astype(f)
    pos = np.concatenate([np.arange(TP), np.tile(PAST + np.arange(TS), NSEQ)]).astype(f)
    ang = (pos[None, :] * inv[:, None]).astype(f)
    put("cos", np.tile(np.cos(ang), (8, 1)))
    put("sin", np.tile(np.concatenate([-np.sin(ang), np.sin(ang)], 0), (4, 1)))
    return np.concatenate(out, 1).astype(f), at


def build(nc, I, O, at, ncols):
    with ExitStack() as ctx:
        def sb(name, shape, dt=F32):
            return ctx.enter_context(nc.sbuf_tensor(name, shape, dt))[tuple(slice(None) for _ in shape)]

        sems = {}

        def S(name):
            if name not in sems:
                sems[name] = ctx.enter_context(nc.semaphore(name))
            return sems[name]

        const = sb("const", [P, ncols])

        def cst(name, rows=P):
            a, w = at[name]
            return const[0:rows, a:a + w]

        ident, ones, block = cst("ident"), cst("ones"), cst("block")
        vecrows = sb("vecrows", [P, P])
        vec = sb("vec", [P, P])
        bif = sb("bif", [4, 2 * DEPTH])
        routerw = sb("routerw", [P, KD, E])
        rbias = sb("rbias", [P, E])
        xT = sb("xT", [P, KD, T])
        zT = sb("zT", [P, KD, T])
        mix = sb("mix", [P, KD, T])
        wslot = sb("wslot", [P, NSLOT, KD, P])
        lnr = sb("lnr", [P, T])
        OVN = 28064
        over = sb("over", [P, OVN])
        ps = ctx.enter_context(nc.psum_tensor("ps", [P, 8, 512], F32))

        def col(name, l, k=0):
            r = VROW[name] + (l * VW[name] if name in VW else 0) + k
            return vec[:, r:r + 1]

        class Area:
            def __init__(self, start):
                self.n = start

            def get(self, *dims):
                w = int(np.prod(dims))
                v = over[:, self.n:self.n + w]
                self.n += w
                assert self.n <= OVN, self.n
                if len(dims) == 2:
                    v = v.rearrange("p (a b) -> p a b", b=dims[1])
                elif len(dims) == 3:
                    v = v.rearrange("p (a b c) -> p a b c", b=dims[1], c=dims[2])
                elif len(dims) == 4:
                    v = v.rearrange("p (a b c d) -> p a b c d", b=dims[1], c=dims[2], d=dims[3])
                return v

        io = Area(0)
        xtok = io.get(TT, D)
        base = Area(0)
        cq = base.get(2, T)
        ckv = base.get(T)
        small = base.get(T)
        rec = Area(base.n)
        og = rec.get(2, T)
        gq, gk = og[:, 0, :], og[:, 1, :]
        gv, gr, mv, mo = (rec.get(2, T) for _ in range(4))
        mup = rec.get(2, TP + CONV - 1)
        mus = rec.get(2, NSEQ, TS + CONV - 1)
        qm = rec.get(GH, T)
        kt, geb = mix[:, 6, :], mix[:, 7, :]
        uc = rec.get(2, T)
        mqm = rec.get(2, 2, T)
        wsm = over[:, rec.n:rec.n + KD * SMALL].rearrange("p (a b) -> p a b", b=SMALL)
        mqw = rec.get(2, 2, T)
        mk = rec.get(2, T)
        wpb = rec.get(2, T)
        nd = rec.get(2, 2, T)
        tmp1, tmp2, gb = nd[:, 0, 0, :], nd[:, 0, 1, :], nd[:, 1, 0, :]
        wqk = rec.get(2, 2, P)
        wa = rec.get(P)
        sg = rec.get(GV)
        sgs = rec.get(NSEQ, GV)
        cn = rec.get(2, 2 * DH)
        cns = rec.get(2, NSEQ, 2 * DH)
        nst = rec.get(2, NSEQ)
        gtok = rec.get(3 * P)
        vaug = rec.get(MH, 2 * DH)
        am = rec.get(4 * C)
        wd_ = rec.get(4 * C)
        qkw = rec.get(4 * C)
        kws = rec.get(MH, DH)
        ws = rec.get(MH)
        rec_end = rec.n
        enmb = zT[:, 0:2, :]
        vm = zT[:, 2:4, 0:512]
        ig, fg, rowF, rowm, rowwp, rowe = (mix[0:4, i, :] for i in range(6))
        rowM, rowt = fg, ig
        negM = zT[0:4, 4:8, :]
        ms0 = rec.get(NCH)
        msS = rec.get(NSEQ)
        att = Area(base.n)
        wuq = att.get(2, 1024)
        wukv = att.get(1024)
        wukT = att.get(4, P)
        qlat = att.get(T, H)
        ctok = att.get(9, LAT + ROPE)
        kro = att.get(T)
        idx = att.get(NSEQ).bitcast(I32)
        ptab = att.get(NSEQ).bitcast(I32)
        qrM = att.get(4, NS, H)
        mx = att.get(8)
        nmx = att.get(2)
        sums = att.get(8)
        rs = att.get(2)
        pbuf0 = att.n
        qn = att.get(4, T)
        qra = att.get(2, T)
        qrb = att.get(2, T)
        sq = att.get(T)
        att2 = Area(pbuf0)
        NPB = 3
        pq = att2.get(NPB, TP)
        pT = att2.get(NPB, 5 * P)
        mxq = att2.get(NPB, 2)
        nmq = att2.get(NPB)
        smq = att2.get(NPB, 2)
        rsq = att2.get(NPB)
        att3 = Area(pbuf0)
        kg = att3.get(2, KEYS_ROW * LAT)
        krg = att3.get(2, KEYS_ROW * ROPE)
        kT = att3.get(2, PAST)
        krT = att3.get(2, 512)
        psm = att3.get(PAST + 16)
        psT = mix[:, 0:4, :].rearrange("p a b -> p (a b)")[:, 0:17 * P]
        qr0 = zT.rearrange("p a b -> p (a b)").rearrange("p (t h) -> p t h", h=H)
        moe = Area(0)
        wg = moe.get(2, KD, F)
        wu = moe.get(2, KD, F)
        wdn = moe.get(2, 2, D)
        wT = moe.get(T)
        wb = moe.get(2, T)
        hx = moe.get(2, T)
        hh = moe.get(2, 2, T)
        sc, sel, r1, r2, r3, w16 = (moe.get(TT, E) for _ in range(6))
        g4 = [moe.get(TT, 4) for _ in range(6)]
        g1 = [moe.get(TT) for _ in range(3)]

        plan = []
        index = {}

        def nth(g):
            return sum(1 for c in plan[:g + 1] if c == plan[g])

        rel_sem = {"A": S("released_by_scalar"), "D": S("released_by_vector")}
        filled = S("bank_filled")

        def full(eng, key):
            eng.wait_ge(filled, index[key] + 1)

        def bank(key):
            return ps[:, index[key] % 8, :]

        def rel(ins, key, who):
            assert plan[index[key]] == who, key
            ins.then_inc(rel_sem[who], 1)

        barriers = {}

        def barrier(eng, name):
            barriers[name] = barriers.get(name, 0) + 1
            eng.drain().then_inc(S("stage_ended"), 1)
            eng.wait_ge(S("stage_ended"), 5 * barriers[name])

        wloads = []
        wlast = {}

        def wseq(l, what, j):
            return l * (len(CHUNKS) + KD) + (j if what == "in" else len(CHUNKS) + j)

        block_ = ctx.enter_context(nc.Block())

        @block_.tensor
        def _(pe):
            mm = nc.tensor.matmul
            waited = {}

            def wait(name, v):
                pe.wait_ge(S(name), v)

            def released(g):
                c = plan[g]
                v = nth(g)
                if waited.get(c, 0) < v:
                    waited[c] = v
                    pe.wait_ge(rel_sem[c], v)

            def group(key, consumer):
                g = len(plan)
                plan.append(consumer)
                index[key] = g
                if g >= 8:
                    released(g - 8)
                return ps[:, g % 8, :]

            def drained(key):
                released(index[key])

            def done(ins):
                ins.then_inc(filled, 1)

            def tr(out, in_, n):
                return nc.tensor.transpose(out, in_, ident[0:n, 0:n])

            def layer_norm(n):
                for h in range(2):
                    b = group(("mean", n, h), "D")
                    for k in range(KD):
                        i = mm(b[:, 0:HALF], ones, zT[:, k, SH[h]], start=(k == 0), stop=(k == KD - 1))
                    done(i)
                for h in range(2):
                    wait("ln_squared", 2 * n + h + 1)
                    b = group(("var", n, h), "A")
                    for k in range(KD):
                        i = mm(b[:, 0:HALF], ones, xT[:, k, SH[h]], start=(k == 0), stop=(k == KD - 1))
                    done(i)

            wait("const_loaded", 16)
            wait("vec_loaded", 16 * (len(VEC) + 5))
            b = group("vec", "A")
            done(tr(b[:, 0:P], vecrows[:, :], P))
            wait("x_loaded", 16 * 5)
            for t in range(TT):
                r = P if t < TT - 1 else LAST
                for q in range(2):
                    b = group(("xin", t, q), "A" if q else "D")
                    for k in range(4):
                        i = tr(b[:, k * P:k * P + r], xtok[0:r, t, (4 * q + k) * P:(4 * q + k + 1) * P], r)
                    done(i)
            for q in range(2):
                drained(("xin", TT - 1, q))
            layer_norm(0)

            for l in range(DEPTH):
                wait("ln_done", 2 * l + 1)
                barrier(pe, "pe")
                wait("wsmall_loaded", 16 * 5 * (l + 1))
                wait("rec_zeroed", l + 1)
                for h in range(2):
                    b = group(("small", l, h), "A")
                    for k in range(KD):
                        i = mm(b[0:SMALL, 0:HALF], wsm[:, k, :], xT[:, k, SH[h]], start=(k == 0), stop=(k == KD - 1))
                    done(i)
                for j, (name, part) in enumerate(CHUNKS):
                    u = wseq(l, "in", j)
                    wait(f"wslot{u % NSLOT}", 16 * (u // NSLOT + 1))
                    for h in range(2):
                        b = group(("in", l, j, h), "DA"[h] if name != "mu" else "A")
                        for k in range(KD):
                            i = mm(b[:, 0:HALF], wslot[:, u % NSLOT, k, :], xT[:, k, SH[h]], start=(k == 0), stop=(k == KD - 1))
                        done(i)
                    wlast[u] = ("in", l, j, 1)
                wait("rec_loaded", 16 * 13 * (l + 1))
                drained(("small", l, 1))
                for h in range(2):
                    b = group(("ga", l, h), "D")
                    done(mm(b[:, 0:HALF], wa[64:64 + GR, :], small[64:64 + GR, SH[h]], start=True, stop=True))
                wait("conv_done", l + 1)
                wait("wqk_loaded", 16 * 8 * (l + 1))
                for qk in range(2):
                    for j in range(2):
                        for h in range(2):
                            b = group(("mqk", l, qk, j, h), "A")
                            done(mm(b[:, 0:HALF], wqk[:, qk, j, :], uc[:, j, SH[h]], start=True, stop=True))
                wait("rows_done", l + 1)
                for n, row in enumerate((rowwp, rowe)):
                    for j in range(2):
                        for h in range(2):
                            b = group(("spread", l, n, j, h), "A")
                            done(mm(b[:, 0:HALF], cst("pairsel", 4)[:, j * P:(j + 1) * P], row[:, SH[h]], start=True, stop=True))
                drained(("in", l, len(CHUNKS) - 1, 0))
                drained(("in", l, len(CHUNKS) - 1, 1))
                wait("gla_inputs", l + 1)
                wait("mqw_done", l + 1)
                wait("states_ready", l + 1)
                for c in range(NCH + 1):
                    smp = c == NCH
                    n = NS if smp else C
                    cs = slice(c * C, c * C + n)
                    w = 4 * n
                    b = group(("gtok", l, c), "A")
                    for q, src in enumerate((gv[:, 0, cs], gv[:, 1, cs], kt[:, cs])):
                        i = tr(b[0:n, q * P:(q + 1) * P], src, P)
                    done(i)
                    b = group(("vtok", l, c), "A")
                    for q in range(2):
                        i = tr(b[0:n, q * P:(q + 1) * P], mv[:, q, cs], P)
                    done(i)
                    b = group(("ga_s", l, c), "D")
                    done(mm(b[0:n, 0:w], kt[:, cs], qm[:, :, cs], start=True, stop=True))
                    b = group(("logw", l, c), "A")
                    mm(b[0:n, 0:w], rowt[:, cs], cst("rowsel", 4).rearrange("p (h t) -> p h t", h=4)[:, :, 0:n], start=True, stop=False)
                    mm(b[0:n, 0:w], ones[0:4, 0:n], negM[:, :, cs], start=False, stop=False)
                    done(mm(b[0:n, 0:w], ident[0:n, 0:n], cst("trineg_s" if smp else "trineg", n), start=False, stop=True))
                    b = group(("qk", l, c), "D")
                    for j in range(2):
                        i = mm(b[0:n, 2 * j * n:2 * (j + 1) * n], mk[:, j, cs], mqm[:, j, :, cs], start=True, stop=True)
                    done(i)
                    b = group(("ktok", l, c), "D")
                    for q in range(2):
                        i = tr(b[0:n, q * P:(q + 1) * P], mk[:, q, cs], P)
                    done(i)
                    drained(("gtok", l, c))
                    drained(("ga_s", l, c))
                    if c and not smp:
                        wait("gla_state", (NCH + 1) * l + c)
                    b = group(("go", l, c), "A")
                    for hd in range(GH):
                        r = slice(64 * (hd % 2), 64 * (hd % 2) + 64)
                        o = b[r, (hd // 2) * n:(hd // 2) * n + n]
                        mm(o, gtok[0:n, hd * GV:(hd + 1) * GV], am[0:n, hd * n:(hd + 1) * n], start=True, stop=False)
                        if smp:
                            for s in range(NSEQ):
                                i = mm(o[:, s * TS:(s + 1) * TS], sgs[:, s, :], qm[:, hd, TP + s * TS:TP + (s + 1) * TS],
                                       start=False, stop=(s == NSEQ - 1))
                        else:
                            i = mm(o, sg[:, :], qm[:, hd, cs], start=False, stop=True)
                    done(i)
                    b = group(("gs", l, c), "D")
                    if smp:
                        for hd in range(GH):
                            wait("gla_vmask", GH * l + hd + 1)
                            i = mm(b[32 * hd:32 * hd + 32, 0:512], gtok[0:n, 2 * P + GK * hd:2 * P + GK * hd + GK], vm[0:n, hd % 2, :],
                                   start=True, stop=True, tile_position=(0, 32 * hd))
                            if hd < GH - 1:
                                i.then_inc(S("gla_vm_read"), 1)
                    else:
                        for hd in range(GH):
                            i = mm(b[32 * hd:32 * hd + 32, 0:GV], gtok[0:n, 2 * P + GK * hd:2 * P + GK * hd + GK],
                                   gtok[0:n, hd * GV:(hd + 1) * GV], start=True, stop=True, tile_position=(0, 32 * hd))
                    done(i)
                    drained(("vtok", l, c))
                    drained(("qk", l, c))
                    if c and not smp:
                        wait("ml_state", (NCH + 1) * l + c)
                    b = group(("nd", l, c), "A")
                    for hd in range(MH):
                        r = slice(64 * (hd % 2), 64 * (hd % 2) + 64)
                        j = hd // 2
                        for x in range(2):
                            o = b[r, (2 * x + j) * n:(2 * x + j + 1) * n]
                            mm(o, vaug[0:n, hd, x * DH:(x + 1) * DH], qkw[0:n, hd * n:(hd + 1) * n], start=True, stop=False)
                            if smp:
                                for s in range(NSEQ):
                                    i = mm(o[:, s * TS:(s + 1) * TS], cns[:, j, s, x * DH:(x + 1) * DH],
                                           mqw[:, j, hd % 2, TP + s * TS:TP + (s + 1) * TS], start=False, stop=(s == NSEQ - 1))
                            else:
                                i = mm(o, cn[:, j, x * DH:(x + 1) * DH], mqw[:, j, hd % 2, cs], start=False, stop=True)
                    done(i)
                    drained(("ktok", l, c))
                    if smp:
                        for j in range(2):
                            b = group(("mu_c", l, j), "D")
                            for a in range(2):
                                hd = 2 * j + a
                                wait("ml_vmask", MH * l + hd + 1)
                                i = mm(b[64 * a:64 * a + 64, 0:512], kws[0:n, hd, :], vm[0:n, hd % 2, :], start=True, stop=True)
                                if a == 0:
                                    i.then_inc(S("ml_vm_read"), 1)
                            done(i)
                            b = group(("mu_n", l, j), "D")
                            for a in range(2):
                                i = mm(b[64 * a:64 * a + 64, 0:512], kws[0:n, 2 * j + a, :],
                                       cst("seqmask", n).unsqueeze(2).to_broadcast([n, NSEQ, DH]), start=True, stop=True)
                            done(i)
                    else:
                        b = group(("mu", l, c), "D")
                        for hd in range(MH):
                            i = mm(b[64 * (hd % 2):64 * (hd % 2) + 64, (hd // 2) * P:(hd // 2) * P + P], kws[0:n, hd, :], vaug[0:n, hd, :],
                                   start=True, stop=True)
                        done(i)
                for j in range(2):
                    for h in range(2):
                        wait("gla_sq", l + 1)
                        b = group(("gn", l, j, h), "A")
                        done(mm(b[:, 0:HALF], block, qm[:, j, SH[h]], start=True, stop=True))
                wait("ml_h", l + 1)
                for j in range(2):
                    for h in range(2):
                        b = group(("mm_", l, j, h), "D")
                        done(mm(b[:, 0:HALF], block, nd[:, 0, j, SH[h]], start=True, stop=True))
                wait("ml_hsq", l + 1)
                for j in range(2):
                    for h in range(2):
                        b = group(("mvv", l, j, h), "A")
                        done(mm(b[:, 0:HALF], block, nd[:, 1, j, SH[h]], start=True, stop=True))
                barrier(pe, "pe")

                wait("att_loaded", 16 * 10 * (l + 1))
                for j in range(4):
                    b = group(("wukT", l, j), "A")
                    done(tr(b[:, 0:P], wukv[:, j * P:(j + 1) * P], P))
                wait("cq_sq", l + 1)
                for h in range(2):
                    b = group(("cqn", l, h), "A")
                    for k in range(2):
                        i = mm(b[:, 0:HALF], ones, qn[:, k, SH[h]], start=(k == 0), stop=(k == 1))
                    done(i)
                for h in range(2):
                    b = group(("ckn", l, h), "A")
                    done(mm(b[:, 0:HALF], ones, sq[:, SH[h]], start=True, stop=True))
                wait("cq_done", l + 1)
                for m in range(8):
                    for h in range(2):
                        b = group(("q", l, m, h), "A" if m < 6 else "D")
                        for k in range(2):
                            i = mm(b[:, 0:HALF], wuq[:, k, m * P:(m + 1) * P], cq[:, k, SH[h]], start=(k == 0), stop=(k == 1))
                        done(i)
                for hd in range(H):
                    r = slice(64 * (hd % 2), 64 * (hd % 2) + 64)
                    if hd == 0:
                        drained(("q", l, 5, 1))
                        drained(("wukT", l, 3))
                    for h in range(2):
                        b = group(("qlat", l, hd, h), "DA"[h])
                        done(mm(b[:, 0:HALF], wukT[r, hd // 2, :], qn[r, hd // 2, SH[h]], start=True, stop=True))
                wait("ckv_done", l + 1)
                for t in range(9):
                    n = P if t < 4 else QT
                    cs = slice(t * P, t * P + n) if t < 5 else slice(TP + (t - 5) * QT, TP + (t - 4) * QT)
                    b = group(("ctok", l, t), "A")
                    tr(b[0:n, 0:LAT], ckv[:, cs], P)
                    done(tr(b[0:n, LAT:LAT + ROPE], kro[0:ROPE, cs], ROPE))
                drained(("qlat", l, H - 1, 0))
                drained(("qlat", l, H - 1, 1))
                drained(("ctok", l, 8))
                barrier(pe, "pe")

                for step in range(NQ + 2):
                    if step < NQ:
                        i_ = step
                        W = QT * (i_ + 1)
                        cs = slice(QT * i_, W)
                        ql = qlat[:, cs, :].rearrange("p t h -> p (t h)")
                        qr = qr0[0:ROPE, cs, :].rearrange("p t h -> p (t h)")
                        for x, (a, z) in enumerate(((0, min(W, 512)), (512, W))):
                            if z <= a:
                                continue
                            b = group(("s", l, i_, x), "A")
                            o = b[:, 0:z - a]
                            mm(o, ql, ckv[:, a:z], start=True, stop=False)
                            last = z == W
                            i = mm(o, qr, kro[0:ROPE, a:z], start=False, stop=not last)
                            if last:
                                i = mm(b[:, z - a - QT:z - a], ident, cst("mask_q"), start=False, stop=True)
                            done(i)
                    if 1 <= step <= NQ:
                        i_ = step - 1
                        W = QT * (i_ + 1)
                        nb = -(-W // P)
                        wait("pq_normed", NQ * l + i_ + 1)
                        for x in range(2):
                            blocks = range(4 * x, min(nb, 4 * x + 4))
                            if not len(blocks):
                                continue
                            b = group(("pt", l, i_, x), "DA"[i_ % 2])
                            for kb in blocks:
                                wk = min(P, W - kb * P)
                                i = tr(b[0:wk, (kb % 4) * P:(kb % 4) * P + P], pq[:, i_ % NPB, kb * P:kb * P + wk], P)
                            done(i)
                    if step >= 2:
                        i_ = step - 2
                        W = QT * (i_ + 1)
                        nb = -(-W // P)
                        drained(("pt", l, i_, (nb - 1) // 4))
                        b = group(("o", l, i_), "D")
                        for kb in range(nb):
                            wk = min(P, W - kb * P)
                            i = mm(b[:, 0:P], ctok[0:wk, kb, 0:LAT], pT[0:wk, i_ % NPB, kb * P:(kb + 1) * P],
                                   start=(kb == 0), stop=(kb == nb - 1))
                        done(i)
                barrier(pe, "pe")

                for p_ in range(NSEQ // 2):
                    for s in range(2):
                        wait(f"pages{s}", 32 * (l * NSEQ // 2 + p_ + 1))
                        for q in range(4):
                            b = group(("kT", l, p_, s, q), "DA"[q % 2])
                            for k in range(4):
                                j = 4 * q + k
                                i = tr(b[:, k * P:(k + 1) * P], kg[:, s, j * LAT:(j + 1) * LAT], P)
                            done(i)
                        b = group(("krT", l, p_, s), "DA"[s])
                        for q in range(4):
                            i = tr(b[:, q * P:(q + 1) * P], krg[:, s, q * P:(q + 1) * P], P)
                        done(i)
                    cols = [slice(TP + (2 * p_ + s) * TS, TP + (2 * p_ + s + 1) * TS) for s in range(2)]
                    for s in range(2):
                        drained(("kT", l, p_, s, 3))
                        drained(("kT", l, p_, s, 2))
                        drained(("krT", l, p_, s))
                    for q in range(4):
                        b = group(("ss", l, p_, q), "A")
                        for s in range(2):
                            o = b[64 * s:64 * s + 64, :]
                            mm(o, qlat[:, cols[s], :].rearrange("p t h -> p (t h)"), kT[:, s, q * 512:(q + 1) * 512], start=True, stop=False)
                            for jj in range(4):
                                c0 = (2 * p_ + s) * TS
                                i = mm(o[:, jj * P:(jj + 1) * P], qrM[:, jj, c0:c0 + TS, :].rearrange("p t h -> p (t h)"),
                                       krT[:, s, q * P:(q + 1) * P], start=False, stop=(jj == 3))
                        done(i)
                    b = group(("sn", l, p_), "A")
                    new = slice(TP + p_ * QT, TP + (p_ + 1) * QT)
                    for s in range(2):
                        o = b[64 * s:64 * s + 64, 0:QT]
                        mm(o, qlat[:, cols[s], :].rearrange("p t h -> p (t h)"), ckv[:, new], start=True, stop=False)
                        mm(o, qr0[0:ROPE, cols[s], :].rearrange("p t h -> p (t h)"), kro[0:ROPE, new], start=False, stop=False)
                    done(mm(b[:, 0:QT], ident, cst("mask_n"), start=False, stop=True))
                    wait("ps_normed", l * (NSEQ // 2) + p_ + 1)
                    for q in range(4):
                        b = group(("psT", l, p_, q), "DA"[q % 2])
                        for k in range(4):
                            i = tr(b[:, k * P:(k + 1) * P], psm[:, (4 * q + k) * P:(4 * q + k + 1) * P], P)
                        done(i)
                    b = group(("psT", l, p_, 4), "D")
                    done(tr(b[0:QT, 0:P], psm[:, PAST:PAST + QT], P))
                    drained(("psT", l, p_, 4))
                    drained(("psT", l, p_, 3))
                    b = group(("so", l, p_), "D")
                    for s in range(2):
                        o = b[:, 64 * s:64 * s + 64]
                        for j in range(16):
                            mm(o, kg[:, s, j * LAT:(j + 1) * LAT], psT[:, j * P + 64 * s:j * P + 64 * s + 64], start=(j == 0), stop=False)
                        i = mm(o, ctok[0:QT, 5 + p_, 0:LAT], psT[0:QT, 16 * P + 64 * s:16 * P + 64 * s + 64], start=False, stop=True)
                    done(i)
                drained(("so", l, NSEQ // 2 - 1))
                for j in range(4):
                    for h in range(2):
                        b = group(("omla", l, j, h), "DA"[h])
                        for a in range(2):
                            hd = 2 * j + a
                            i = mm(b[64 * a:64 * a + 64, 0:HALF], wukv[:, 512 + hd * MV:512 + (hd + 1) * MV], qlat[:, SH[h], hd], start=True, stop=True)
                        done(i)
                drained(("omla", l, 3, 0))
                drained(("omla", l, 3, 1))
                barrier(pe, "pe")
                for m in range(KD):
                    u = wseq(l, "out", m)
                    wait(f"wslot{u % NSLOT}", 16 * (u // NSLOT + 1))
                    for h in range(2):
                        b = group(("out", l, m, h), "D")
                        for k in range(KD):
                            i = mm(b[:, 0:HALF], wslot[:, u % NSLOT, k, :], mix[:, k, SH[h]], start=(k == 0), stop=(k == KD - 1))
                        done(i)
                    wlast[u] = ("out", l, m, 1)
                drained(("out", l, KD - 1, 1))
                layer_norm(2 * l + 1)

                wait("ln_done", 2 * l + 2)
                b = group(("route", l), "A")
                for t in range(TT):
                    r = P if t < TT - 1 else LAST
                    for k in range(KD):
                        i = mm(b[0:r, t * E:(t + 1) * E], xT[:, k, t * P:t * P + r], routerw[:, k, :], start=(k == 0), stop=(k == KD - 1))
                done(i)
                wait("weights16", l + 1)
                for x in range(2):
                    b = group(("wT", l, x), "A")
                    for t in ((0, 1, 2, 3), (4,))[x]:
                        r = P if t < TT - 1 else LAST
                        i = tr(b[0:E, (t % 4) * P:(t % 4) * P + r], w16[0:r, t, :], r)
                    done(i)
                drained(("wT", l, 1))

                def up(e):
                    n = l * E + e
                    wait(f"wgu{e % 2}", 32 * (n // 2 + 1))
                    for h in range(2):
                        b = group(("wb", l, e, h), "A")
                        done(mm(b[:, 0:HALF], cst("expsel", E)[:, e * P:(e + 1) * P], wT[0:E, SH[h]], start=True, stop=True))
                    for f in range(2):
                        for h in range(2):
                            for nm, w_ in (("hg", wg), ("hu", wu)):
                                b = group((nm, l, e, f, h), "D")
                                for k in range(KD):
                                    i = mm(b[:, 0:HALF], w_[:, e % 2, k, f * P:(f + 1) * P], xT[:, k, SH[h]], start=(k == 0), stop=(k == KD - 1))
                                done(i)

                def down(e):
                    n = l * E + e
                    wait(f"wdn{e % 2}", 16 * (n // 2 + 1))
                    wait("h_done", 4 * n + 4)
                    for m in range(KD):
                        for h in range(2):
                            b = group(("dn", l, e, m, h), "D")
                            for f in range(2):
                                i = mm(b[:, 0:HALF], wdn[:, e % 2, f, m * P:(m + 1) * P], hh[:, e % 2, f, SH[h]], start=(f == 0), stop=(f == 1))
                            done(i)

                up(0)
                for e in range(E):
                    if e + 1 < E:
                        up(e + 1)
                    down(e)
                drained(("dn", l, E - 1, KD - 1, 1))
                layer_norm(2 * l + 2)
            wait("ln_done", 2 * DEPTH + 1)
            barrier(pe, "pe")
            for t in range(TT):
                r = P if t < TT - 1 else LAST
                for q in range(2):
                    b = group(("yout", t, q), "DA"[q])
                    for k in range(4):
                        i = tr(b[0:r, k * P:(k + 1) * P], xT[:, 4 * q + k, t * P:t * P + r], P)
                    done(i)

        def drained_by_other(eng, key):
            eng.wait_ge(rel_sem[plan[index[key]]], nth(index[key]))

        def prompt_pT(eng, l, i_, op, who):
            W = QT * (i_ + 1)
            nb = -(-W // P)
            if i_ >= NPB:
                eng.wait_ge(filled, index[("o", l, i_ - NPB)] + 1)
            for x in range(2):
                n = min(nb, 4 * x + 4) - 4 * x
                if n <= 0:
                    continue
                key = ("pt", l, i_, x)
                full(eng, key)
                wl = min(P, W - (4 * x + n - 1) * P)
                d = pT[:, i_ % NPB, :]
                if wl == P or n == 1:
                    rows = P if wl == P else wl
                    i = op(d[0:rows, 4 * x * P:(4 * x + n) * P], bank(key)[0:rows, 0:n * P])
                else:
                    op(d[:, 4 * x * P:(4 * x + n - 1) * P], bank(key)[:, 0:(n - 1) * P])
                    i = op(d[0:wl, (4 * x + n - 1) * P:(4 * x + n) * P], bank(key)[0:wl, (n - 1) * P:n * P])
                rel(i, key, who)

        @block_.scalar
        def _(act):
            f_ = nc.scalar.activation

            def sig(ins, name, k=1):
                ins.then_inc(S(name), k)

            def inverse_root(key, out, scale, eps):
                full(act, key)
                rel(f_(out, bank(key)[:, 0:HALF], ACT.Ln, bias=eps, scale=scale), key, "A")
                act.drain()
                return f_(out, out, ACT.Exp, scale=-0.5)

            def copy(key, dst, src, scale=None):
                full(act, key)
                if scale is None:
                    rel(f_(dst, src, ACT.Copy), key, "A")
                else:
                    rel(f_(dst, src, ACT.Copy, scale=scale), key, "A")

            def layer_norm(n):
                for h in range(2):
                    act.wait_ge(S("ln_centred"), 2 * n + h + 1)
                    sig(f_(xT[:, :, SH[h]], zT[:, :, SH[h]], ACT.Square), "ln_squared")
                for h in range(2):
                    sig(inverse_root(("var", n, h), lnr[:, SH[h]], 1.0 / D, cst("epsln")), "ln_root")

            copy("vec", vec[:, :], bank("vec")[:, 0:P])
            act.drain().then_inc(S("vec_ready"), 1)
            for t in range(TT):
                r = P if t < TT - 1 else LAST
                copy(("xin", t, 1), zT[:, 4:8, t * P:t * P + r], bank(("xin", t, 1)).rearrange("p (k n) -> p k n", k=4)[:, :, 0:r])
            layer_norm(0)

            for l in range(DEPTH):
                barrier(act, "act")
                for h in range(2):
                    copy(("small", l, h), small[0:SMALL, SH[h]], bank(("small", l, h))[0:SMALL, 0:HALF])
                act.drain().then_inc(S("small_ready"), 1)
                for j, (name, part) in enumerate(CHUNKS):
                    dst = dict(cq=cq, gv=gv, gr=gr, mv=mv, mo=mo).get(name)
                    dst = dst[:, part, :] if dst is not None else dict(ckv=ckv, gq=gq, gk=gk).get(name)
                    if name == "mu":
                        copy(("in", l, j, 0), mup[:, part, CONV - 1:CONV - 1 + HALF], bank(("in", l, j, 0))[:, 0:HALF])
                        b = bank(("in", l, j, 1))
                        full(act, ("in", l, j, 1))
                        f_(mup[:, part, CONV - 1 + HALF:CONV - 1 + TP], b[:, 0:TP - HALF], ACT.Copy)
                        rel(f_(mus[:, part, :, CONV - 1:], b[:, TP - HALF:HALF].rearrange("p (s t) -> p s t", s=NSEQ), ACT.Copy),
                            ("in", l, j, 1), "A")
                        if part == 1:
                            act.drain().then_inc(S("mu_ready"), 1)
                    else:
                        copy(("in", l, j, 1), dst[:, SH[1]], bank(("in", l, j, 1))[:, 0:HALF])
                act.drain().then_inc(S("in_half_ready"), 1)
                act.wait_ge(S("fgate_abs"), l + 1)
                f_(rowe, rowe, ACT.Exp, scale=-1.0)
                act.drain()
                sig(f_(rowe, rowe, ACT.Ln, bias=cst("one", 4)), "fgate_ln")
                act.wait_ge(S("ga_abs"), l + 1)
                f_(tmp1, tmp1, ACT.Exp, scale=-1.0)
                act.drain()
                sig(f_(tmp1, tmp1, ACT.Ln, bias=cst("one")), "ga_ln")
                act.wait_ge(S("conv_sum"), l + 1)
                sig(f_(wpb, uc, ACT.Exp, scale=-1.0), "conv_exp")
                act.wait_ge(S("rows_logs"), l + 1)
                f_(rowwp, rowwp, ACT.Exp)
                sig(f_(rowe, rowm, ACT.Exp, scale=-1.0), "rows_exp")
                act.wait_ge(S("ga_cum"), l + 1)
                f_(geb, tmp2, ACT.Exp, scale=1.0 / TAU)
                sig(f_(gb, tmp2, ACT.Exp, scale=-1.0 / TAU), "ga_decay")
                for qk in range(2):
                    for j in range(2):
                        for h in range(2):
                            key = ("mqk", l, qk, j, h)
                            b = bank(key)
                            if qk:
                                copy(key, mk[:, j, SH[h]], b[:, 0:HALF], DH ** -0.5)
                            else:
                                full(act, key)
                                f_(mqm[0:64, j, 0, SH[h]], b[0:64, 0:HALF], ACT.Copy)
                                rel(f_(mqm[64:128, j, 1, SH[h]], b[64:128, 0:HALF], ACT.Copy), key, "A")
                for n, dst in enumerate((wpb, enmb)):
                    for j in range(2):
                        for h in range(2):
                            copy(("spread", l, n, j, h), dst[:, j, SH[h]], bank(("spread", l, n, j, h))[:, 0:HALF])
                act.drain().then_inc(S("spread_ready"), 1)
                for c in range(NCH + 1):
                    smp = c == NCH
                    n = NS if smp else C
                    cs = slice(c * C, c * C + n)
                    copy(("gtok", l, c), gtok[0:n, :], bank(("gtok", l, c))[0:n, 0:3 * P])
                    copy(("vtok", l, c), vaug[0:n, :, 0:DH], bank(("vtok", l, c))[0:n, 0:256].rearrange("p (h v) -> p h v", h=MH))
                    key = ("logw", l, c)
                    full(act, key)
                    if c:
                        act.wait_ge(S("kws_done"), (NCH + 1) * l + c)
                    i = f_(wd_[0:n, 0:4 * n], bank(key)[0:n, 0:4 * n], ACT.Exp)
                    rel(i, key, "A")
                    act.drain().then_inc(S("w_ready"), 1)
                    copy(("go", l, c), og[:, :, cs], bank(("go", l, c))[:, 0:2 * n].rearrange("p (j t) -> p j t", j=2))
                    copy(("nd", l, c), nd[:, :, :, cs], bank(("nd", l, c))[:, 0:4 * n].rearrange("p (x j t) -> p x j t", x=2, j=2))
                act.drain().then_inc(S("chunks_out"), 1)
                act.wait_ge(filled, index[("nd", l, NCH)] + 1)
                f_(mo, mo, ACT.Exp, scale=-1.0).then_inc(S("mo_exp"), 1)
                f_(mqm[:, 0, :, :], gr, ACT.Exp, scale=-1.0).then_inc(S("gr_exp"), 1)
                f_(qm[:, 0:2, :], og, ACT.Square).then_inc(S("gla_sq"), 1)
                for j in range(2):
                    for h in range(2):
                        i = inverse_root(("gn", l, j, h), gv[:, j, SH[h]], 1.0 / GV, cst("epsrms"))
                i.then_inc(S("gla_root"), 1)
                act.wait_ge(S("ml_centred"), l + 1)
                f_(nd[:, 1, :, :], nd[:, 0, :, :], ACT.Square).then_inc(S("ml_hsq"), 1)
                for j in range(2):
                    for h in range(2):
                        i = inverse_root(("mvv", l, j, h), mk[:, j, SH[h]], 1.0 / DH, cst("epsln"))
                i.then_inc(S("ml_root"), 1)
                barrier(act, "act")

                for j in range(4):
                    copy(("wukT", l, j), wukT[:, j, :], bank(("wukT", l, j))[:, 0:P])
                f_(qn[:, 0:2, :], cq, ACT.Square)
                f_(sq, ckv, ACT.Square)
                act.drain().then_inc(S("cq_sq"), 1)
                for h in range(2):
                    inverse_root(("cqn", l, h), lnr[:, SH[h]], 1.0 / 256, cst("epsrms"))
                for h in range(2):
                    inverse_root(("ckn", l, h), qra[:, 0, SH[h]], 1.0 / LAT, cst("epsrms"))
                act.drain().then_inc(S("cq_root"), 1)
                for m in range(6):
                    if m == 4:
                        act.wait_ge(S("ckv_done"), l + 1)
                    for h in range(2):
                        dst = qn[:, m, SH[h]] if m < 4 else qra[:, m - 4, SH[h]]
                        copy(("q", l, m, h), dst, bank(("q", l, m, h))[:, 0:HALF])
                act.drain().then_inc(S("qra_ready"), 1)
                for hd in range(H):
                    copy(("qlat", l, hd, 1), qlat[:, SH[1], hd], bank(("qlat", l, hd, 1))[:, 0:HALF])
                for t in range(9):
                    n = P if t < 4 else QT
                    copy(("ctok", l, t), ctok[0:n, t, :], bank(("ctok", l, t))[0:n, 0:LAT + ROPE])
                act.drain().then_inc(S("ctok_ready"), 1)
                barrier(act, "act")

                for step in range(NQ + 1):
                    if step < NQ:
                        i_ = step
                        W = QT * (i_ + 1)
                        act.wait_ge(S("pq_max"), NQ * l + i_ + 1)
                        if i_ >= NPB:
                            W0 = QT * (i_ - NPB + 1)
                            act.wait_ge(filled, index[("pt", l, i_ - NPB, (-(-W0 // P) - 1) // 4)] + 1)
                        for x, (a, z) in enumerate(((0, min(W, 512)), (512, W))):
                            if z <= a:
                                continue
                            key = ("s", l, i_, x)
                            full(act, key)
                            i = f_(pq[:, i_ % NPB, a:z], bank(key)[:, 0:z - a], ACT.Exp, bias=nmq[:, i_ % NPB:i_ % NPB + 1],
                                   scale=SCALE, accum_out=smq[:, i_ % NPB, x:x + 1])
                            rel(i, key, "A")
                        act.drain().then_inc(S("pq_exp"), 1)
                    if step >= 1 and (step - 1) % 2 == 1:
                        i_ = step - 1
                        prompt_pT(act, l, i_, lambda d, s_: f_(d, s_, ACT.Copy), "A")
                barrier(act, "act")

                for p_ in range(NSEQ // 2):
                    for s in range(2):
                        for q in (1, 3):
                            copy(("kT", l, p_, s, q), kT[:, s, q * 512:(q + 1) * 512], bank(("kT", l, p_, s, q)))
                    copy(("krT", l, p_, 1), krT[:, 1, :], bank(("krT", l, p_, 1)))
                    act.wait_ge(S("ps_max"), l * (NSEQ // 2) + p_ + 1)
                    for q in range(5):
                        key = ("ss", l, p_, q) if q < 4 else ("sn", l, p_)
                        w = 512 if q < 4 else QT
                        full(act, key)
                        i = f_(psm[:, q * 512:q * 512 + w], bank(key)[:, 0:w], ACT.Exp, bias=nmx[:, 0:1], scale=SCALE,
                               accum_out=sums[:, q:q + 1])
                        rel(i, key, "A")
                    act.drain().then_inc(S("ps_exp"), 1)
                    for q in (1, 3):
                        copy(("psT", l, p_, q), psT[:, q * 512:(q + 1) * 512], bank(("psT", l, p_, q)))
                for j in range(4):
                    copy(("omla", l, j, 1), mix[:, j, SH[1]], bank(("omla", l, j, 1))[:, 0:HALF])
                barrier(act, "act")
                layer_norm(2 * l + 1)

                act.wait_ge(S("logits_zeroed"), l + 1)
                key = ("route", l)
                full(act, key)
                b = bank(key).rearrange("p (t e) -> p t e", e=E)
                f_(sc[:, 0:4, :], b[:, 0:4, :], ACT.Exp, scale=-1.0)
                rel(f_(sc[0:LAST, 4, :], b[0:LAST, 4, :], ACT.Exp, scale=-1.0), key, "A")
                act.drain().then_inc(S("logits_exp"), 1)
                copy(("wT", l, 0), wT[0:E, 0:512], bank(("wT", l, 0))[0:E, :])
                copy(("wT", l, 1), wT[0:E, 512:T], bank(("wT", l, 1))[0:E, 0:LAST])
                for e in range(E):
                    n = l * E + e
                    if n >= 2:
                        act.wait_ge(S("h_done"), 4 * (n - 1))
                    for h in range(2):
                        copy(("wb", l, e, h), wb[:, e % 2, SH[h]], bank(("wb", l, e, h))[:, 0:HALF])
                    for f in range(2):
                        for h in range(2):
                            q = 2 * f + h
                            if n >= 1:
                                act.wait_ge(S("h_done"), 4 * (n - 1) + q + 1)
                            full(act, ("hg", l, e, f, h))
                            sig(f_(hx[:, f, SH[h]], bank(("hg", l, e, f, h))[:, 0:HALF], ACT.Exp, scale=-1.0), "hg_exp")
                layer_norm(2 * l + 2)
            barrier(act, "act")
            for t in range(TT):
                r = P if t < TT - 1 else LAST
                copy(("yout", t, 1), xtok[0:r, t, 512:1024], bank(("yout", t, 1))[0:r, :])
            act.drain().then_inc(S("y_ready"), 1)

        @block_.vector
        def _(dve):
            v = nc.vector
            tt, ts_, stt = v.tensor_tensor, v.tensor_scalar, v.scalar_tensor_tensor

            def sig(name):
                dve.drain().then_inc(S(name), 1)

            def copy(key, dst, src):
                full(dve, key)
                rel(v.tensor_copy(dst, src), key, "D")

            def layer_norm(n, g, b, l):
                for h in range(2):
                    key = ("mean", n, h)
                    full(dve, key)
                    z = zT[:, :, SH[h]]
                    i = stt(z, bank(key)[:, 0:HALF].unsqueeze(1).to_broadcast([P, KD, HALF]), -1.0 / D, z, ALU.mult, ALU.add)
                    rel(i, key, "D")
                    sig("ln_centred")
                for h in range(2):
                    dve.wait_ge(S("ln_root"), 2 * n + h + 1)
                    tt(xT[:, :, SH[h]], zT[:, :, SH[h]], lnr[:, SH[h]].unsqueeze(1).to_broadcast([P, KD, HALF]), ALU.mult)
                dve.drain()
                for k in range(KD):
                    ts_(xT[:, k, :], xT[:, k, :], col(g, l, k), col(b, l, k), ALU.mult, ALU.add)
                sig("ln_done")

            def one_over_one_plus(x):
                ts_(x, x, 1.0, None, ALU.add)
                dve.drain()
                v.reciprocal(x, x)
                dve.drain()

            for t in range(TT):
                r = P if t < TT - 1 else LAST
                copy(("xin", t, 0), zT[:, 0:4, t * P:t * P + r], bank(("xin", t, 0)).rearrange("p (k n) -> p k n", k=4)[:, :, 0:r])
            dve.wait_ge(S("vec_ready"), 1)
            layer_norm(0, "ln_in_g", "ln_in_b", 0)

            for l in range(DEPTH):
                barrier(dve, "dve")
                for j, (name, part) in enumerate(CHUNKS):
                    dst = dict(cq=cq, gv=gv, gr=gr, mv=mv, mo=mo).get(name)
                    dst = dst[:, part, :] if dst is not None else dict(ckv=ckv, gq=gq, gk=gk).get(name)
                    if name != "mu":
                        copy(("in", l, j, 0), dst[:, SH[0]], bank(("in", l, j, 0))[:, 0:HALF])
                dve.wait_ge(S("rec_loaded"), 16 * 13 * (l + 1))
                dve.wait_ge(S("rec_zeroed"), l + 1)
                dve.wait_ge(S("mu_ready"), l + 1)
                for c in range(2):
                    outs = (uc[:, c, 0:TP], uc[:, c, TP:T].rearrange("p (s t) -> p s t", s=NSEQ))
                    for k in range(CONV):
                        for o, src in zip(outs, (mup[:, c, k:k + TP], mus[:, c, :, k:k + TS])):
                            w = col("conv_w", l, 2 * k + c)
                            if k == 0:
                                ts_(o, src, w, col("conv_b", l, c), ALU.mult, ALU.add)
                            else:
                                stt(o, src, w, o, ALU.mult, ALU.add)
                        dve.drain()
                sig("conv_sum")
                for h in range(2):
                    key = ("ga", l, h)
                    full(dve, key)
                    rel(ts_(gb[:, SH[h]], bank(key)[:, 0:HALF], col("b_a", l), None, ALU.add), key, "D")
                dve.drain()
                stt(tmp1, gb, -1.0, gb, ALU.mult, ALU.max)
                sig("ga_abs")
                dve.wait_ge(S("rows_moved"), 32 * (l + 1))
                ts_(fg, fg, bif[:, DEPTH + l:DEPTH + l + 1], None, ALU.add)
                ts_(ig, ig, bif[:, l:l + 1], None, ALU.add)
                dve.drain()
                stt(rowe, fg, -1.0, fg, ALU.mult, ALU.max)
                sig("fgate_abs")
                dve.wait_ge(S("fgate_ln"), l + 1)
                stt(fg, fg, 0.0, rowe, ALU.min, ALU.subtract)
                dve.drain()
                v.tensor_tensor_scan(rowF, cst("reset", 4), fg, 0.0, ALU.mult, ALU.add)
                v.tensor_tensor_scan(rowm[:, 0:TP], fg[:, 0:TP], ig[:, 0:TP], 0.0, ALU.add, ALU.max)
                for s in range(NSEQ):
                    q = slice(TP + s * TS, TP + (s + 1) * TS)
                    v.tensor_tensor_scan(rowm[:, q], fg[:, q], ig[:, q], msS[0:4, s:s + 1], ALU.add, ALU.max)
                v.memset(ms0[0:4, 0:1], 0.0)
                dve.drain()
                tt(rowM, rowm, rowF, ALU.subtract)
                tt(rowt, ig, rowF, ALU.subtract)
                v.tensor_copy(ms0[0:4, 1:NCH], rowm[:, C - 1:TP - C:C])
                dve.drain()
                tt(rowwp[:, 0:TP].rearrange("p (c t) -> p c t", c=NCH), ms0[0:4, :].unsqueeze(2).to_broadcast([4, NCH, C]),
                   rowM[:, 0:TP].rearrange("p (c t) -> p c t", c=NCH), ALU.subtract)
                tt(rowwp[:, TP:T].rearrange("p (c t) -> p c t", c=NSEQ), msS[0:4, :].unsqueeze(2).to_broadcast([4, NSEQ, TS]),
                   rowM[:, TP:T].rearrange("p (c t) -> p c t", c=NSEQ), ALU.subtract)
                sig("rows_logs")
                for hd in range(MH):
                    ts_(negM[:, hd, :], rowM, cst("negid", 4)[:, hd:hd + 1], None, ALU.mult)
                dve.wait_ge(S("rows_exp"), l + 1)
                sig("rows_done")
                dve.wait_ge(S("ga_ln"), l + 1)
                stt(gb, gb, 0.0, tmp1, ALU.min, ALU.subtract)
                dve.drain()
                v.tensor_tensor_scan(tmp2, cst("reset"), gb, 0.0, ALU.mult, ALU.add)
                sig("ga_cum")
                dve.wait_ge(S("conv_exp"), l + 1)
                one_over_one_plus(wpb)
                tt(uc, uc, wpb, ALU.mult)
                sig("conv_done")
                dve.wait_ge(S("ga_decay"), l + 1)
                dve.wait_ge(S("in_half_ready"), l + 1)
                for hd in range(GH):
                    r = slice(GK * hd, GK * hd + GK)
                    stt(qm[r, hd, :], gq[r, :], GK ** -0.5, geb[r, :], ALU.mult, ALU.mult)
                tt(kt, gk, gb, ALU.mult)
                sig("gla_inputs")
                for j in range(2):
                    v.tensor_copy(cns[:, j, :, DH:2 * DH], nst[:, j, :].unsqueeze(2).to_broadcast([P, NSEQ, DH]))
                sig("states_ready")
                dve.wait_ge(S("spread_ready"), l + 1)
                for j in range(2):
                    tt(mqw[:, j, :, :], mqm[:, j, :, :], wpb[:, j, :].unsqueeze(1).to_broadcast([P, 2, T]), ALU.mult)
                sig("mqw_done")
                for c in range(NCH + 1):
                    smp = c == NCH
                    n = NS if smp else C
                    w = 4 * n
                    lastc = c * C + n - 1
                    key = ("ga_s", l, c)
                    full(dve, key)
                    rel(tt(am[0:n, 0:w], bank(key)[0:n, 0:w], cst("tri_s" if smp else "tri", n), ALU.mult), key, "D")
                    dve.wait_ge(S("w_ready"), (NCH + 1) * l + c + 1)
                    key = ("qk", l, c)
                    full(dve, key)
                    rel(tt(qkw[0:n, 0:w], bank(key)[0:n, 0:w], wd_[0:n, 0:w], ALU.mult), key, "D")
                    if smp:
                        v.tensor_reduce(ws[0:n, :], wd_[0:n, 0:w].rearrange("p (h s t) -> p h s t", h=4, s=NSEQ)[:, :, :, TS - 1], AX.X, ALU.add)
                        dve.drain()
                        wlast_ = ws[0:n, :].unsqueeze(2)
                    else:
                        wlast_ = wd_[0:n, 0:w].rearrange("p (h t) -> p h t", h=4)[:, :, n - 1:n]
                    key = ("ktok", l, c)
                    full(dve, key)
                    i = tt(kws[0:n, :, :], bank(key)[0:n, 0:256].rearrange("p (h d) -> p h d", h=MH), wlast_.to_broadcast([n, MH, DH]), ALU.mult)
                    rel(i, key, "D")
                    sig("kws_done")
                    seqm = cst("seqmask", NS).unsqueeze(2).to_broadcast([NS, NSEQ, DH])
                    if smp:
                        drained_by_other(dve, ("gtok", l, c))
                        for hd in range(GH):
                            if hd >= 2:
                                dve.wait_ge(S("gla_vm_read"), (GH - 1) * l + hd - 1)
                            tt(vm[0:n, hd % 2, :].rearrange("p (s v) -> p s v", s=NSEQ),
                               gtok[0:n, hd * GV:(hd + 1) * GV].unsqueeze(1).to_broadcast([n, NSEQ, GV]), seqm, ALU.mult)
                            sig("gla_vmask")
                        key = ("gs", l, c)
                        full(dve, key)
                        rel(tt(sgs, sgs, bank(key).rearrange("p (s v) -> p s v", s=NSEQ), ALU.add), key, "D")
                        dve.drain()
                        tt(sgs, sgs, geb[:, TP + TS - 1:T:TS].unsqueeze(2).to_broadcast([P, NSEQ, GV]), ALU.mult)
                        sig("gla_state")
                        drained_by_other(dve, ("vtok", l, c))
                        for hd in range(MH):
                            if hd == 2:
                                dve.wait_ge(S("ml_vm_read"), 2 * l + 1)
                            if hd == 3:
                                full(dve, ("mu_c", l, 0))
                            tt(vm[0:n, hd % 2, :].rearrange("p (s v) -> p s v", s=NSEQ),
                               vaug[0:n, hd, 0:DH].unsqueeze(1).to_broadcast([n, NSEQ, DH]), seqm, ALU.mult)
                            sig("ml_vmask")
                            if hd in (1, 3):
                                j = hd // 2
                                wl = wpb[:, j, TP + TS - 1:T:TS].unsqueeze(2).to_broadcast([P, NSEQ, 2 * DH])
                                full(dve, ("mu_n", l, j))
                                tt(cns[:, j, :, :], cns[:, j, :, :], wl, ALU.mult)
                                dve.drain()
                                for x, nm in enumerate(("mu_c", "mu_n")):
                                    key = (nm, l, j)
                                    cv = cns[:, j, :, x * DH:(x + 1) * DH]
                                    rel(tt(cv, cv, bank(key).rearrange("p (s v) -> p s v", s=NSEQ), ALU.add), key, "D")
                        sig("ml_state")
                    else:
                        key = ("gs", l, c)
                        full(dve, key)
                        rel(tt(sg, sg, bank(key)[:, 0:GV], ALU.add), key, "D")
                        dve.drain()
                        ts_(sg, sg, geb[:, lastc:lastc + 1], None, ALU.mult)
                        sig("gla_state")
                        key = ("mu", l, c)
                        full(dve, key)
                        b = bank(key)
                        stt(cn[:, 0, :], cn[:, 0, :], wpb[:, 0, lastc:lastc + 1], b[:, 0:P], ALU.mult, ALU.add)
                        rel(stt(cn[:, 1, :], cn[:, 1, :], wpb[:, 1, lastc:lastc + 1], b[:, P:2 * P], ALU.mult, ALU.add), key, "D")
                        sig("ml_state")
                dve.wait_ge(S("chunks_out"), l + 1)
                stt(nd[:, 1, :, :], nd[:, 1, :, :], -1.0, nd[:, 1, :, :], ALU.mult, ALU.max)
                dve.drain()
                tt(nd[:, 1, :, :], nd[:, 1, :, :], enmb, ALU.max)
                dve.drain()
                v.reciprocal(nd[:, 1, :, :], nd[:, 1, :, :])
                dve.drain()
                tt(nd[:, 0, :, :], nd[:, 0, :, :], nd[:, 1, :, :], ALU.mult)
                dve.wait_ge(S("mo_exp"), l + 1)
                one_over_one_plus(mo)
                tt(nd[:, 0, :, :], nd[:, 0, :, :], mo, ALU.mult)
                sig("ml_h")
                dve.wait_ge(S("gr_exp"), l + 1)
                sl = mqm[:, 0, :, :]
                one_over_one_plus(sl)
                tt(sl, sl, gr, ALU.mult)
                dve.wait_ge(S("gla_root"), l + 1)
                for j in range(2):
                    stt(og[:, j, :], og[:, j, :], col("gla_norm", l), gv[:, j, :], ALU.mult, ALU.mult)
                dve.drain()
                tt(mix[:, 4:6, :], og, sl, ALU.mult)
                for j in range(2):
                    for h in range(2):
                        key = ("mm_", l, j, h)
                        full(dve, key)
                        z = nd[:, 0, j, SH[h]]
                        rel(stt(z, bank(key)[:, 0:HALF], -1.0 / DH, z, ALU.mult, ALU.add), key, "D")
                sig("ml_centred")
                dve.wait_ge(S("ml_root"), l + 1)
                for j in range(2):
                    stt(mix[:, 6 + j, :], nd[:, 0, j, :], col("ml_norm", l, j), mk[:, j, :], ALU.mult, ALU.mult)
                dve.drain()
                for j in range(2):
                    stt(mix[:, 6 + j, :], uc[:, j, :], col("ml_skip", l, j), mix[:, 6 + j, :], ALU.mult, ALU.add)
                barrier(dve, "dve")

                dve.wait_ge(S("pages_table_loaded"), 16 * 8 * (l + 1))
                ts_(idx, ptab, float(ROWS_PAGE), cst("rowrem")[:, l:l + 1], ALU.mult, ALU.add)
                sig("rows_to_gather")
                tt(kro[0:ROPE, :], small[ROPE:2 * ROPE, :], cst("sin")[ROPE:2 * ROPE, :], ALU.mult)
                tt(small[0:ROPE, :], small[0:ROPE, :], cst("cos")[0:ROPE, :], ALU.mult)
                dve.drain()
                tt(kro[0:ROPE, :], kro[0:ROPE, :], small[0:ROPE, :], ALU.add)
                dve.wait_ge(S("cq_root"), l + 1)
                for k in range(2):
                    stt(cq[:, k, :], cq[:, k, :], col("q_norm", l, k), lnr[:, :], ALU.mult, ALU.mult)
                sig("cq_done")
                stt(ckv, ckv, col("kv_norm", l), qra[:, 0, :], ALU.mult, ALU.mult)
                sig("ckv_done")
                for m in range(6, 8):
                    for h in range(2):
                        copy(("q", l, m, h), qrb[:, m - 6, SH[h]], bank(("q", l, m, h))[:, 0:HALF])
                dve.wait_ge(S("qra_ready"), l + 1)
                dve.drain()
                for src, tab in ((qra, "cos"), (qrb, "sin")):
                    tt(src, src, cst(tab).unsqueeze(1).to_broadcast([P, 2, T]), ALU.mult)
                dve.drain()
                for a in range(4):
                    a_ = slice(32 * a, 32 * a + 32)
                    tt(qr0[0:ROPE, :, a:H:4].rearrange("p t c -> p c t"), qra[a_], qrb[a_], ALU.add)
                dve.wait_ge(S("qrM_zeroed"), l + 1)
                dve.drain()
                for a in range(4):
                    v.tensor_copy(qrM[32 * a:32 * a + 32, a, :, :], qr0[0:ROPE, TP:T, :])
                for hd in range(H):
                    copy(("qlat", l, hd, 0), qlat[:, SH[0], hd], bank(("qlat", l, hd, 0))[:, 0:HALF])
                barrier(dve, "dve")

                for step in range(NQ + 2):
                    if step < NQ:
                        i_ = step
                        W = QT * (i_ + 1)
                        sl = i_ % NPB
                        for x, (a, z) in enumerate(((0, min(W, 512)), (512, W))):
                            if z <= a:
                                continue
                            full(dve, ("s", l, i_, x))
                            v.tensor_reduce(mxq[:, sl, x:x + 1], bank(("s", l, i_, x))[:, 0:z - a], AX.X, ALU.max)
                        dve.drain()
                        if W > 512:
                            tt(mxq[:, sl, 0:1], mxq[:, sl, 0:1], mxq[:, sl, 1:2], ALU.max)
                            dve.drain()
                        ts_(nmq[:, sl:sl + 1], mxq[:, sl, 0:1], -SCALE, None, ALU.mult)
                        sig("pq_max")
                    if 1 <= step <= NQ:
                        i_ = step - 1
                        W = QT * (i_ + 1)
                        sl = i_ % NPB
                        dve.wait_ge(S("pq_exp"), NQ * l + i_ + 1)
                        if W > 512:
                            tt(smq[:, sl, 0:1], smq[:, sl, 0:1], smq[:, sl, 1:2], ALU.add)
                            dve.drain()
                        v.reciprocal(rsq[:, sl:sl + 1], smq[:, sl, 0:1])
                        dve.drain()
                        ts_(pq[:, sl, 0:W], pq[:, sl, 0:W], rsq[:, sl:sl + 1], None, ALU.mult)
                        sig("pq_normed")
                        if i_ % 2 == 0:
                            prompt_pT(dve, l, i_, v.tensor_copy, "D")
                    if step >= 2:
                        i_ = step - 2
                        key = ("o", l, i_)
                        copy(key, qlat[:, QT * i_:QT * (i_ + 1), :],
                             bank(key)[:, 0:P].rearrange("p (t h) -> p t h", h=H))
                barrier(dve, "dve")

                for p_ in range(NSEQ // 2):
                    for s in range(2):
                        for q in (0, 2):
                            copy(("kT", l, p_, s, q), kT[:, s, q * 512:(q + 1) * 512], bank(("kT", l, p_, s, q)))
                        if s == 0:
                            copy(("krT", l, p_, 0), krT[:, 0, :], bank(("krT", l, p_, 0)))
                    for q in range(5):
                        key = ("ss", l, p_, q) if q < 4 else ("sn", l, p_)
                        full(dve, key)
                        v.tensor_reduce(mx[:, q:q + 1], bank(key)[:, 0:(512 if q < 4 else QT)], AX.X, ALU.max)
                    dve.drain()
                    v.tensor_reduce(mx[:, 5:6], mx[:, 0:5], AX.X, ALU.max)
                    dve.drain()
                    ts_(nmx[:, 0:1], mx[:, 5:6], -SCALE, None, ALU.mult)
                    sig("ps_max")
                    dve.wait_ge(S("ps_exp"), l * (NSEQ // 2) + p_ + 1)
                    v.tensor_reduce(sums[:, 5:6], sums[:, 0:5], AX.X, ALU.add)
                    dve.drain()
                    v.reciprocal(rs[:, 0:1], sums[:, 5:6])
                    dve.drain()
                    ts_(psm, psm, rs[:, 0:1], None, ALU.mult)
                    sig("ps_normed")
                    for q in (0, 2):
                        copy(("psT", l, p_, q), psT[:, q * 512:(q + 1) * 512], bank(("psT", l, p_, q)))
                    copy(("psT", l, p_, 4), psT[0:QT, 16 * P:17 * P], bank(("psT", l, p_, 4))[0:QT, 0:P])
                    key = ("so", l, p_)
                    full(dve, key)
                    for s in range(2):
                        c0 = TP + (2 * p_ + s) * TS
                        i = v.tensor_copy(qlat[:, c0:c0 + TS, :],
                                          bank(key)[:, 64 * s:64 * s + 64].rearrange("p (t h) -> p t h", h=H))
                    rel(i, key, "D")
                for j in range(4):
                    copy(("omla", l, j, 0), mix[:, j, SH[0]], bank(("omla", l, j, 0))[:, 0:HALF])
                barrier(dve, "dve")
                for m in range(KD):
                    for h in range(2):
                        key = ("out", l, m, h)
                        full(dve, key)
                        rel(stt(zT[:, m, SH[h]], xT[:, m, SH[h]], ALPHA, bank(key)[:, 0:HALF], ALU.mult, ALU.add), key, "D")
                layer_norm(2 * l + 1, "ln1_g", "ln1_b", l)

                v.memset(sc, 1.0)
                sig("logits_zeroed")
                ts_(zT, xT, ALPHA, None, ALU.mult)
                dve.wait_ge(S("logits_exp"), l + 1)
                one_over_one_plus(sc)
                tt(sel, sc, rbias[:, :].unsqueeze(1).to_broadcast([P, TT, E]), ALU.add)
                dve.drain()
                se = sel.rearrange("p t (g e) -> p t g e", e=4)
                hi1, lo1, hi2, lo2, ta, tb = g4
                e_ = [se[:, :, :, k] for k in range(4)]
                tt(hi1, e_[0], e_[1], ALU.max)
                tt(lo1, e_[0], e_[1], ALU.min)
                tt(hi2, e_[2], e_[3], ALU.max)
                tt(lo2, e_[2], e_[3], ALU.min)
                dve.drain()
                tt(ta, hi1, hi2, ALU.min)
                tt(tb, lo1, lo2, ALU.max)
                tt(hi1, hi1, hi2, ALU.max)
                dve.drain()
                tt(ta, ta, tb, ALU.max)
                dve.drain()
                tt(hi1, hi1, ta, ALU.add)
                dve.drain()

                def first_max(x, mx_, out, rank, n):
                    v.tensor_reduce(mx_, x, AX.X, ALU.max)
                    dve.drain()
                    tt(out, x, mx_.unsqueeze(2).to_broadcast([P, TT, n]), ALU.is_equal)
                    dve.drain()
                    tt(out, out, cst(rank).unsqueeze(1).to_broadcast([P, TT, n]), ALU.mult)
                    dve.drain()
                    v.tensor_reduce(mx_, out, AX.X, ALU.max)
                    dve.drain()
                    tt(out, out, mx_.unsqueeze(2).to_broadcast([P, TT, n]), ALU.is_equal)
                    dve.drain()

                first_max(hi1, g1[0], lo1, "rank4", 4)
                ts_(lo2, lo1, -1.0, -NEG, ALU.add, ALU.mult)
                dve.drain()
                g_of = lo1.unsqueeze(3).to_broadcast([P, TT, 4, 4])
                tt(r3.rearrange("p t (g e) -> p t g e", e=4), se, g_of, ALU.mult)
                dve.drain()
                tt(r3.rearrange("p t (g e) -> p t g e", e=4), r3.rearrange("p t (g e) -> p t g e", e=4),
                   lo2.unsqueeze(3).to_broadcast([P, TT, 4, 4]), ALU.add)
                dve.drain()
                first_max(r3, g1[1], r1, "rank16", E)
                stt(r3, r1, 2 * NEG, r3, ALU.mult, ALU.add)
                dve.drain()
                first_max(r3, g1[2], r2, "rank16", E)
                tt(r1, r1, r2, ALU.add)
                dve.drain()
                tt(w16, r1, sc, ALU.mult)
                dve.drain()
                v.tensor_reduce(g1[0], w16, AX.X, ALU.add)
                dve.drain()
                v.reciprocal(g1[0], g1[0])
                dve.drain()
                tt(w16, w16, g1[0].unsqueeze(2).to_broadcast([P, TT, E]), ALU.mult)
                sig("weights16")
                def gated(e):
                    drained_by_other(dve, ("wb", l, e, 1))
                    for f in range(2):
                        for h in range(2):
                            n = (l * E + e) * 4 + 2 * f + h
                            x = hx[:, f, SH[h]]
                            dve.wait_ge(S("hg_exp"), n + 1)
                            ts_(x, x, 1.0, None, ALU.add)
                            dve.drain()
                            v.reciprocal(x, x)
                            dve.drain()
                            rel(tt(x, bank(("hg", l, e, f, h))[:, 0:HALF], x, ALU.mult), ("hg", l, e, f, h), "D")
                            dve.drain()
                            full(dve, ("hu", l, e, f, h))
                            rel(tt(x, bank(("hu", l, e, f, h))[:, 0:HALF], x, ALU.mult), ("hu", l, e, f, h), "D")
                            dve.drain()
                            tt(hh[:, e % 2, f, SH[h]], x, wb[:, e % 2, SH[h]], ALU.mult)
                            sig("h_done")

                def add_up(e):
                    for m in range(KD):
                        for h in range(2):
                            key = ("dn", l, e, m, h)
                            full(dve, key)
                            z = zT[:, m, SH[h]]
                            rel(tt(z, z, bank(key)[:, 0:HALF], ALU.add), key, "D")
                    dve.drain()

                gated(0)
                for e in range(E):
                    if e + 1 < E:
                        gated(e + 1)
                    add_up(e)
                layer_norm(2 * l + 2, "ln2_g", "ln2_b", l)
            barrier(dve, "dve")
            for t in range(TT):
                r = P if t < TT - 1 else LAST
                copy(("yout", t, 0), xtok[0:r, t, 0:512], bank(("yout", t, 0))[0:r, :])
            sig("y_ready")

        @block_.gpsimd
        def _(pool):
            g = nc.gpsimd
            g.memset(vecrows[:, :], 0.0)
            pool.drain().then_inc(S("vec_zeroed"), 1)
            for l in range(DEPTH):
                barrier(pool, "pool")
                g.memset(wsm[:, :, 80:96], 0.0)
                for z in (wqk, qm, mqm, mup[:, :, 0:CONV - 1], sg, cn):
                    g.memset(z, 0.0)
                g.memset(vaug[:, :, DH:2 * DH], 1.0)
                pool.drain().then_inc(S("rec_zeroed"), 1)
                barrier(pool, "pool")
                g.memset(qrM, 0.0)
                pool.drain().then_inc(S("qrM_zeroed"), 1)
                barrier(pool, "pool")
                barrier(pool, "pool")
                for p_ in range(NSEQ // 2):
                    if p_ == 0:
                        pool.wait_ge(S("rows_to_gather"), l + 1)
                    else:
                        pool.wait_ge(filled, index[("so", l, p_ - 1)] + 1)
                    for s in range(2):
                        sq_ = 2 * p_ + s
                        off = bass.IndirectOffsetOnAxis(ap=idx[:, sq_:sq_ + 1], axis=0)
                        g.indirect_dma_start(kg[:, s, :], None, I["cache_kv_latent"].rearrange("l n (a b) r -> (l n a) (b r)", b=KEYS_ROW), off)\
                            .then_inc(S(f"pages{s}"), 16)
                        g.indirect_dma_start(krg[:, s, :], None, I["cache_k_rope"].rearrange("l n (a b) r -> (l n a) (b r)", b=KEYS_ROW), off)\
                            .then_inc(S(f"pages{s}"), 16)
                barrier(pool, "pool")
            barrier(pool, "pool")

        @block_.sync
        def _(sp):
            def ld(dst, src, name):
                return sp.dma_start(dst, src, allow_slow_non_contiguous=True).then_inc(S(name), 16)

            def load_slot(u):
                per = len(CHUNKS) + KD
                l, j = u // per, u % per
                if u >= NSLOT:
                    sp.wait_ge(filled, index[wlast[u - NSLOT]] + 1)
                if j < len(CHUNKS):
                    c0 = COL[CHUNKS[j][0]] + P * CHUNKS[j][1]
                    src = I["w_in"][l][:, c0:c0 + P]
                else:
                    m = j - len(CHUNKS)
                    src = I["w_out"][l][:, m * P:(m + 1) * P]
                ld(wslot[:, u % NSLOT, :, :], src.rearrange("(k p) c -> p k c", p=P), f"wslot{u % NSLOT}")

            ld(const[:, :], I["consts"], "const_loaded")
            x = I["x_prompt"][0]
            ld(xtok[0:N_META, 0, :], I["meta_tokens"], "x_loaded")
            ld(xtok[N_META:P, 0, :], x[0:P - N_META, :], "x_loaded")
            ld(xtok[:, 1:4, :], x[P - N_META:4 * P - N_META, :].rearrange("(t p) d -> p t d", p=P), "x_loaded")
            ld(xtok[0:N_META, 4, :], x[4 * P - N_META:SEQ, :], "x_loaded")
            ld(xtok[N_META:N_META + NS, 4, :], I["x_sample"].rearrange("s t d -> (s t) d"), "x_loaded")
            sp.wait_ge(S("vec_zeroed"), 1)
            src = dict(q_norm="mla_q_norm", kv_norm="mla_kv_norm", b_a="gla_b_a", conv_w="ml_conv_w", conv_b="ml_conv_b",
                       ml_norm="ml_norm", ml_skip="ml_skip", ln1_g="ln1_g", ln1_b="ln1_b", ln2_g="ln2_g", ln2_b="ln2_b")
            for name, w in VEC:
                r = VROW[name]
                if name == "gla_norm":
                    for a in range(2):
                        ld(vecrows[r:r + DEPTH, 64 * a:64 * a + 64], I["gla_norm"], "vec_loaded")
                elif name == "conv_w":
                    ld(vecrows[r:r + DEPTH * w, :], I["ml_conv_w"].rearrange("l i (k p) -> (l i k) p", p=P), "vec_loaded")
                else:
                    ld(vecrows[r:r + DEPTH * w, :], I[src[name]].rearrange("l (k p) -> (l k) p", p=P), "vec_loaded")
            for name in ("ln_in_g", "ln_in_b"):
                r = VROW[name]
                ld(vecrows[r:r + KD, :], I[name].rearrange("(k p) -> k p", p=P), "vec_loaded")
            ld(bif[:, 0:DEPTH], I["ml_b_i"].rearrange("l h -> h l"), "vec_loaded")
            ld(bif[:, DEPTH:2 * DEPTH], I["ml_b_f"].rearrange("l h -> h l"), "vec_loaded")
            for u in range(NSLOT):
                load_slot(u)
            ld(routerw[:, :, :], I["router_w"].rearrange("(k p) e -> p k e", p=P), "router_loaded")
            ld(rbias[:, :], I["router_bias"].rearrange("(a e) -> a e", a=1).to_broadcast([P, E]), "router_loaded")

            per = len(CHUNKS) + KD
            for l in range(DEPTH):
                barrier(sp, "sp")
                w = I["w_in"][l].rearrange("(k p) c -> p k c", p=P)
                kr = COL["kr"]
                for d0, s0, n in ((0, kr, ROPE), (32, kr + 16, 16), (48, kr, 16), (64, COL["ga"], GR), (96, COL["mi"], 2 * MH)):
                    ld(wsm[:, :, d0:d0 + n], w[:, :, s0:s0 + n], "wsmall_loaded")
                ld(wa[64:64 + GR, :], I["gla_w_a"][l], "rec_loaded")
                for c in range(2):
                    for k in range(CONV - 1):
                        ld(mus[:, c, :, k], I["state_mlstm_conv"][l][:, k, c * P:(c + 1) * P].rearrange("s p -> p s"), "rec_loaded")
                ld(sgs, I["state_gla"][l].rearrange("s h k v -> (h k) s v"), "rec_loaded")
                for j in range(2):
                    ld(cns[:, j, :, 0:DH], I["state_mlstm_C"][l][:, 2 * j:2 * j + 2].rearrange("s h d v -> (h d) s v"), "rec_loaded")
                    ld(nst[:, j, :], I["state_mlstm_n"][l][:, 2 * j:2 * j + 2].rearrange("s h d -> (h d) s"), "rec_loaded")
                ld(msS[0:4, :], I["state_mlstm_m"][l].rearrange("s h -> h s"), "rec_loaded")
                sp.wait_ge(S("rec_zeroed"), l + 1)
                for qk, nm in enumerate(("ml_w_q", "ml_w_k")):
                    for hd in range(MH):
                        a = slice(64 * (hd % 2), 64 * (hd % 2) + 64)
                        ld(wqk[a, qk, hd // 2, a], I[nm][l, hd], "wqk_loaded")
                sp.wait_ge(S("small_ready"), l + 1)
                ld(ig, small[96:100, :], "rows_moved")
                ld(fg, small[100:104, :], "rows_moved")
                for j in range(NSLOT, len(CHUNKS) + NSLOT):
                    load_slot(l * per + j)
                sp.wait_ge(S("gla_state"), (NCH + 1) * (l + 1))
                sp.wait_ge(S("ml_state"), (NCH + 1) * (l + 1))
                n_out = 0
                for dst, srcv in (
                        (O["p_gla"][l, 0].rearrange("h k v -> (h k) v"), sg),
                        (O["s_gla"][l].rearrange("s h k v -> (h k) s v"), sgs),
                        (O["p_m"][l, 0].rearrange("(h a) -> h a", a=1), rowm[:, TP - 1:TP]),
                        (O["s_m"][l].rearrange("s h -> h s"), rowm[:, TP + TS - 1:T:TS])):
                    ld(dst, srcv, "states_out")
                    n_out += 1
                for j in range(2):
                    hs = slice(2 * j, 2 * j + 2)
                    fs = slice(j * P, (j + 1) * P)
                    for dst, srcv in (
                            (O["p_C"][l, 0, hs].rearrange("h d v -> (h d) v"), cn[:, j, 0:DH]),
                            (O["p_n"][l, 0, hs].rearrange("h (d a) -> (h d) a", a=1), cn[:, j, DH:DH + 1]),
                            (O["s_C"][l][:, hs].rearrange("s h d v -> (h d) s v"), cns[:, j, :, 0:DH]),
                            (O["s_n"][l][:, hs].rearrange("s h d -> (h d) s"), cns[:, j, :, DH]),
                            (O["p_conv"][l, 0][:, fs].rearrange("i p -> p i"), mup[:, j, TP:TP + CONV - 1]),
                            *((O["s_conv"][l][:, k, fs].rearrange("s p -> p s"), mus[:, j, :, TS + k]) for k in range(CONV - 1))):
                        ld(dst, srcv, "states_out")
                        n_out += 1
                sp.wait_ge(S("states_out"), 16 * n_out * (l + 1))
                barrier(sp, "sp")

                uq = I["mla_w_uq"][l].rearrange("(k p) (h c) -> k p h c", p=P, h=H)
                for k in range(2):
                    for d0, s0, n, st in ((0, 0, NOPE, 64), (512, NOPE, ROPE, 32), (768, NOPE + 16, 16, 32), (784, NOPE, 16, 32)):
                        d = wuq[:, k, d0 - d0 % 32:(d0 - d0 % 32) + H * st].rearrange("p (h c) -> p h c", h=H)
                        ld(d[:, :, d0 % 32:d0 % 32 + n], uq[k][:, :, s0:s0 + n], "att_loaded")
                ukv = I["mla_w_ukv"][l].rearrange("r (h c) -> r h c", h=H)
                for x in range(2):
                    ld(wukv[:, 512 * x:512 * (x + 1)].rearrange("p (h c) -> p h c", h=H), ukv[:, :, 64 * x:64 * (x + 1)], "att_loaded")
                for r in range(ROWS_PAGE):
                    ld(ptab[r:P:ROWS_PAGE, :], I["page_table"].rearrange("s g -> g s"), "pages_table_loaded")
                sp.wait_ge(S("ctok_ready"), l + 1)
                for nm, a, z in (("kv", 0, LAT), ("kr", LAT, LAT + ROPE)):
                    ld(O["p_" + nm][l, 0, 0:4 * P].rearrange("(t p) r -> p t r", p=P), ctok[:, 0:4, a:z], "cache_rows_out")
                    ld(O["p_" + nm][l, 0, 4 * P:TP], ctok[0:QT, 4, a:z], "cache_rows_out")
                    ld(O["s_" + nm][l].rearrange("(a b) t r -> (b t) a r", b=2), ctok[0:QT, 5:9, a:z], "cache_rows_out")
                barrier(sp, "sp")
                barrier(sp, "sp")
                sp.wait_ge(S("cache_rows_out"), 96 * (l + 1))
                barrier(sp, "sp")

                def load_expert(e):
                    if e >= 2:
                        sp.wait_ge(filled, index[("hu", l, e - 2, 1, 1)] + 1)
                    ld(wg[:, e % 2, :, :], I["moe_w_gate"][l, e].rearrange("(k p) f -> p k f", p=P), f"wgu{e % 2}")
                    ld(wu[:, e % 2, :, :], I["moe_w_up"][l, e].rearrange("(k p) f -> p k f", p=P), f"wgu{e % 2}")
                    if e >= 2:
                        sp.wait_ge(filled, index[("dn", l, e - 2, KD - 1, 1)] + 1)
                    ld(wdn[:, e % 2, :, :], I["moe_w_down"][l, e].rearrange("(k p) d -> p k d", p=P), f"wdn{e % 2}")

                load_expert(0)
                load_expert(1)
                for j in range(NSLOT, KD):
                    load_slot(l * per + len(CHUNKS) + j)
                for e in range(2, E):
                    load_expert(e)
                if l + 1 < DEPTH:
                    for j in range(NSLOT):
                        load_slot((l + 1) * per + j)
            barrier(sp, "sp")
            sp.wait_ge(S("y_ready"), 2)
            y = O["y_prompt"][0]
            ld(y[0:P - N_META, :], xtok[N_META:P, 0, :], "y_out")
            ld(y[P - N_META:4 * P - N_META, :].rearrange("(t p) d -> p t d", p=P), xtok[:, 1:4, :], "y_out")
            ld(y[4 * P - N_META:SEQ, :], xtok[0:N_META, 4, :], "y_out")
            ld(O["y_sample"].rearrange("s t d -> (s t) d"), xtok[N_META:N_META + NS, 4, :], "y_out")
            sp.wait_ge(S("y_out"), 64)


_INS = ["x_prompt", "x_sample", "cache_kv_latent", "cache_k_rope", "state_gla", "state_mlstm_C", "state_mlstm_n",
        "state_mlstm_m", "state_mlstm_conv", "page_table", "meta_tokens", "ln_in_g", "ln_in_b", "w_in", "mla_q_norm",
        "mla_w_uq", "mla_kv_norm", "mla_w_ukv", "gla_w_a", "gla_b_a", "gla_norm", "ml_conv_w", "ml_conv_b", "ml_w_q", "ml_w_k",
        "ml_b_i", "ml_b_f", "ml_norm", "ml_skip", "w_out", "ln1_g", "ln1_b", "ln2_g", "ln2_b", "router_w", "router_bias",
        "moe_w_gate", "moe_w_up", "moe_w_down"]


def _states(b, rows):
    return [(DEPTH, b, rows, LAT), (DEPTH, b, rows, ROPE), (DEPTH, b, GH, GK, GV), (DEPTH, b, MH, DH, DH), (DEPTH, b, MH, DH),
            (DEPTH, b, MH), (DEPTH, b, CONV - 1, MH * DH)]


_STATE = ["kv", "kr", "gla", "C", "n", "m", "conv"]
_OUTS = [("y_prompt", (1, SEQ, D)), ("y_sample", (NSEQ, TS, D))]
_OUTS += [("p_" + n, s) for n, s in zip(_STATE, _states(1, TP))] + [("s_" + n, s) for n, s in zip(_STATE, _states(NSEQ, TS))]


def kernel(**inputs):
    import numpy as _np
    import concourse.bacc as _bacc
    from concourse import mybir as _mybir
    from concourse.bass_utils import run_bass_kernel_spmd as _run

    nc = _bacc.Bacc("TRN2", target_bir_lowering=False, num_devices=1)
    table, at = shape_constants()
    arrays, ins, outs = {"in_consts": table}, {}, {}
    ins["consts"] = nc.dram_tensor("in_consts", table.shape, _mybir.dt.float32, kind="ExternalInput").ap()
    for name in _INS:
        a = _np.ascontiguousarray(inputs[name])
        arrays["in_" + name] = a
        ins[name] = nc.dram_tensor("in_" + name, a.shape, _mybir.dt.from_np(a.dtype), kind="ExternalInput").ap()
    for name, shape in _OUTS:
        outs[name] = nc.dram_tensor("out_" + name, shape, _mybir.dt.float32, kind="ExternalOutput").ap()
    build(nc, ins, outs, at, table.shape[1])
    r = _run(nc, [arrays], core_ids=[0])
    return tuple(r.results[0]["out_" + name] for name, _ in _OUTS)
```

```python
from contextlib import ExitStack

import numpy as np
import concourse.bass as bass
from concourse import mybir

F32 = mybir.dt.float32
I32 = mybir.dt.int32
ALU = mybir.AluOpType
ACT = mybir.ActivationFunctionType
AX = mybir.AxisListType

P = 128
D = 1024
KD = D // P
DEPTH = 2
N_META, SEQ = 16, 512
TP = N_META + SEQ
NSEQ, TS = 8, 8
T = TP + NSEQ * TS
HALF = T // 2
TT = -(-T // P)
LAST = T - (TT - 1) * P
H = 8
LAT, ROPE, NOPE, MV = 128, 32, 64, 64
PAST, PAGE = 2048, 128
NPAGES = PAST // PAGE
POOL = NSEQ * NPAGES * 5 // 4
KEYS_ROW = 16
ROWS_PAGE = PAGE // KEYS_ROW
SCALE = float((NOPE + ROPE) ** -0.5)
GK, GV, GH = 32, 64, 4
GR = 16
TAU = 16.0
MH, DH = 4, 64
CONV = 4
C = 66
NCH = TP // C
NS = NSEQ * TS
E = 16
F = 256
ALPHA = float((2 * DEPTH) ** 0.25)
LN_EPS, RMS_EPS = 1e-5, 1e-6
NEG = -1.0e30
QT = 16
NQ = TP // QT
NOVER = 2 * T // P
NTILE = E + NOVER
SH = [slice(0, HALF), slice(HALF, T)]
COL = dict(cq=0, ckv=256, kr=384, gq=416, gk=544, gv=672, ga=928, gr=944, mu=1200, mv=1456, mi=1712, mo=1720)
CHUNKS = [("mu", 0), ("mu", 1), ("gq", 0), ("gk", 0), ("gv", 0), ("gv", 1), ("mv", 0), ("mv", 1),
          ("gr", 0), ("gr", 1), ("mo", 0), ("mo", 1), ("cq", 0), ("cq", 1), ("ckv", 0)]
EARLY = 8
NSLOT = 4
SMALL = 104
VEC = [("q_norm", 2), ("kv_norm", 1), ("b_a", 1), ("gla_norm", 1), ("conv_w", 8), ("conv_b", 2), ("ml_norm", 2),
       ("ml_skip", 2), ("ln1_g", 8), ("ln1_b", 8), ("ln2_g", 8), ("ln2_b", 8)]
VROW, _n = {}, 0
for _k, _w in VEC:
    VROW[_k] = _n
    _n += DEPTH * _w
VROW["ln_in_g"] = _n
VROW["ln_in_b"] = _n + KD
NVEC = _n + 2 * KD
VW = dict(VEC)


def shape_constants():
    f = np.float32
    p = np.arange(P)
    out, at, n = [], {}, 0

    def put(name, a):
        nonlocal n
        a = np.asarray(a, f).reshape(a.shape[0], -1)
        full = np.zeros((P, a.shape[1]), f)
        full[:a.shape[0]] = a
        at[name] = (n, a.shape[1])
        n += a.shape[1]
        out.append(full)

    put("ident", np.eye(P))
    put("ones", np.ones((P, P)))
    put("block", (p[:, None] // 64 == p[None, :] // 64))
    k = np.arange(QT)
    put("mask_q", np.where(p[:, None] >= 8 * k[None, :], 0.0, NEG))
    put("mask_n", np.where((p[:, None] >= 8 * k[None, :]) & (p[:, None] // 64 == k[None, :] // 8), 0.0, NEG))
    s = np.arange(C)
    ok = s[:, None] <= s[None, :]
    put("tri", np.repeat(ok[:, None, :], 4, 1))
    put("trineg", np.where(np.repeat(ok[:, None, :], 4, 1), 0.0, NEG))
    s = np.arange(NS)
    ok = (s[:, None] <= s[None, :]) & (s[:, None] // TS == s[None, :] // TS)
    put("tri_s", np.repeat(ok[:, None, :], 4, 1))
    put("trineg_s", np.where(np.repeat(ok[:, None, :], 4, 1), 0.0, NEG))
    put("seqmask", s[:, None] // TS == np.arange(NSEQ)[None, :])
    put("rowsel", np.repeat(np.eye(4)[:, :, None], C, 2))
    put("negid", -np.eye(4))
    put("pairsel", (np.arange(4)[:, None, None] == 2 * np.arange(2)[None, :, None] + p[None, None, :] // 64))
    put("before", p[:, None] < p[None, :])
    put("valid", (p[:, None] + P * np.arange(TT)[None, :]) < T)
    put("token", p[:, None] + P * np.arange(TT)[None, :])
    put("expert_slot", np.repeat(P * np.arange(E)[None, :], P, 0))
    put("over_slot", np.repeat((E - 1) * P - P * np.arange(E)[None, :], P, 0))
    put("tile_no", np.repeat(np.arange(NOVER)[None, :], P, 0))
    put("epsln", np.full((P, 1), LN_EPS))
    put("epsrms", np.full((P, 1), RMS_EPS))
    put("one", np.ones((P, 1)))
    put("rank16", np.repeat(E - np.arange(E)[None, :], P, 0))
    put("rank4", np.repeat(4 - np.arange(4)[None, :], P, 0))
    put("rowrem", np.stack([p % ROWS_PAGE + l * POOL * ROWS_PAGE for l in range(DEPTH)], 1))
    reset = np.ones((P, T))
    reset[:, 0:TP:C] = 0
    reset[:, TP::TS] = 0
    put("reset", reset)
    half = ROPE // 2
    inv = (f(10000.0) ** (-np.arange(half, dtype=f) / f(half))).astype(f)
    pos = np.concatenate([np.arange(TP), np.tile(PAST + np.arange(TS), NSEQ)]).astype(f)
    ang = (pos[None, :] * inv[:, None]).astype(f)
    put("cos", np.tile(np.cos(ang), (8, 1)))
    put("sin", np.tile(np.concatenate([-np.sin(ang), np.sin(ang)], 0), (4, 1)))
    return np.concatenate(out, 1).astype(f), at


def build(nc, I, O, at, ncols):
    with ExitStack() as ctx:
        def sb(name, shape, dt=F32):
            return ctx.enter_context(nc.sbuf_tensor(name, shape, dt))[tuple(slice(None) for _ in shape)]

        sems = {}

        def S(name):
            if name not in sems:
                sems[name] = ctx.enter_context(nc.semaphore(name))
            return sems[name]

        const = sb("const", [P, ncols])

        def cst(name, rows=P):
            a, w = at[name]
            return const[0:rows, a:a + w]

        ident, ones, block = cst("ident"), cst("ones"), cst("block")
        vecrows = sb("vecrows", [P, P])
        vec = sb("vec", [P, P])
        bif = sb("bif", [4, 2 * DEPTH])
        routerw = sb("routerw", [P, KD, E])
        rbias = sb("rbias", [P, E])
        xT = sb("xT", [P, KD, T])
        zT = sb("zT", [P, KD, T])
        mix = sb("mix", [P, KD, T])
        wslot = sb("wslot", [P, NSLOT, KD, P])
        lnr = sb("lnr", [P, T])
        OVN = 28900
        over = sb("over", [P, OVN])
        ps = ctx.enter_context(nc.psum_tensor("ps", [P, 8, 512], F32))

        def col(name, l, k=0):
            r = VROW[name] + (l * VW[name] if name in VW else 0) + k
            return vec[:, r:r + 1]

        class Area:
            def __init__(self, start):
                self.n = start

            def get(self, *dims):
                w = int(np.prod(dims))
                v = over[:, self.n:self.n + w]
                self.n += w
                assert self.n <= OVN, self.n
                if len(dims) == 2:
                    v = v.rearrange("p (a b) -> p a b", b=dims[1])
                elif len(dims) == 3:
                    v = v.rearrange("p (a b c) -> p a b c", b=dims[1], c=dims[2])
                elif len(dims) == 4:
                    v = v.rearrange("p (a b c d) -> p a b c d", b=dims[1], c=dims[2], d=dims[3])
                return v

        zflat = zT.rearrange("p a b -> p (a b)")
        mflat = mix.rearrange("p a b -> p (a b)")

        def tok(t, rows=P, cols=slice(0, D)):
            v = zflat[0:rows, t * D:(t + 1) * D] if t < 4 else mflat[0:rows, 0:D]
            return v[:, cols]

        def rows_of(t):
            return P if t < TT - 1 else LAST

        base = Area(0)
        cq = base.get(2, T)
        ckv = base.get(T)
        small = base.get(T)
        rec = Area(base.n)
        og = rec.get(2, T)
        gq, gk = og[:, 0, :], og[:, 1, :]
        gv, mo = rec.get(2, T), rec.get(2, T)
        mup = rec.get(2, TP + CONV - 1)
        mus = rec.get(2, NSEQ, TS + CONV - 1)
        qm = rec.get(GH, T)
        kt, geb = mix[:, 6, :], mix[:, 7, :]
        uc = rec.get(2, T)
        weights_at = rec.n
        gr, mv = rec.get(2, T), rec.get(2, T)
        mqm = rec.get(2, 2, T)
        wsm = over[:, rec.n:rec.n + KD * SMALL].rearrange("p (a b) -> p a b", b=SMALL)
        mqw = rec.get(2, 2, T)
        mk = rec.get(2, T)
        wpb = rec.get(2, T)
        nd = rec.get(2, 2, T)
        tmp1, tmp2, gb = nd[:, 0, 0, :], nd[:, 0, 1, :], nd[:, 1, 0, :]
        wqk = rec.get(2, 2, P)
        wa = rec.get(P)
        sg = rec.get(GV)
        sgs = rec.get(NSEQ, GV)
        cn = rec.get(2, 2 * DH)
        cns = rec.get(2, NSEQ, 2 * DH)
        nst = rec.get(2, NSEQ)
        gtok = rec.get(3 * P)
        vaug = rec.get(MH, 2 * DH)
        am = rec.get(4 * C)
        wd_ = rec.get(4 * C)
        qkw = rec.get(4 * C)
        kws = rec.get(MH, DH)
        ws = rec.get(MH)
        rec_end = rec.n
        enmb = zT[:, 0:2, :]
        vm = zT[:, 2:4, 0:512]
        ig, fg, rowF, rowm, rowwp, rowe = (mix[0:4, i, :] for i in range(6))
        rowM, rowt = fg, ig
        negM = zT[0:4, 4:8, :]
        ms0 = rec.get(NCH)
        msS = rec.get(NSEQ)
        att = Area(base.n)
        wukT = att.get(4, P)
        qlat = att.get(T, H)
        ctok = att.get(9, LAT + ROPE)
        kro = att.get(T)
        mx = att.get(8)
        nmx = att.get(2)
        sums = att.get(8)
        rs = att.get(2)
        assert att.n <= weights_at
        att = Area(weights_at)
        wuq = att.get(2, 1024)
        wukv = att.get(1024)
        idx = att.get(NSEQ).bitcast(I32)
        ptab = att.get(NSEQ).bitcast(I32)
        assert att.n <= weights_at + 4 * T + 2 * T
        cq_sq, ckv_sq, ckv_root = mqm[:, 1, :, :], wpb[:, 0, :], wpb[:, 1, :]
        qrM = att.get(4, NS, H)
        pbuf0 = att.n
        qn = att.get(4, T)
        qra = att.get(2, T)
        qrb = att.get(2, T)
        att2 = Area(pbuf0)
        NPB = 5
        pq = att2.get(NPB, TP)
        pT = att2.get(NPB, 5 * P)
        mxq = att2.get(NPB, 2)
        nmq = att2.get(NPB)
        smq = att2.get(NPB, 2)
        rsq = att2.get(NPB)
        att3 = Area(pbuf0)
        kT = att3.get(2, PAST)
        krT = att3.get(2, 512)
        assert att3.n <= att2.n
        att4 = Area(att2.n)
        kgs = [att4.get(2, KEYS_ROW * LAT), zT.rearrange("p a b -> p (a b)")[:, 0:2 * KEYS_ROW * LAT].rearrange("p (s k) -> p s k", s=2)]
        krgs = [att4.get(2, KEYS_ROW * ROPE), over[:, 0:2 * KEYS_ROW * ROPE].rearrange("p (s k) -> p s k", s=2)]
        assert 2 * KEYS_ROW * LAT <= TP * H and 2 * KEYS_ROW * ROPE <= 2 * T
        psm = att4.get(PAST + 16)
        psT = mix[:, 0:4, :].rearrange("p a b -> p (a b)")[:, 0:17 * P]
        qr0 = zT.rearrange("p a b -> p (a b)").rearrange("p (t h) -> p t h", h=H)
        moe = Area(0)
        wgu = moe.get(2, KD, 2 * F)
        wdn = moe.get(2, 2, D)
        xg = moe.get(3, D)
        xgT = moe.get(2, KD, P)
        eh = moe.get(2, F)
        hh = moe.get(2, F)
        hT = moe.get(2, 2, P)
        yt = moe.get(2, D)
        lnrow = moe.get(2, D)
        yg = over[:, 0:2 * TT * D].rearrange("p (a b) -> p a b", b=D)
        assert 2 * TT * D <= 2 * KD * 2 * F + 2 * 2 * D
        sc, sel, r1, r2, r3, r4 = (moe.get(TT, E) for _ in range(6))
        g4 = [moe.get(TT, 4) for _ in range(6)]
        g1 = [moe.get(TT) for _ in range(3)]
        gate = moe.get(2, TT)
        slotf = moe.get(2, TT)
        ov, ovi, ob = (moe.get(E) for _ in range(3))
        tcmp = moe.get(NOVER, E)
        tef = moe.get(NOVER + 1)
        slot = sb("slot", [P, 2, TT], I32)
        tokid = sb("tokid", [P, TT], I32)
        fetch = sb("fetch", [P, NTILE], I32)
        zero_ids = sb("zero_ids", [NTILE, P], I32)
        dyn = sb("dyn", [P, NOVER + 1], I32)
        bnst = sb("bnst", [P, TT, 2, 6])
        bnag = sb("bnag", [P, TT, 2])
        rstd = sb("rstd", [P, TT])
        shift = sb("shift", [P, TT])
        x_rows = nc.dram_tensor("x_rows", [T, D], F32, kind="Internal").ap()
        y_rows = nc.dram_tensor("y_rows", [NTILE * P, D], F32, kind="Internal").ap()
        slot_token = nc.dram_tensor("slot_token", [NTILE * P, 1], I32, kind="Internal").ap()

        def projection(j):
            name, part = CHUNKS[j]
            return dict(cq=cq, gv=gv, gr=gr, mv=mv, mo=mo)[name][:, part, :] if name not in ("ckv", "gq", "gk") \
                else dict(ckv=ckv, gq=gq, gk=gk)[name]

        def late_halves(c):
            n = 2 * (len(CHUNKS) - EARLY)
            two = n - (NCH + 1)
            first = 2 * c if c < two else two + c
            return [(x, EARLY + (first + x) // 2, (first + x) % 2) for x in range(2 if c < two else 1)]

        plan = []
        index = {}

        def nth(g):
            return sum(1 for c in plan[:g + 1] if c == plan[g])

        rel_sem = {"A": S("released_by_scalar"), "D": S("released_by_vector")}
        filled = S("bank_filled")

        def full(eng, key):
            eng.wait_ge(filled, index[key] + 1)

        def bank(key):
            return ps[:, index[key] % 8, :]

        def rel(ins, key, who):
            assert plan[index[key]] == who, key
            ins.then_inc(rel_sem[who], 1)

        barriers = {}

        def barrier(eng, name):
            barriers[name] = barriers.get(name, 0) + 1
            eng.drain().then_inc(S("stage_ended"), 1)
            eng.wait_ge(S("stage_ended"), 5 * barriers[name])

        def fetches(l, e):
            return l * len(range(e % 3, E, 3)) + e // 3 + 1

        wlast = {}

        def wseq(l, what, j):
            return l * (len(CHUNKS) + KD) + (j if what == "in" else len(CHUNKS) + j)

        block_ = ctx.enter_context(nc.Block())

        @block_.tensor
        def _(pe):
            mm = nc.tensor.matmul
            waited = {}

            def wait(name, v):
                pe.wait_ge(S(name), v)

            def released(g):
                c = plan[g]
                v = nth(g)
                if waited.get(c, 0) < v:
                    waited[c] = v
                    pe.wait_ge(rel_sem[c], v)

            def group(key, consumer):
                g = len(plan)
                plan.append(consumer)
                index[key] = g
                if g >= 8:
                    released(g - 8)
                return ps[:, g % 8, :]

            def drained(key):
                released(index[key])

            def done(ins):
                ins.then_inc(filled, 1)

            def tr(out, in_, n):
                return nc.tensor.transpose(out, in_, ident[0:n, 0:n])

            def layer_norm(n):
                for h in range(2):
                    b = group(("mean", n, h), "D")
                    for k in range(KD):
                        i = mm(b[:, 0:HALF], ones, zT[:, k, SH[h]], start=(k == 0), stop=(k == KD - 1))
                    done(i)
                for h in range(2):
                    wait("ln_squared", 2 * n + h + 1)
                    b = group(("var", n, h), "A")
                    for k in range(KD):
                        i = mm(b[:, 0:HALF], ones, xT[:, k, SH[h]], start=(k == 0), stop=(k == KD - 1))
                    done(i)

            wait("const_loaded", 16)
            wait("vec_loaded", 16 * (len(VEC) + 5))
            b = group("vec", "A")
            done(tr(b[:, 0:P], vecrows[:, :], P))

            def to_features(n):
                wait("rows_normed", n + 1)
                wait("odd_rows_normed", n + 1)
                for k in range(KD):
                    for x in range(2):
                        b = group(("xin", n, k, x), "DA"[k % 2])
                        for t in ((0, 1, 2, 3), (4,))[x]:
                            q = rows_of(t)
                            i = tr(b[:, (t % 4) * P:(t % 4) * P + q], tok(t, q, slice(k * P, (k + 1) * P)), q)
                        done(i)

            to_features(0)

            for l in range(DEPTH):
                barrier(pe, "pe")
                def project(j, h):
                    u = wseq(l, "in", j)
                    wait(f"wslot{u % NSLOT}", 16 * (u // NSLOT + 1))
                    b = group(("in", l, j, h), "DA"[h] if CHUNKS[j][0] != "mu" else "A")
                    for k in range(KD):
                        i = mm(b[:, 0:HALF], wslot[:, u % NSLOT, k, :], xT[:, k, SH[h]], start=(k == 0), stop=(k == KD - 1))
                    done(i)
                    wlast[u] = ("in", l, j, 1)

                for j in range(2):
                    project(j, 0)
                    project(j, 1)
                wait("wsmall_loaded", 16 * 5 * (l + 1))
                wait("rec_zeroed", l + 1)
                for h in range(2):
                    b = group(("small", l, h), "A")
                    for k in range(KD):
                        i = mm(b[0:SMALL, 0:HALF], wsm[:, k, :], xT[:, k, SH[h]], start=(k == 0), stop=(k == KD - 1))
                    done(i)
                wait("rec_loaded", 16 * 13 * (l + 1))
                drained(("small", l, 1))
                for h in range(2):
                    b = group(("ga", l, h), "D")
                    done(mm(b[:, 0:HALF], wa[64:64 + GR, :], small[64:64 + GR, SH[h]], start=True, stop=True))
                for j in range(2, EARLY):
                    project(j, 0)
                    project(j, 1)
                wait("conv_done", l + 1)
                wait("wqk_loaded", 16 * 8 * (l + 1))
                for qk in range(2):
                    for j in range(2):
                        for h in range(2):
                            b = group(("mqk", l, qk, j, h), "A")
                            done(mm(b[:, 0:HALF], wqk[:, qk, j, :], uc[:, j, SH[h]], start=True, stop=True))
                wait("rows_done", l + 1)
                for n, row in enumerate((rowwp, rowe)):
                    for j in range(2):
                        for h in range(2):
                            b = group(("spread", l, n, j, h), "A")
                            done(mm(b[:, 0:HALF], cst("pairsel", 4)[:, j * P:(j + 1) * P], row[:, SH[h]], start=True, stop=True))
                drained(("in", l, EARLY - 1, 0))
                drained(("in", l, EARLY - 1, 1))
                wait("gla_inputs", l + 1)
                wait("mqw_done", l + 1)
                wait("states_ready", l + 1)
                for c in range(NCH + 1):
                    smp = c == NCH
                    n = NS if smp else C
                    cs = slice(c * C, c * C + n)
                    w = 4 * n
                    b = group(("gtok", l, c), "A")
                    for q, src in enumerate((gv[:, 0, cs], gv[:, 1, cs], kt[:, cs])):
                        i = tr(b[0:n, q * P:(q + 1) * P], src, P)
                    done(i)
                    b = group(("vtok", l, c), "A")
                    for q in range(2):
                        i = tr(b[0:n, q * P:(q + 1) * P], mv[:, q, cs], P)
                    done(i)
                    b = group(("ga_s", l, c), "D")
                    done(mm(b[0:n, 0:w], kt[:, cs], qm[:, :, cs], start=True, stop=True))
                    b = group(("logw", l, c), "A")
                    mm(b[0:n, 0:w], rowt[:, cs], cst("rowsel", 4).rearrange("p (h t) -> p h t", h=4)[:, :, 0:n], start=True, stop=False)
                    mm(b[0:n, 0:w], ones[0:4, 0:n], negM[:, :, cs], start=False, stop=False)
                    done(mm(b[0:n, 0:w], ident[0:n, 0:n], cst("trineg_s" if smp else "trineg", n), start=False, stop=True))
                    b = group(("qk", l, c), "D")
                    for j in range(2):
                        i = mm(b[0:n, 2 * j * n:2 * (j + 1) * n], mk[:, j, cs], mqm[:, j, :, cs], start=True, stop=True)
                    done(i)
                    b = group(("ktok", l, c), "D")
                    for q in range(2):
                        i = tr(b[0:n, q * P:(q + 1) * P], mk[:, q, cs], P)
                    done(i)
                    late = late_halves(c)
                    project(*late[0][1:])
                    drained(("gtok", l, c))
                    drained(("ga_s", l, c))
                    if c and not smp:
                        wait("gla_state", (NCH + 1) * l + c)
                    b = group(("go", l, c), "A")
                    for hd in range(GH):
                        r = slice(64 * (hd % 2), 64 * (hd % 2) + 64)
                        o = b[r, (hd // 2) * n:(hd // 2) * n + n]
                        mm(o, gtok[0:n, hd * GV:(hd + 1) * GV], am[0:n, hd * n:(hd + 1) * n], start=True, stop=False)
                        if smp:
                            for s in range(NSEQ):
                                i = mm(o[:, s * TS:(s + 1) * TS], sgs[:, s, :], qm[:, hd, TP + s * TS:TP + (s + 1) * TS],
                                       start=False, stop=(s == NSEQ - 1))
                        else:
                            i = mm(o, sg[:, :], qm[:, hd, cs], start=False, stop=True)
                    done(i)
                    b = group(("gs", l, c), "D")
                    if smp:
                        for hd in range(GH):
                            wait("gla_vmask", GH * l + hd + 1)
                            i = mm(b[32 * hd:32 * hd + 32, 0:512], gtok[0:n, 2 * P + GK * hd:2 * P + GK * hd + GK], vm[0:n, hd % 2, :],
                                   start=True, stop=True, tile_position=(0, 32 * hd))
                            if hd < GH - 1:
                                i.then_inc(S("gla_vm_read"), 1)
                    else:
                        for hd in range(GH):
                            i = mm(b[32 * hd:32 * hd + 32, 0:GV], gtok[0:n, 2 * P + GK * hd:2 * P + GK * hd + GK],
                                   gtok[0:n, hd * GV:(hd + 1) * GV], start=True, stop=True, tile_position=(0, 32 * hd))
                    done(i)
                    if len(late) > 1:
                        project(*late[1][1:])
                    drained(("vtok", l, c))
                    drained(("qk", l, c))
                    if c and not smp:
                        wait("ml_state", (NCH + 1) * l + c)
                    b = group(("nd", l, c), "A")
                    for hd in range(MH):
                        r = slice(64 * (hd % 2), 64 * (hd % 2) + 64)
                        j = hd // 2
                        for x in range(2):
                            o = b[r, (2 * x + j) * n:(2 * x + j + 1) * n]
                            mm(o, vaug[0:n, hd, x * DH:(x + 1) * DH], qkw[0:n, hd * n:(hd + 1) * n], start=True, stop=False)
                            if smp:
                                for s in range(NSEQ):
                                    i = mm(o[:, s * TS:(s + 1) * TS], cns[:, j, s, x * DH:(x + 1) * DH],
                                           mqw[:, j, hd % 2, TP + s * TS:TP + (s + 1) * TS], start=False, stop=(s == NSEQ - 1))
                            else:
                                i = mm(o, cn[:, j, x * DH:(x + 1) * DH], mqw[:, j, hd % 2, cs], start=False, stop=True)
                    done(i)
                    drained(("ktok", l, c))
                    if smp:
                        for j in range(2):
                            b = group(("mu_c", l, j), "D")
                            for a in range(2):
                                hd = 2 * j + a
                                wait("ml_vmask", MH * l + hd + 1)
                                i = mm(b[64 * a:64 * a + 64, 0:512], kws[0:n, hd, :], vm[0:n, hd % 2, :], start=True, stop=True)
                                if a == 0:
                                    i.then_inc(S("ml_vm_read"), 1)
                            done(i)
                            b = group(("mu_n", l, j), "D")
                            for a in range(2):
                                i = mm(b[64 * a:64 * a + 64, 0:512], kws[0:n, 2 * j + a, :],
                                       cst("seqmask", n).unsqueeze(2).to_broadcast([n, NSEQ, DH]), start=True, stop=True)
                            done(i)
                    else:
                        b = group(("mu", l, c), "D")
                        for hd in range(MH):
                            i = mm(b[64 * (hd % 2):64 * (hd % 2) + 64, (hd // 2) * P:(hd // 2) * P + P], kws[0:n, hd, :], vaug[0:n, hd, :],
                                   start=True, stop=True)
                        done(i)
                for j in range(2):
                    for h in range(2):
                        wait("gla_sq", l + 1)
                        b = group(("gn", l, j, h), "A")
                        done(mm(b[:, 0:HALF], block, qm[:, j, SH[h]], start=True, stop=True))
                wait("ml_h", l + 1)
                for j in range(2):
                    for h in range(2):
                        b = group(("mm_", l, j, h), "D")
                        done(mm(b[:, 0:HALF], block, nd[:, 0, j, SH[h]], start=True, stop=True))
                wait("latents_squared", l + 1)
                for h in range(2):
                    b = group(("cqn", l, h), "A")
                    for k in range(2):
                        i = mm(b[:, 0:HALF], ones, cq_sq[:, k, SH[h]], start=(k == 0), stop=(k == 1))
                    done(i)
                for h in range(2):
                    b = group(("ckn", l, h), "A")
                    done(mm(b[:, 0:HALF], ones, ckv_sq[:, SH[h]], start=True, stop=True))
                wait("ml_hsq", l + 1)
                for j in range(2):
                    for h in range(2):
                        b = group(("mvv", l, j, h), "A")
                        done(mm(b[:, 0:HALF], block, nd[:, 1, j, SH[h]], start=True, stop=True))
                barrier(pe, "pe")

                wait("att_loaded", 16 * 10 * (l + 1))
                for j in range(4):
                    b = group(("wukT", l, j), "A")
                    done(tr(b[:, 0:P], wukv[:, j * P:(j + 1) * P], P))
                for m in range(8):
                    for h in range(2):
                        b = group(("q", l, m, h), "A" if m < 6 else "D")
                        for k in range(2):
                            i = mm(b[:, 0:HALF], wuq[:, k, m * P:(m + 1) * P], cq[:, k, SH[h]], start=(k == 0), stop=(k == 1))
                        done(i)
                wait("key_rotated", l + 1)
                for t in range(9):
                    n = P if t < 4 else QT
                    cs = slice(t * P, t * P + n) if t < 5 else slice(TP + (t - 5) * QT, TP + (t - 4) * QT)
                    b = group(("ctok", l, t), "A")
                    tr(b[0:n, 0:LAT], ckv[:, cs], P)
                    done(tr(b[0:n, LAT:LAT + ROPE], kro[0:ROPE, cs], ROPE))
                for hd in range(H):
                    r = slice(64 * (hd % 2), 64 * (hd % 2) + 64)
                    if hd == 0:
                        drained(("q", l, 5, 1))
                        drained(("wukT", l, 3))
                    for h in range(2):
                        b = group(("qlat", l, hd, h), "AD"[hd // 4])
                        done(mm(b[:, 0:HALF], wukT[r, hd // 2, :], qn[r, hd // 2, SH[h]], start=True, stop=True))
                drained(("qlat", l, H // 2 - 1, 1))
                drained(("qlat", l, H - 1, 1))
                drained(("ctok", l, 8))
                barrier(pe, "pe")

                for step in range(NQ + 3):
                    if step < NQ:
                        i_ = step
                        W = QT * (i_ + 1)
                        cs = slice(QT * i_, W)
                        ql = qlat[:, cs, :].rearrange("p t h -> p (t h)")
                        qr = qr0[0:ROPE, cs, :].rearrange("p t h -> p (t h)")
                        for x, (a, z) in enumerate(((0, min(W, 512)), (512, W))):
                            if z <= a:
                                continue
                            b = group(("s", l, i_, x), "A")
                            o = b[:, 0:z - a]
                            mm(o, ql, ckv[:, a:z], start=True, stop=False)
                            last = z == W
                            i = mm(o, qr, kro[0:ROPE, a:z], start=False, stop=not last)
                            if last:
                                i = mm(b[:, z - a - QT:z - a], ident, cst("mask_q"), start=False, stop=True)
                            done(i)
                    if 2 <= step <= NQ + 1:
                        i_ = step - 2
                        W = QT * (i_ + 1)
                        nb = -(-W // P)
                        wait("pq_normed", NQ * l + i_ + 1)
                        for x in range(2):
                            blocks = range(4 * x, min(nb, 4 * x + 4))
                            if not len(blocks):
                                continue
                            b = group(("pt", l, i_, x), "DA"[i_ % 2])
                            for kb in blocks:
                                wk = min(P, W - kb * P)
                                i = tr(b[0:wk, (kb % 4) * P:(kb % 4) * P + P], pq[:, i_ % NPB, kb * P:kb * P + wk], P)
                            done(i)
                    if step >= 3:
                        i_ = step - 3
                        W = QT * (i_ + 1)
                        nb = -(-W // P)
                        drained(("pt", l, i_, (nb - 1) // 4))
                        b = group(("o", l, i_), "D")
                        for kb in range(nb):
                            wk = min(P, W - kb * P)
                            i = mm(b[:, 0:P], ctok[0:wk, kb, 0:LAT], pT[0:wk, i_ % NPB, kb * P:(kb + 1) * P],
                                   start=(kb == 0), stop=(kb == nb - 1))
                        done(i)
                barrier(pe, "pe")

                def keys_turned(p_):
                    for s in range(2):
                        wait(f"pages{s}_{p_ % 2}", 32 * (l * NSEQ // 4 + p_ // 2 + 1))
                        kg, krg = kgs[p_ % 2], krgs[p_ % 2]
                        for q in range(4):
                            b = group(("kT", l, p_, s, q), "DA"[q % 2])
                            for k in range(4):
                                j = 4 * q + k
                                i = tr(b[:, k * P:(k + 1) * P], kg[:, s, j * LAT:(j + 1) * LAT], P)
                            done(i)
                        b = group(("krT", l, p_, s), "DA"[s])
                        for q in range(4):
                            i = tr(b[:, q * P:(q + 1) * P], krg[:, s, q * P:(q + 1) * P], P)
                        done(i)

                def scores_of(p_):
                    cols = [slice(TP + (2 * p_ + s) * TS, TP + (2 * p_ + s + 1) * TS) for s in range(2)]
                    for s in range(2):
                        drained(("kT", l, p_, s, 3))
                        drained(("kT", l, p_, s, 2))
                        drained(("krT", l, p_, s))
                    for q in range(4):
                        b = group(("ss", l, p_, q), "A")
                        for s in range(2):
                            o = b[64 * s:64 * s + 64, :]
                            mm(o, qlat[:, cols[s], :].rearrange("p t h -> p (t h)"), kT[:, s, q * 512:(q + 1) * 512], start=True, stop=False)
                            for jj in range(4):
                                c0 = (2 * p_ + s) * TS
                                i = mm(o[:, jj * P:(jj + 1) * P], qrM[:, jj, c0:c0 + TS, :].rearrange("p t h -> p (t h)"),
                                       krT[:, s, q * P:(q + 1) * P], start=False, stop=(jj == 3))
                        done(i)
                    b = group(("sn", l, p_), "A")
                    new = slice(TP + p_ * QT, TP + (p_ + 1) * QT)
                    for s in range(2):
                        o = b[64 * s:64 * s + 64, 0:QT]
                        mm(o, qlat[:, cols[s], :].rearrange("p t h -> p (t h)"), ckv[:, new], start=True, stop=False)
                        mm(o, qr0[0:ROPE, cols[s], :].rearrange("p t h -> p (t h)"), kro[0:ROPE, new], start=False, stop=False)
                    done(mm(b[:, 0:QT], ident, cst("mask_n"), start=False, stop=True))

                def probs_turned(p_):
                    wait("ps_normed", l * (NSEQ // 2) + p_ + 1)
                    for q in range(4):
                        b = group(("psT", l, p_, q), "DA"[q % 2])
                        for k in range(4):
                            i = tr(b[:, k * P:(k + 1) * P], psm[:, (4 * q + k) * P:(4 * q + k + 1) * P], P)
                        done(i)
                    b = group(("psT", l, p_, 4), "D")
                    done(tr(b[0:QT, 0:P], psm[:, PAST:PAST + QT], P))

                def latents_of(p_):
                    drained(("psT", l, p_, 4))
                    drained(("psT", l, p_, 3))
                    kg = kgs[p_ % 2]
                    b = group(("so", l, p_), "D")
                    for s in range(2):
                        o = b[:, 64 * s:64 * s + 64]
                        for j in range(16):
                            mm(o, kg[:, s, j * LAT:(j + 1) * LAT], psT[:, j * P + 64 * s:j * P + 64 * s + 64], start=(j == 0), stop=False)
                        i = mm(o, ctok[0:QT, 5 + p_, 0:LAT], psT[0:QT, 16 * P + 64 * s:16 * P + 64 * s + 64], start=False, stop=True)
                    done(i)

                keys_turned(0)
                scores_of(0)
                for p_ in range(NSEQ // 2):
                    if p_ + 1 < NSEQ // 2:
                        keys_turned(p_ + 1)
                    probs_turned(p_)
                    latents_of(p_)
                    if p_ + 1 < NSEQ // 2:
                        scores_of(p_ + 1)
                drained(("so", l, NSEQ // 2 - 1))
                for j in range(4):
                    for h in range(2):
                        b = group(("omla", l, j, h), "DA"[h])
                        for a in range(2):
                            hd = 2 * j + a
                            i = mm(b[64 * a:64 * a + 64, 0:HALF], wukv[:, 512 + hd * MV:512 + (hd + 1) * MV], qlat[:, SH[h], hd], start=True, stop=True)
                        done(i)
                drained(("omla", l, 3, 0))
                drained(("omla", l, 3, 1))
                barrier(pe, "pe")
                for m in range(KD):
                    u = wseq(l, "out", m)
                    wait(f"wslot{u % NSLOT}", 16 * (u // NSLOT + 1))
                    for h in range(2):
                        b = group(("out", l, m, h), "D")
                        for k in range(KD):
                            i = mm(b[:, 0:HALF], wslot[:, u % NSLOT, k, :], mix[:, k, SH[h]], start=(k == 0), stop=(k == KD - 1))
                        done(i)
                    wlast[u] = ("out", l, m, 1)
                drained(("out", l, KD - 1, 1))
                layer_norm(l)

                wait("ln_done", l + 1)
                b = group(("route", l), "A")
                for t in range(TT):
                    r = P if t < TT - 1 else LAST
                    for k in range(KD):
                        i = mm(b[0:r, t * E:(t + 1) * E], xT[:, k, t * P:t * P + r], routerw[:, k, :], start=(k == 0), stop=(k == KD - 1))
                done(i)
                for t in range(TT):
                    q = rows_of(t)
                    for x in range(2):
                        b = group(("xt", l, t, x), "DA"[x])
                        for k in range(4):
                            i = tr(b[0:q, k * P:(k + 1) * P], xT[:, 4 * x + k, t * P:t * P + q], P)
                        done(i)
                wait("onehots", l + 1)
                b = group(("rank", l), "D")
                for t in range(TT):
                    o = b[:, t * E:(t + 1) * E]
                    i = mm(o, cst("before"), r4[:, t, :], start=True, stop=(t == 0))
                    for u in range(t):
                        i = mm(o, ones, r4[:, u, :], start=False, stop=(u == t - 1))
                for t in range(TT):
                    i = mm(b[:, TT * E:(TT + 1) * E], ones, r4[:, t, :], start=(t == 0), stop=(t == TT - 1))
                done(i)

                def turn(e):
                    wait(f"x_fetched{e % 3}", 16 * fetches(l, e))
                    for x in range(2):
                        b = group(("xg", l, e, x), "A")
                        for k in range(4):
                            i = tr(b[:, k * P:(k + 1) * P], xg[:, e % 3, (4 * x + k) * P:(4 * x + k + 1) * P], P)
                        done(i)

                def up(e):
                    wait(f"wgu{e % 2}", 32 * ((l * E + e) // 2 + 1))
                    for x in range(2):
                        drained(("xg", l, e, x))
                    b = group(("up", l, e), "D")
                    for k in range(KD):
                        i = mm(b, xgT[:, e % 2, k, :], wgu[:, e % 2, k, :], start=(k == 0), stop=(k == KD - 1))
                    done(i)

                def turn_h(e):
                    wait("h_done", l * E + e + 1)
                    b = group(("hT", l, e), "D")
                    for f in range(2):
                        i = tr(b[:, f * P:(f + 1) * P], hh[:, e % 2, f * P:(f + 1) * P], P)
                    done(i)

                def down(e):
                    wait(f"wdn{e % 2}", 16 * ((l * E + e) // 2 + 1))
                    drained(("hT", l, e))
                    for x in range(2):
                        b = group(("dn", l, e, x), "A")
                        for f in range(2):
                            i = mm(b, hT[:, e % 2, f, :], wdn[:, e % 2, f, x * 512:(x + 1) * 512], start=(f == 0), stop=(f == 1))
                        done(i)

                turn(0)
                for e in range(E + 1):
                    if e >= 1:
                        turn_h(e - 1)
                    if e < E:
                        up(e)
                    if e + 1 < E:
                        turn(e + 1)
                    if e >= 1:
                        down(e - 1)
                barrier(pe, "pe")

                def overflow(k, count):
                    with pe.If(count > k):
                        pe.wait_ge(S(f"over_fetched_{l}"), 16 * (k + 1))
                        for c in range(KD):
                            i = tr(ps[:, c // 4, (c % 4) * P:(c % 4 + 1) * P], xg[:, 1, c * P:(c + 1) * P], P)
                        i.then_inc(S(f"over_x_turned_{l}"), 1)
                        pe.wait_ge(S(f"over_x_copied_{l}"), k + 1)
                        pe.wait_ge(S(f"over_weights_{l}"), 48 * (k + 1))
                        for c in range(KD):
                            i = mm(ps[:, 2, :], xgT[:, 0, c, :], wgu[:, 0, c, :], start=(c == 0), stop=(c == KD - 1))
                        i.then_inc(S(f"over_up_{l}"), 1)
                        pe.wait_ge(S(f"over_h_{l}"), k + 1)
                        for f in range(2):
                            i = tr(ps[:, 3, f * P:(f + 1) * P], hh[:, 0, f * P:(f + 1) * P], P)
                        i.then_inc(S(f"over_h_turned_{l}"), 1)
                        pe.wait_ge(S(f"over_h_copied_{l}"), k + 1)
                        for x in range(2):
                            for f in range(2):
                                i = mm(ps[:, 4 + x, :], hT[:, 0, f, :], wdn[:, 0, f, x * 512:(x + 1) * 512], start=(f == 0), stop=(f == 1))
                        i.then_inc(S(f"over_down_{l}"), 1)
                        if k + 1 < NOVER:
                            overflow(k + 1, count)

                overflow(0, pe.value_load(dyn[0:1, NOVER:NOVER + 1], min_val=0, max_val=NOVER))
                barrier(pe, "pe")
                if l + 1 < DEPTH:
                    to_features(l + 1)
            barrier(pe, "pe")

        def drained_by_other(eng, key):
            eng.wait_ge(rel_sem[plan[index[key]]], nth(index[key]))

        def prompt_pT(eng, l, i_, op, who):
            W = QT * (i_ + 1)
            nb = -(-W // P)
            if i_ >= NPB:
                eng.wait_ge(filled, index[("o", l, i_ - NPB)] + 1)
            for x in range(2):
                n = min(nb, 4 * x + 4) - 4 * x
                if n <= 0:
                    continue
                key = ("pt", l, i_, x)
                full(eng, key)
                wl = min(P, W - (4 * x + n - 1) * P)
                d = pT[:, i_ % NPB, :]
                if wl == P or n == 1:
                    rows = P if wl == P else wl
                    i = op(d[0:rows, 4 * x * P:(4 * x + n) * P], bank(key)[0:rows, 0:n * P])
                else:
                    op(d[:, 4 * x * P:(4 * x + n - 1) * P], bank(key)[:, 0:(n - 1) * P])
                    i = op(d[0:wl, (4 * x + n - 1) * P:(4 * x + n) * P], bank(key)[0:wl, (n - 1) * P:n * P])
                rel(i, key, who)

        @block_.scalar
        def _(act):
            f_ = nc.scalar.activation

            def sig(ins, name, k=1):
                ins.then_inc(S(name), k)

            def log_of(key, out, scale, eps):
                full(act, key)
                rel(f_(out, bank(key)[:, 0:HALF], ACT.Ln, bias=eps, scale=scale), key, "A")

            def copy(key, dst, src, scale=None):
                full(act, key)
                if scale is None:
                    rel(f_(dst, src, ACT.Copy), key, "A")
                else:
                    rel(f_(dst, src, ACT.Copy, scale=scale), key, "A")

            def layer_norm(n):
                for h in range(2):
                    act.wait_ge(S("ln_centred"), 2 * n + h + 1)
                    sig(f_(xT[:, :, SH[h]], zT[:, :, SH[h]], ACT.Square), "ln_squared")
                for h in range(2):
                    log_of(("var", n, h), lnr[:, SH[h]], 1.0 / D, cst("epsln"))
                act.drain()
                sig(f_(lnr, lnr, ACT.Exp, scale=-0.5), "ln_root")
                for k in range(KD):
                    act.wait_ge(S("ln_scaled"), KD * n + k + 1)
                    f_(xT[:, k, :], xT[:, k, :], ACT.Identity, bias=col("ln1_b", n, k))
                act.drain().then_inc(S("ln_done"), 1)

            copy("vec", vec[:, :], bank("vec")[:, 0:P])
            act.drain().then_inc(S("vec_ready"), 1)

            def root_of_rows(n, rows=True):
                act.wait_ge(S("rows_var"), n + 1)
                f_(rstd, bnag[:, :, 1], ACT.Ln, bias=cst("epsln"))
                act.drain()
                sig(f_(rstd, rstd, ACT.Exp, scale=-0.5), "rows_root")
                if not rows:
                    return
                act.wait_ge(S("rows_shift"), n + 1)
                for t in range(1, TT, 2):
                    q = rows_of(t)
                    f_(tok(t, q), tok(t, q), ACT.Identity, bias=shift[0:q, t:t + 1], scale=rstd[0:q, t:t + 1])
                act.drain().then_inc(S("odd_rows_normed"), 1)

            def to_features(n, g, b, l):
                for k in range(1, KD, 2):
                    for x in range(2):
                        key = ("xin", n, k, x)
                        full(act, key)
                        q = slice(0, 512) if x == 0 else slice(512, T)
                        rel(f_(xT[:, k, q], bank(key)[:, 0:q.stop - q.start], ACT.Identity, bias=col(b, l, k), scale=col(g, l, k)), key, "A")

            root_of_rows(0)
            to_features(0, "ln_in_g", "ln_in_b", 0)

            for l in range(DEPTH):
                barrier(act, "act")
                for part in range(2):
                    copy(("in", l, part, 0), mup[:, part, CONV - 1:CONV - 1 + HALF], bank(("in", l, part, 0))[:, 0:HALF])
                    b = bank(("in", l, part, 1))
                    full(act, ("in", l, part, 1))
                    f_(mup[:, part, CONV - 1 + HALF:CONV - 1 + TP], b[:, 0:TP - HALF], ACT.Copy)
                    rel(f_(mus[:, part, :, CONV - 1:], b[:, TP - HALF:HALF].rearrange("p (s t) -> p s t", s=NSEQ), ACT.Copy),
                        ("in", l, part, 1), "A")
                act.drain().then_inc(S("mu_ready"), 1)
                for h in range(2):
                    copy(("small", l, h), small[0:SMALL, SH[h]], bank(("small", l, h))[0:SMALL, 0:HALF])
                act.drain().then_inc(S("small_ready"), 1)

                def projected(j):
                    copy(("in", l, j, 1), projection(j)[:, SH[1]], bank(("in", l, j, 1))[:, 0:HALF])

                act.wait_ge(S("fgate_abs"), l + 1)
                f_(rowe, rowe, ACT.Exp, scale=-1.0)
                act.drain()
                sig(f_(rowe, rowe, ACT.Ln, bias=cst("one", 4)), "fgate_ln")
                act.wait_ge(S("ga_abs"), l + 1)
                f_(tmp1, tmp1, ACT.Exp, scale=-1.0)
                act.drain()
                sig(f_(tmp1, tmp1, ACT.Ln, bias=cst("one")), "ga_ln")
                projected(2)
                projected(3)
                act.drain().then_inc(S("in_half_ready"), 1)
                act.wait_ge(S("conv_sum"), l + 1)
                sig(f_(wpb, uc, ACT.Exp, scale=-1.0), "conv_exp")
                projected(4)
                act.wait_ge(S("rows_logs"), l + 1)
                f_(rowwp, rowwp, ACT.Exp)
                sig(f_(rowe, rowm, ACT.Exp, scale=-1.0), "rows_exp")
                projected(5)
                act.wait_ge(S("ga_cum"), l + 1)
                f_(geb, tmp2, ACT.Exp, scale=1.0 / TAU)
                sig(f_(gb, tmp2, ACT.Exp, scale=-1.0 / TAU), "ga_decay")
                projected(6)
                projected(7)
                for qk in range(2):
                    for j in range(2):
                        for h in range(2):
                            key = ("mqk", l, qk, j, h)
                            b = bank(key)
                            if qk:
                                copy(key, mk[:, j, SH[h]], b[:, 0:HALF], DH ** -0.5)
                            else:
                                full(act, key)
                                f_(mqm[0:64, j, 0, SH[h]], b[0:64, 0:HALF], ACT.Copy)
                                rel(f_(mqm[64:128, j, 1, SH[h]], b[64:128, 0:HALF], ACT.Copy), key, "A")
                for n, dst in enumerate((wpb, enmb)):
                    for j in range(2):
                        for h in range(2):
                            copy(("spread", l, n, j, h), dst[:, j, SH[h]], bank(("spread", l, n, j, h))[:, 0:HALF])
                act.drain().then_inc(S("spread_ready"), 1)
                for c in range(NCH + 1):
                    smp = c == NCH
                    n = NS if smp else C
                    cs = slice(c * C, c * C + n)
                    copy(("gtok", l, c), gtok[0:n, :], bank(("gtok", l, c))[0:n, 0:3 * P])
                    copy(("vtok", l, c), vaug[0:n, :, 0:DH], bank(("vtok", l, c))[0:n, 0:256].rearrange("p (h v) -> p h v", h=MH))
                    key = ("logw", l, c)
                    full(act, key)
                    if c:
                        act.wait_ge(S("kws_done"), (NCH + 1) * l + c)
                    i = f_(wd_[0:n, 0:4 * n], bank(key)[0:n, 0:4 * n], ACT.Exp)
                    rel(i, key, "A")
                    act.drain().then_inc(S("w_ready"), 1)
                    late = late_halves(c)
                    if late[0][2] == 1:
                        projected(late[0][1])
                    copy(("go", l, c), og[:, :, cs], bank(("go", l, c))[:, 0:2 * n].rearrange("p (j t) -> p j t", j=2))
                    if len(late) > 1:
                        projected(late[1][1])
                    copy(("nd", l, c), nd[:, :, :, cs], bank(("nd", l, c))[:, 0:4 * n].rearrange("p (x j t) -> p x j t", x=2, j=2))
                    if c == 3:
                        f_(mix[:, 4:6, :], gr, ACT.Exp, scale=-1.0).then_inc(S("gr_exp"), 1)
                    if c == 5:
                        f_(mo, mo, ACT.Exp, scale=-1.0).then_inc(S("mo_exp"), 1)
                act.drain().then_inc(S("chunks_out"), 1)
                act.wait_ge(filled, index[("nd", l, NCH)] + 1)
                f_(qm[:, 0:2, :], og, ACT.Square).then_inc(S("gla_sq"), 1)
                act.wait_ge(S("ml_state"), (NCH + 1) * (l + 1))
                f_(cq_sq, cq, ACT.Square)
                sig(f_(ckv_sq, ckv, ACT.Square), "latents_squared")
                act.wait_ge(S("ml_centred"), l + 1)
                sig(f_(nd[:, 1, :, :], nd[:, 0, :, :], ACT.Square), "ml_hsq")
                for j in range(2):
                    for h in range(2):
                        log_of(("gn", l, j, h), gv[:, j, SH[h]], 1.0 / GV, cst("epsrms"))
                for h in range(2):
                    log_of(("cqn", l, h), lnr[:, SH[h]], 1.0 / 256, cst("epsrms"))
                for h in range(2):
                    log_of(("ckn", l, h), ckv_root[:, SH[h]], 1.0 / LAT, cst("epsrms"))
                for j in range(2):
                    for h in range(2):
                        log_of(("mvv", l, j, h), mk[:, j, SH[h]], 1.0 / DH, cst("epsln"))
                act.drain()
                sig(f_(gv, gv, ACT.Exp, scale=-0.5), "gla_root")
                f_(lnr, lnr, ACT.Exp, scale=-0.5)
                sig(f_(ckv_root, ckv_root, ACT.Exp, scale=-0.5), "latents_root")
                sig(f_(mk, mk, ACT.Exp, scale=-0.5), "ml_root")
                barrier(act, "act")

                for j in range(4):
                    copy(("wukT", l, j), wukT[:, j, :], bank(("wukT", l, j))[:, 0:P])
                for m in range(6):
                    for h in range(2):
                        dst = qn[:, m, SH[h]] if m < 4 else qra[:, m - 4, SH[h]]
                        copy(("q", l, m, h), dst, bank(("q", l, m, h))[:, 0:HALF])
                act.drain().then_inc(S("qra_ready"), 1)
                for t in range(9):
                    n = P if t < 4 else QT
                    copy(("ctok", l, t), ctok[0:n, t, :], bank(("ctok", l, t))[0:n, 0:LAT + ROPE])
                act.drain().then_inc(S("ctok_ready"), 1)
                for hd in range(H // 2):
                    for h in range(2):
                        copy(("qlat", l, hd, h), qlat[:, SH[h], hd], bank(("qlat", l, hd, h))[:, 0:HALF])
                barrier(act, "act")

                for step in range(NQ + 2):
                    if step < NQ:
                        i_ = step
                        W = QT * (i_ + 1)
                        act.wait_ge(S("pq_max"), NQ * l + i_ + 1)
                        if i_ >= NPB:
                            W0 = QT * (i_ - NPB + 1)
                            act.wait_ge(filled, index[("pt", l, i_ - NPB, (-(-W0 // P) - 1) // 4)] + 1)
                        for x, (a, z) in enumerate(((0, min(W, 512)), (512, W))):
                            if z <= a:
                                continue
                            key = ("s", l, i_, x)
                            full(act, key)
                            i = f_(pq[:, i_ % NPB, a:z], bank(key)[:, 0:z - a], ACT.Exp, bias=nmq[:, i_ % NPB:i_ % NPB + 1],
                                   scale=SCALE, accum_out=smq[:, i_ % NPB, x:x + 1])
                            rel(i, key, "A")
                        act.drain().then_inc(S("pq_exp"), 1)
                    if step >= 2 and step % 2 == 1:
                        i_ = step - 2
                        prompt_pT(act, l, i_, lambda d, s_: f_(d, s_, ACT.Copy), "A")
                barrier(act, "act")

                def keys_turned(p_):
                    for s in range(2):
                        for q in (1, 3):
                            copy(("kT", l, p_, s, q), kT[:, s, q * 512:(q + 1) * 512], bank(("kT", l, p_, s, q)))
                    copy(("krT", l, p_, 1), krT[:, 1, :], bank(("krT", l, p_, 1)))

                def exps_of(p_):
                    act.wait_ge(S("ps_max"), l * (NSEQ // 2) + p_ + 1)
                    for q in range(5):
                        key = ("ss", l, p_, q) if q < 4 else ("sn", l, p_)
                        w = 512 if q < 4 else QT
                        full(act, key)
                        i = f_(psm[:, q * 512:q * 512 + w], bank(key)[:, 0:w], ACT.Exp, bias=nmx[:, 0:1], scale=SCALE,
                               accum_out=sums[:, q:q + 1])
                        rel(i, key, "A")
                    act.drain().then_inc(S("ps_exp"), 1)

                keys_turned(0)
                exps_of(0)
                for p_ in range(NSEQ // 2):
                    if p_ + 1 < NSEQ // 2:
                        keys_turned(p_ + 1)
                    for q in (1, 3):
                        copy(("psT", l, p_, q), psT[:, q * 512:(q + 1) * 512], bank(("psT", l, p_, q)))
                    if p_ + 1 < NSEQ // 2:
                        exps_of(p_ + 1)
                for j in range(4):
                    copy(("omla", l, j, 1), mix[:, j, SH[1]], bank(("omla", l, j, 1))[:, 0:HALF])
                barrier(act, "act")
                layer_norm(l)

                act.wait_ge(S("logits_zeroed"), l + 1)
                key = ("route", l)
                full(act, key)
                b = bank(key).rearrange("p (t e) -> p t e", e=E)
                f_(sc[:, 0:4, :], b[:, 0:4, :], ACT.Exp, scale=-1.0)
                rel(f_(sc[0:LAST, 4, :], b[0:LAST, 4, :], ACT.Exp, scale=-1.0), key, "A")
                act.drain().then_inc(S("logits_exp"), 1)
                for t in range(TT):
                    q = rows_of(t)
                    copy(("xt", l, t, 1), tok(t, q, slice(512, D)), bank(("xt", l, t, 1))[0:q, :])
                act.drain().then_inc(S("xt_half"), 1)

                def x_in(e):
                    for x in range(2):
                        copy(("xg", l, e, x), xgT[:, e % 2, 4 * x:4 * x + 4, :], bank(("xg", l, e, x)).rearrange("p (k n) -> p k n", k=4))

                def gate_exp(e):
                    full(act, ("up", l, e))
                    if l * E + e >= 2:
                        act.wait_ge(S("h_done"), l * E + e - 1)
                    sig(f_(eh[:, e % 2, :], bank(("up", l, e))[:, 0:F], ACT.Exp, scale=-1.0), "hg_exp")

                def y_out(e):
                    n = l * E + e
                    if n >= 2:
                        act.wait_ge(S(f"y_written{e % 2}"), 16 * (n // 2))
                    for x in range(2):
                        copy(("dn", l, e, x), yt[:, e % 2, x * 512:(x + 1) * 512], bank(("dn", l, e, x)))
                    act.drain().then_inc(S("y_copied"), 1)
                    act.wait_ge(S("y_copied"), n + 1)
                    act.dma_start(y_rows[e * P:(e + 1) * P, :], yt[:, e % 2, :]).then_inc(S(f"y_written{e % 2}"), 16)

                x_in(0)
                for e in range(E + 1):
                    if e < E:
                        gate_exp(e)
                    if e + 1 < E:
                        x_in(e + 1)
                    if e >= 1:
                        y_out(e - 1)
                for q in range(2):
                    act.wait_ge(S(f"y_written{q}"), 16 * (E // 2) * (l + 1))
                barrier(act, "act")

                def overflow(k, count):
                    with act.If(count > k):
                        act.wait_ge(S(f"over_x_turned_{l}"), k + 1)
                        f_(xgT[:, 0, :, :], ps[:, 0:2, :].rearrange("p b (k n) -> p (b k) n", k=4), ACT.Copy)\
                            .then_inc(S(f"over_x_copied_{l}"), 1)
                        act.wait_ge(S(f"over_up_{l}"), k + 1)
                        f_(eh[:, 0, :], ps[:, 2, 0:F], ACT.Exp, scale=-1.0).then_inc(S(f"over_exp_{l}"), 1)
                        act.wait_ge(S(f"over_down_{l}"), k + 1)
                        f_(yt[:, 0, :], ps[:, 4:6, :].rearrange("p b n -> p (b n)"), ACT.Copy).then_inc(S(f"over_y_{l}"), 1)
                        act.wait_ge(S(f"over_y_{l}"), k + 1)
                        act.dma_start(y_rows[(E + k) * P:(E + k + 1) * P, :], yt[:, 0, :]).then_inc(S(f"over_written_{l}"), 16)
                        act.wait_ge(S(f"over_written_{l}"), 16 * (k + 1))
                        if k + 1 < NOVER:
                            overflow(k + 1, count)

                overflow(0, act.value_load(dyn[0:1, NOVER:NOVER + 1], min_val=0, max_val=NOVER))
                barrier(act, "act")
                root_of_rows(l + 1, l + 1 < DEPTH)
                if l + 1 < DEPTH:
                    to_features(l + 1, "ln2_g", "ln2_b", l)
            barrier(act, "act")

        @block_.vector
        def _(dve):
            v = nc.vector
            tt, ts_, stt = v.tensor_tensor, v.tensor_scalar, v.scalar_tensor_tensor

            def sig(name):
                dve.drain().then_inc(S(name), 1)

            def copy(key, dst, src):
                full(dve, key)
                rel(v.tensor_copy(dst, src), key, "D")

            def layer_norm(n, g, l):
                for h in range(2):
                    key = ("mean", n, h)
                    full(dve, key)
                    z = zT[:, :, SH[h]]
                    i = stt(z, bank(key)[:, 0:HALF].unsqueeze(1).to_broadcast([P, KD, HALF]), -1.0 / D, z, ALU.mult, ALU.add)
                    rel(i, key, "D")
                    sig("ln_centred")
                dve.wait_ge(S("ln_root"), n + 1)
                for k in range(KD):
                    stt(xT[:, k, :], zT[:, k, :], col(g, l, k), lnr, ALU.mult, ALU.mult)
                    sig("ln_scaled")

            def one_over_one_plus(x):
                ts_(x, x, 1.0, None, ALU.add)
                dve.drain()
                v.reciprocal(x, x)
                dve.drain()


            def row_sums(t):
                q = rows_of(t)
                for x in range(2):
                    v.bn_stats(bnst[0:q, t, x, :], tok(t, q, slice(512 * x, 512 * x + 512)))

            def variances():
                dve.drain()
                for t in range(TT):
                    q = rows_of(t)
                    v.bn_aggr(bnag[0:q, t, :], bnst[0:q, t, :, :])
                sig("rows_var")

            def norm_rows(n):
                variances()
                dve.wait_ge(S("rows_root"), n + 1)
                stt(shift, bnag[:, :, 0], -1.0, rstd, ALU.mult, ALU.mult)
                sig("rows_shift")
                for t in range(0, TT, 2):
                    q = rows_of(t)
                    ts_(tok(t, q), tok(t, q), bnag[0:q, t, 0:1], rstd[0:q, t:t + 1], ALU.subtract, ALU.mult)
                sig("rows_normed")

            def to_features(n, g, b, l):
                for k in range(0, KD, 2):
                    for x in range(2):
                        key = ("xin", n, k, x)
                        full(dve, key)
                        q = slice(0, 512) if x == 0 else slice(512, T)
                        rel(ts_(xT[:, k, q], bank(key)[:, 0:q.stop - q.start], col(g, l, k), col(b, l, k), ALU.mult, ALU.add), key, "D")

            v.memset(bnag, 1.0)
            dve.wait_ge(S("x_loaded"), 16 * 5)
            for t in range(TT):
                row_sums(t)
            dve.wait_ge(S("const_loaded"), 16)
            v.tensor_copy(tokid, cst("token"))
            sig("token_ids")
            norm_rows(0)
            dve.wait_ge(S("vec_ready"), 1)
            to_features(0, "ln_in_g", "ln_in_b", 0)

            for l in range(DEPTH):
                barrier(dve, "dve")
                def projected(j):
                    copy(("in", l, j, 0), projection(j)[:, SH[0]], bank(("in", l, j, 0))[:, 0:HALF])

                dve.wait_ge(S("rec_loaded"), 16 * 13 * (l + 1))
                dve.wait_ge(S("rec_zeroed"), l + 1)
                dve.wait_ge(S("mu_ready"), l + 1)
                for c in range(2):
                    outs = (uc[:, c, 0:TP], uc[:, c, TP:T].rearrange("p (s t) -> p s t", s=NSEQ))
                    for k in range(CONV):
                        for o, src in zip(outs, (mup[:, c, k:k + TP], mus[:, c, :, k:k + TS])):
                            w = col("conv_w", l, 2 * k + c)
                            if k == 0:
                                ts_(o, src, w, col("conv_b", l, c), ALU.mult, ALU.add)
                            else:
                                stt(o, src, w, o, ALU.mult, ALU.add)
                        dve.drain()
                sig("conv_sum")
                dve.wait_ge(S("rows_moved"), 32 * (l + 1))
                ts_(fg, fg, bif[:, DEPTH + l:DEPTH + l + 1], None, ALU.add)
                ts_(ig, ig, bif[:, l:l + 1], None, ALU.add)
                dve.drain()
                stt(rowe, fg, -1.0, fg, ALU.mult, ALU.max)
                sig("fgate_abs")
                for h in range(2):
                    key = ("ga", l, h)
                    full(dve, key)
                    rel(ts_(gb[:, SH[h]], bank(key)[:, 0:HALF], col("b_a", l), None, ALU.add), key, "D")
                dve.drain()
                stt(tmp1, gb, -1.0, gb, ALU.mult, ALU.max)
                sig("ga_abs")
                projected(2)
                dve.wait_ge(S("fgate_ln"), l + 1)
                stt(fg, fg, 0.0, rowe, ALU.min, ALU.subtract)
                dve.drain()
                v.tensor_tensor_scan(rowF, cst("reset", 4), fg, 0.0, ALU.mult, ALU.add)
                v.tensor_tensor_scan(rowm[:, 0:TP], fg[:, 0:TP], ig[:, 0:TP], 0.0, ALU.add, ALU.max)
                for s in range(NSEQ):
                    q = slice(TP + s * TS, TP + (s + 1) * TS)
                    v.tensor_tensor_scan(rowm[:, q], fg[:, q], ig[:, q], msS[0:4, s:s + 1], ALU.add, ALU.max)
                v.memset(ms0[0:4, 0:1], 0.0)
                dve.drain()
                tt(rowM, rowm, rowF, ALU.subtract)
                tt(rowt, ig, rowF, ALU.subtract)
                v.tensor_copy(ms0[0:4, 1:NCH], rowm[:, C - 1:TP - C:C])
                dve.drain()
                tt(rowwp[:, 0:TP].rearrange("p (c t) -> p c t", c=NCH), ms0[0:4, :].unsqueeze(2).to_broadcast([4, NCH, C]),
                   rowM[:, 0:TP].rearrange("p (c t) -> p c t", c=NCH), ALU.subtract)
                tt(rowwp[:, TP:T].rearrange("p (c t) -> p c t", c=NSEQ), msS[0:4, :].unsqueeze(2).to_broadcast([4, NSEQ, TS]),
                   rowM[:, TP:T].rearrange("p (c t) -> p c t", c=NSEQ), ALU.subtract)
                sig("rows_logs")
                for hd in range(MH):
                    ts_(negM[:, hd, :], rowM, cst("negid", 4)[:, hd:hd + 1], None, ALU.mult)
                projected(3)
                dve.wait_ge(S("ga_ln"), l + 1)
                stt(gb, gb, 0.0, tmp1, ALU.min, ALU.subtract)
                dve.drain()
                v.tensor_tensor_scan(tmp2, cst("reset"), gb, 0.0, ALU.mult, ALU.add)
                sig("ga_cum")
                projected(4)
                dve.wait_ge(S("conv_exp"), l + 1)
                one_over_one_plus(wpb)
                tt(uc, uc, wpb, ALU.mult)
                sig("conv_done")
                projected(5)
                dve.wait_ge(S("rows_exp"), l + 1)
                sig("rows_done")
                dve.wait_ge(S("ga_decay"), l + 1)
                dve.wait_ge(S("in_half_ready"), l + 1)
                for hd in range(GH):
                    r = slice(GK * hd, GK * hd + GK)
                    stt(qm[r, hd, :], gq[r, :], GK ** -0.5, geb[r, :], ALU.mult, ALU.mult)
                tt(kt, gk, gb, ALU.mult)
                sig("gla_inputs")
                projected(6)
                projected(7)
                for j in range(2):
                    v.tensor_copy(cns[:, j, :, DH:2 * DH], nst[:, j, :].unsqueeze(2).to_broadcast([P, NSEQ, DH]))
                sig("states_ready")
                dve.wait_ge(S("spread_ready"), l + 1)
                for j in range(2):
                    tt(mqw[:, j, :, :], mqm[:, j, :, :], wpb[:, j, :].unsqueeze(1).to_broadcast([P, 2, T]), ALU.mult)
                sig("mqw_done")
                def divide(c):
                    cs = slice(c * C, min((c + 1) * C, T))
                    num, den = nd[:, 0, :, cs], nd[:, 1, :, cs]
                    stt(den, den, -1.0, den, ALU.mult, ALU.max)
                    dve.drain()
                    tt(den, den, enmb[:, :, cs], ALU.max)
                    dve.drain()
                    v.reciprocal(den, den)
                    dve.drain()
                    tt(num, num, den, ALU.mult)
                    dve.drain()

                for c in range(NCH + 1):
                    smp = c == NCH
                    n = NS if smp else C
                    w = 4 * n
                    lastc = c * C + n - 1
                    key = ("ga_s", l, c)
                    full(dve, key)
                    rel(tt(am[0:n, 0:w], bank(key)[0:n, 0:w], cst("tri_s" if smp else "tri", n), ALU.mult), key, "D")
                    dve.wait_ge(S("w_ready"), (NCH + 1) * l + c + 1)
                    key = ("qk", l, c)
                    full(dve, key)
                    rel(tt(qkw[0:n, 0:w], bank(key)[0:n, 0:w], wd_[0:n, 0:w], ALU.mult), key, "D")
                    if smp:
                        v.tensor_reduce(ws[0:n, :], wd_[0:n, 0:w].rearrange("p (h s t) -> p h s t", h=4, s=NSEQ)[:, :, :, TS - 1], AX.X, ALU.add)
                        dve.drain()
                        wlast_ = ws[0:n, :].unsqueeze(2)
                    else:
                        wlast_ = wd_[0:n, 0:w].rearrange("p (h t) -> p h t", h=4)[:, :, n - 1:n]
                    key = ("ktok", l, c)
                    full(dve, key)
                    i = tt(kws[0:n, :, :], bank(key)[0:n, 0:256].rearrange("p (h d) -> p h d", h=MH), wlast_.to_broadcast([n, MH, DH]), ALU.mult)
                    rel(i, key, "D")
                    sig("kws_done")
                    late = late_halves(c)
                    if late[0][2] == 0:
                        projected(late[0][1])
                    seqm = cst("seqmask", NS).unsqueeze(2).to_broadcast([NS, NSEQ, DH])
                    if c:
                        divide(c - 1)
                    if c in (4, 5):
                        dve.wait_ge(S("gr_exp"), l + 1)
                        one_over_one_plus(mix[:, c, :])
                        tt(mix[:, c, :], mix[:, c, :], gr[:, c - 4, :], ALU.mult)
                    if c in (6, 7):
                        dve.wait_ge(S("mo_exp"), l + 1)
                        one_over_one_plus(mo[:, c - 6, :])
                    if smp:
                        drained_by_other(dve, ("gtok", l, c))
                        for hd in range(GH):
                            if hd >= 2:
                                dve.wait_ge(S("gla_vm_read"), (GH - 1) * l + hd - 1)
                            tt(vm[0:n, hd % 2, :].rearrange("p (s v) -> p s v", s=NSEQ),
                               gtok[0:n, hd * GV:(hd + 1) * GV].unsqueeze(1).to_broadcast([n, NSEQ, GV]), seqm, ALU.mult)
                            sig("gla_vmask")
                        key = ("gs", l, c)
                        full(dve, key)
                        rel(tt(sgs, sgs, bank(key).rearrange("p (s v) -> p s v", s=NSEQ), ALU.add), key, "D")
                        dve.drain()
                        tt(sgs, sgs, geb[:, TP + TS - 1:T:TS].unsqueeze(2).to_broadcast([P, NSEQ, GV]), ALU.mult)
                        sig("gla_state")
                        drained_by_other(dve, ("vtok", l, c))
                        for hd in range(MH):
                            if hd == 2:
                                dve.wait_ge(S("ml_vm_read"), 2 * l + 1)
                            if hd == 3:
                                full(dve, ("mu_c", l, 0))
                            tt(vm[0:n, hd % 2, :].rearrange("p (s v) -> p s v", s=NSEQ),
                               vaug[0:n, hd, 0:DH].unsqueeze(1).to_broadcast([n, NSEQ, DH]), seqm, ALU.mult)
                            sig("ml_vmask")
                            if hd in (1, 3):
                                j = hd // 2
                                wl = wpb[:, j, TP + TS - 1:T:TS].unsqueeze(2).to_broadcast([P, NSEQ, 2 * DH])
                                full(dve, ("mu_n", l, j))
                                tt(cns[:, j, :, :], cns[:, j, :, :], wl, ALU.mult)
                                dve.drain()
                                for x, nm in enumerate(("mu_c", "mu_n")):
                                    key = (nm, l, j)
                                    cv = cns[:, j, :, x * DH:(x + 1) * DH]
                                    rel(tt(cv, cv, bank(key).rearrange("p (s v) -> p s v", s=NSEQ), ALU.add), key, "D")
                        sig("ml_state")
                    else:
                        key = ("gs", l, c)
                        full(dve, key)
                        rel(tt(sg, sg, bank(key)[:, 0:GV], ALU.add), key, "D")
                        dve.drain()
                        ts_(sg, sg, geb[:, lastc:lastc + 1], None, ALU.mult)
                        sig("gla_state")
                        key = ("mu", l, c)
                        full(dve, key)
                        b = bank(key)
                        stt(cn[:, 0, :], cn[:, 0, :], wpb[:, 0, lastc:lastc + 1], b[:, 0:P], ALU.mult, ALU.add)
                        rel(stt(cn[:, 1, :], cn[:, 1, :], wpb[:, 1, lastc:lastc + 1], b[:, P:2 * P], ALU.mult, ALU.add), key, "D")
                        sig("ml_state")
                dve.wait_ge(S("chunks_out"), l + 1)
                divide(NCH)
                tt(nd[:, 0, :, :], nd[:, 0, :, :], mo, ALU.mult)
                sig("ml_h")
                for j in range(2):
                    for h in range(2):
                        key = ("mm_", l, j, h)
                        full(dve, key)
                        z = nd[:, 0, j, SH[h]]
                        rel(stt(z, bank(key)[:, 0:HALF], -1.0 / DH, z, ALU.mult, ALU.add), key, "D")
                sig("ml_centred")
                for j in range(2):
                    stt(mix[:, 4 + j, :], og[:, j, :], col("gla_norm", l), mix[:, 4 + j, :], ALU.mult, ALU.mult)
                dve.drain()
                dve.wait_ge(S("gla_root"), l + 1)
                tt(mix[:, 4:6, :], mix[:, 4:6, :], gv, ALU.mult)
                dve.wait_ge(S("latents_root"), l + 1)
                for k in range(2):
                    stt(cq[:, k, :], cq[:, k, :], col("q_norm", l, k), lnr[:, :], ALU.mult, ALU.mult)
                stt(ckv, ckv, col("kv_norm", l), ckv_root, ALU.mult, ALU.mult)
                dve.wait_ge(S("ml_root"), l + 1)
                for j in range(2):
                    stt(mix[:, 6 + j, :], nd[:, 0, j, :], col("ml_norm", l, j), mk[:, j, :], ALU.mult, ALU.mult)
                dve.drain()
                for j in range(2):
                    stt(mix[:, 6 + j, :], uc[:, j, :], col("ml_skip", l, j), mix[:, 6 + j, :], ALU.mult, ALU.add)
                barrier(dve, "dve")

                dve.wait_ge(S("pages_table_loaded"), 16 * 8 * (l + 1))
                ts_(idx, ptab, float(ROWS_PAGE), cst("rowrem")[:, l:l + 1], ALU.mult, ALU.add)
                sig("rows_to_gather")
                tt(kro[0:ROPE, :], small[ROPE:2 * ROPE, :], cst("sin")[ROPE:2 * ROPE, :], ALU.mult)
                tt(small[0:ROPE, :], small[0:ROPE, :], cst("cos")[0:ROPE, :], ALU.mult)
                dve.drain()
                tt(kro[0:ROPE, :], kro[0:ROPE, :], small[0:ROPE, :], ALU.add)
                sig("key_rotated")
                for m in range(6, 8):
                    for h in range(2):
                        copy(("q", l, m, h), qrb[:, m - 6, SH[h]], bank(("q", l, m, h))[:, 0:HALF])
                dve.wait_ge(S("qra_ready"), l + 1)
                dve.drain()
                for src, tab in ((qra, "cos"), (qrb, "sin")):
                    tt(src, src, cst(tab).unsqueeze(1).to_broadcast([P, 2, T]), ALU.mult)
                dve.drain()
                for a in range(4):
                    a_ = slice(32 * a, 32 * a + 32)
                    tt(qr0[0:ROPE, :, a:H:4].rearrange("p t c -> p c t"), qra[a_], qrb[a_], ALU.add)
                dve.wait_ge(S("qrM_zeroed"), l + 1)
                dve.drain()
                for a in range(4):
                    v.tensor_copy(qrM[32 * a:32 * a + 32, a, :, :], qr0[0:ROPE, TP:T, :])
                for hd in range(H // 2, H):
                    for h in range(2):
                        copy(("qlat", l, hd, h), qlat[:, SH[h], hd], bank(("qlat", l, hd, h))[:, 0:HALF])
                barrier(dve, "dve")

                for step in range(NQ + 3):
                    if step < NQ:
                        i_ = step
                        W = QT * (i_ + 1)
                        sl = i_ % NPB
                        for x, (a, z) in enumerate(((0, min(W, 512)), (512, W))):
                            if z <= a:
                                continue
                            full(dve, ("s", l, i_, x))
                            v.tensor_reduce(mxq[:, sl, x:x + 1], bank(("s", l, i_, x))[:, 0:z - a], AX.X, ALU.max)
                        dve.drain()
                        if W > 512:
                            tt(mxq[:, sl, 0:1], mxq[:, sl, 0:1], mxq[:, sl, 1:2], ALU.max)
                            dve.drain()
                        ts_(nmq[:, sl:sl + 1], mxq[:, sl, 0:1], -SCALE, None, ALU.mult)
                        sig("pq_max")
                    if 1 <= step <= NQ:
                        i_ = step - 1
                        W = QT * (i_ + 1)
                        sl = i_ % NPB
                        dve.wait_ge(S("pq_exp"), NQ * l + i_ + 1)
                        if W > 512:
                            tt(smq[:, sl, 0:1], smq[:, sl, 0:1], smq[:, sl, 1:2], ALU.add)
                            dve.drain()
                        v.reciprocal(rsq[:, sl:sl + 1], smq[:, sl, 0:1])
                        dve.drain()
                        ts_(pq[:, sl, 0:W], pq[:, sl, 0:W], rsq[:, sl:sl + 1], None, ALU.mult)
                        sig("pq_normed")
                    if 2 <= step <= NQ + 1 and step % 2 == 0:
                        prompt_pT(dve, l, step - 2, v.tensor_copy, "D")
                    if step >= 3:
                        i_ = step - 3
                        key = ("o", l, i_)
                        copy(key, qlat[:, QT * i_:QT * (i_ + 1), :],
                             bank(key)[:, 0:P].rearrange("p (t h) -> p t h", h=H))
                barrier(dve, "dve")

                def keys_turned(p_):
                    for s in range(2):
                        for q in (0, 2):
                            copy(("kT", l, p_, s, q), kT[:, s, q * 512:(q + 1) * 512], bank(("kT", l, p_, s, q)))
                        if s == 0:
                            copy(("krT", l, p_, 0), krT[:, 0, :], bank(("krT", l, p_, 0)))

                def maxima_of(p_):
                    for q in range(5):
                        key = ("ss", l, p_, q) if q < 4 else ("sn", l, p_)
                        full(dve, key)
                        v.tensor_reduce(mx[:, q:q + 1], bank(key)[:, 0:(512 if q < 4 else QT)], AX.X, ALU.max)
                    dve.drain()
                    v.tensor_reduce(mx[:, 5:6], mx[:, 0:5], AX.X, ALU.max)
                    dve.drain()
                    ts_(nmx[:, 0:1], mx[:, 5:6], -SCALE, None, ALU.mult)
                    sig("ps_max")

                keys_turned(0)
                maxima_of(0)
                for p_ in range(NSEQ // 2):
                    if p_ + 1 < NSEQ // 2:
                        keys_turned(p_ + 1)
                    dve.wait_ge(S("ps_exp"), l * (NSEQ // 2) + p_ + 1)
                    v.tensor_reduce(sums[:, 5:6], sums[:, 0:5], AX.X, ALU.add)
                    dve.drain()
                    v.reciprocal(rs[:, 0:1], sums[:, 5:6])
                    dve.drain()
                    ts_(psm, psm, rs[:, 0:1], None, ALU.mult)
                    sig("ps_normed")
                    for q in (0, 2):
                        copy(("psT", l, p_, q), psT[:, q * 512:(q + 1) * 512], bank(("psT", l, p_, q)))
                    copy(("psT", l, p_, 4), psT[0:QT, 16 * P:17 * P], bank(("psT", l, p_, 4))[0:QT, 0:P])
                    key = ("so", l, p_)
                    full(dve, key)
                    for s in range(2):
                        c0 = TP + (2 * p_ + s) * TS
                        i = v.tensor_copy(qlat[:, c0:c0 + TS, :],
                                          bank(key)[:, 64 * s:64 * s + 64].rearrange("p (t h) -> p t h", h=H))
                    rel(i, key, "D")
                    if p_ + 1 < NSEQ // 2:
                        maxima_of(p_ + 1)
                for j in range(4):
                    copy(("omla", l, j, 0), mix[:, j, SH[0]], bank(("omla", l, j, 0))[:, 0:HALF])
                barrier(dve, "dve")
                for m in range(KD):
                    for h in range(2):
                        key = ("out", l, m, h)
                        full(dve, key)
                        rel(stt(zT[:, m, SH[h]], xT[:, m, SH[h]], ALPHA, bank(key)[:, 0:HALF], ALU.mult, ALU.add), key, "D")
                layer_norm(l, "ln1_g", l)

                v.memset(sc, 1.0)
                sig("logits_zeroed")
                dve.wait_ge(S("logits_exp"), l + 1)
                one_over_one_plus(sc)
                tt(sel, sc, rbias[:, :].unsqueeze(1).to_broadcast([P, TT, E]), ALU.add)
                dve.drain()
                se = sel.rearrange("p t (g e) -> p t g e", e=4)
                hi1, lo1, hi2, lo2, ta, tb = g4
                e_ = [se[:, :, :, k] for k in range(4)]
                tt(hi1, e_[0], e_[1], ALU.max)
                tt(lo1, e_[0], e_[1], ALU.min)
                tt(hi2, e_[2], e_[3], ALU.max)
                tt(lo2, e_[2], e_[3], ALU.min)
                dve.drain()
                tt(ta, hi1, hi2, ALU.min)
                tt(tb, lo1, lo2, ALU.max)
                tt(hi1, hi1, hi2, ALU.max)
                dve.drain()
                tt(ta, ta, tb, ALU.max)
                dve.drain()
                tt(hi1, hi1, ta, ALU.add)
                dve.drain()

                def first_max(x, mx_, out, rank, n):
                    v.tensor_reduce(mx_, x, AX.X, ALU.max)
                    dve.drain()
                    tt(out, x, mx_.unsqueeze(2).to_broadcast([P, TT, n]), ALU.is_equal)
                    dve.drain()
                    tt(out, out, cst(rank).unsqueeze(1).to_broadcast([P, TT, n]), ALU.mult)
                    dve.drain()
                    v.tensor_reduce(mx_, out, AX.X, ALU.max)
                    dve.drain()
                    tt(out, out, mx_.unsqueeze(2).to_broadcast([P, TT, n]), ALU.is_equal)
                    dve.drain()

                first_max(hi1, g1[0], lo1, "rank4", 4)
                ts_(lo2, lo1, -1.0, -NEG, ALU.add, ALU.mult)
                dve.drain()
                g_of = lo1.unsqueeze(3).to_broadcast([P, TT, 4, 4])
                tt(r3.rearrange("p t (g e) -> p t g e", e=4), se, g_of, ALU.mult)
                dve.drain()
                tt(r3.rearrange("p t (g e) -> p t g e", e=4), r3.rearrange("p t (g e) -> p t g e", e=4),
                   lo2.unsqueeze(3).to_broadcast([P, TT, 4, 4]), ALU.add)
                dve.drain()
                first_max(r3, g1[1], r1, "rank16", E)
                stt(r3, r1, 2 * NEG, r3, ALU.mult, ALU.add)
                dve.drain()
                first_max(r3, g1[2], r2, "rank16", E)
                for x, oh in enumerate((r1, r2)):
                    tt(r3, oh, sc, ALU.mult)
                    dve.drain()
                    v.tensor_reduce(gate[:, x, :], r3, AX.X, ALU.add)
                    dve.drain()
                tt(g1[0], gate[:, 0, :], gate[:, 1, :], ALU.add)
                dve.drain()
                v.reciprocal(g1[0], g1[0])
                dve.drain()
                tt(gate, gate, g1[0].unsqueeze(1).to_broadcast([P, 2, TT]), ALU.mult)
                vld = cst("valid").unsqueeze(2).to_broadcast([P, TT, E])
                tt(r1, r1, vld, ALU.mult)
                tt(r2, r2, vld, ALU.mult)
                dve.drain()
                tt(r4, r1, r2, ALU.add)
                sig("onehots")
                for t in range(TT):
                    q = rows_of(t)
                    copy(("xt", l, t, 0), tok(t, q, slice(0, 512)), bank(("xt", l, t, 0))[0:q, :])
                sig("xt_other_half")
                key = ("rank", l)
                full(dve, key)
                rk = bank(key)[:, 0:TT * E].rearrange("p (t e) -> p t e", e=E)
                tot = bank(key)[:, TT * E:(TT + 1) * E]
                ts_(ov, tot, float(P), None, ALU.is_gt)
                dve.drain()
                for k in range(2, -(-T // P)):
                    stt(ov, tot, float(P * k), ov, ALU.is_gt, ALU.add)
                    dve.drain()
                v.tensor_tensor_scan(ovi, ones[:, 0:E], ov, 0.0, ALU.mult, ALU.add)
                ts_(r3, rk, float(P), None, ALU.is_ge)
                dve.drain()
                tt(ob, ovi, ov, ALU.subtract)
                dve.drain()
                stt(ob, ob, float(P), cst("over_slot"), ALU.mult, ALU.add)
                dve.drain()
                tt(r3, r3, ob.unsqueeze(1).to_broadcast([P, TT, E]), ALU.mult)
                dve.drain()
                rel(tt(r3, rk, r3, ALU.add), key, "D")
                dve.drain()
                tt(r3, r3, cst("expert_slot").unsqueeze(1).to_broadcast([P, TT, E]), ALU.add)
                dve.drain()
                for x, oh in enumerate((r1, r2)):
                    tt(oh, oh, r3, ALU.mult)
                    dve.drain()
                    v.tensor_reduce(slotf[:, x, :], oh, AX.X, ALU.add)
                dve.drain()
                v.tensor_copy(slot, slotf)
                sig("slots_ready")
                tt(tcmp, ovi.unsqueeze(1).to_broadcast([P, NOVER, E]), cst("tile_no").unsqueeze(2).to_broadcast([P, NOVER, E]), ALU.is_le)
                dve.drain()
                v.tensor_reduce(tef[:, 0:NOVER], tcmp, AX.X, ALU.add)
                dve.drain()
                ts_(dyn[:, 0:NOVER], tef[:, 0:NOVER], float(E - 1), None, ALU.min)
                v.tensor_copy(dyn[:, NOVER:NOVER + 1], ovi[:, E - 1:E])
                sig("overflow_known")
                dve.wait_ge(S("xt_half"), l + 1)
                dve.wait_ge(S("x_rows_written"), 32 * (l + 1))
                for t in range(TT):
                    q = rows_of(t)
                    ts_(tok(t, q), tok(t, q), ALPHA, None, ALU.mult)

                def gated(e_h, hg, hu, out):
                    ts_(e_h, e_h, 1.0, None, ALU.add)
                    dve.drain()
                    v.reciprocal(e_h, e_h)
                    dve.drain()
                    tt(e_h, hg, e_h, ALU.mult)
                    dve.drain()
                    return tt(out, hu, e_h, ALU.mult)

                def hidden(e):
                    dve.wait_ge(S("hg_exp"), l * E + e + 1)
                    key = ("up", l, e)
                    b = bank(key)
                    rel(gated(eh[:, e % 2, :], b[:, 0:F], b[:, F:2 * F], hh[:, e % 2, :]), key, "D")
                    sig("h_done")

                for e in range(E + 1):
                    if e >= 1:
                        key = ("hT", l, e - 1)
                        copy(key, hT[:, (e - 1) % 2, :, :], bank(key)[:, 0:2 * P].rearrange("p (f n) -> p f n", f=2))
                    if e < E:
                        hidden(e)
                barrier(dve, "dve")

                def overflow(k, count):
                    with dve.If(count > k):
                        dve.wait_ge(S(f"over_exp_{l}"), k + 1)
                        gated(eh[:, 0, :], ps[:, 2, 0:F], ps[:, 2, F:2 * F], hh[:, 0, :]).then_inc(S(f"over_h_{l}"), 1)
                        dve.wait_ge(S(f"over_h_turned_{l}"), k + 1)
                        v.tensor_copy(hT[:, 0, :, :], ps[:, 3, 0:2 * P].rearrange("p (f n) -> p f n", f=2)).then_inc(S(f"over_h_copied_{l}"), 1)
                        if k + 1 < NOVER:
                            overflow(k + 1, count)

                overflow(0, dve.value_load(dyn[0:1, NOVER:NOVER + 1], min_val=0, max_val=NOVER))
                barrier(dve, "dve")
                for t in range(TT):
                    q = rows_of(t)
                    for x in range(2):
                        n = 2 * t + x
                        dve.wait_ge(S(f"y_fetched{n}"), 16 * (l + 1))
                        stt(tok(t, q), yg[0:q, n, :], gate[0:q, x, t:t + 1], tok(t, q), ALU.mult, ALU.add)
                        dve.drain()
                    row_sums(t)
                if l + 1 < DEPTH:
                    norm_rows(l + 1)
                    to_features(l + 1, "ln2_g", "ln2_b", l)
                else:
                    variances()
                    dve.wait_ge(S("ln_rows_loaded"), 32)
                    for t in range(TT):
                        q = rows_of(t)
                        stt(tok(t, q), tok(t, q), bnag[0:q, t, 0:1], lnrow[0:q, 0, :], ALU.subtract, ALU.mult)
                    dve.wait_ge(S("rows_root"), l + 2)
                    for t in range(TT):
                        q = rows_of(t)
                        dve.drain()
                        stt(tok(t, q), tok(t, q), rstd[0:q, t:t + 1], lnrow[0:q, 1, :], ALU.mult, ALU.add)
                        sig("y_ready")
            barrier(dve, "dve")

        @block_.gpsimd
        def _(pool):
            g = nc.gpsimd
            g.memset(vecrows[:, :], 0.0)
            g.memset(zero_ids, 0)
            g.memset(over[:, 0:D], 0.0)
            pool.drain().then_inc(S("vec_zeroed"), 1)
            for l in range(DEPTH):
                barrier(pool, "pool")
                g.memset(wsm[:, :, 80:96], 0.0)
                for z in (wqk, qm, mqm, mup[:, :, 0:CONV - 1], sg, cn):
                    g.memset(z, 0.0)
                g.memset(vaug[:, :, DH:2 * DH], 1.0)
                pool.drain().then_inc(S("rec_zeroed"), 1)
                barrier(pool, "pool")
                g.memset(qrM, 0.0)
                pool.drain().then_inc(S("qrM_zeroed"), 1)
                barrier(pool, "pool")
                for p_ in range(NSEQ // 2):
                    if p_ == 0:
                        pool.wait_ge(S("rows_to_gather"), l + 1)
                    if p_ == 1:
                        barrier(pool, "pool")
                    if p_ >= 2:
                        pool.wait_ge(filled, index[("so", l, p_ - 2)] + 1)
                    for s in range(2):
                        sq_ = 2 * p_ + s
                        off = bass.IndirectOffsetOnAxis(ap=idx[:, sq_:sq_ + 1], axis=0)
                        g.indirect_dma_start(kgs[p_ % 2][:, s, :], None,
                                             I["cache_kv_latent"].rearrange("l n (a b) r -> (l n a) (b r)", b=KEYS_ROW), off)\
                            .then_inc(S(f"pages{s}_{p_ % 2}"), 16)
                        g.indirect_dma_start(krgs[p_ % 2][:, s, :], None,
                                             I["cache_k_rope"].rearrange("l n (a b) r -> (l n a) (b r)", b=KEYS_ROW), off)\
                            .then_inc(S(f"pages{s}_{p_ % 2}"), 16)
                barrier(pool, "pool")

                pool.wait_ge(S("slots_ready"), l + 1)
                if l == 0:
                    pool.wait_ge(S("token_ids"), 1)
                    pool.wait_ge(S("slots_cleared"), 16)

                def rows_at(ids):
                    return bass.IndirectOffsetOnAxis(ap=ids, axis=0)

                for t in range(TT):
                    q = rows_of(t)
                    for x in range(2):
                        g.indirect_dma_start(slot_token, rows_at(slot[0:q, x, t:t + 1]), tokid[0:q, t:t + 1], None)\
                            .then_inc(S("ids_scattered"), 16)
                pool.wait_ge(S("ids_scattered"), 16 * 2 * TT * (l + 1))
                pool.dma_start(fetch, slot_token.rearrange("(i p) a -> p (i a)", p=P), allow_slow_non_contiguous=True)\
                    .then_inc(S("ids_fetched"), 16)
                pool.wait_ge(S("ids_fetched"), 16 * (l + 1))
                pool.wait_ge(S("x_rows_written"), 32 * (l + 1))
                for e in range(E):
                    if e >= 3:
                        pool.wait_ge(filled, index[("xg", l, e - 3, 1)] + 1)
                    g.indirect_dma_start(xg[:, e % 3, :], None, x_rows, rows_at(fetch[:, e:e + 1])).then_inc(S(f"x_fetched{e % 3}"), 16)

                def fetch_overflow(k):
                    g.indirect_dma_start(xg[:, 1, :], None, x_rows, rows_at(fetch[:, E + k:E + k + 1])).then_inc(S(f"over_fetched_{l}"), 16)

                pool.wait_ge(S("overflow_known"), l + 1)
                count = pool.value_load(dyn[0:1, NOVER:NOVER + 1], min_val=0, max_val=NOVER)
                with pool.If(count > 0):
                    pool.wait_ge(filled, index[("xg", l, E - 3, 1)] + 1)
                    fetch_overflow(0)
                barrier(pool, "pool")

                def overflow(k, count):
                    with pool.If(count > k):
                        if k:
                            pool.wait_ge(S(f"over_x_turned_{l}"), k)
                            fetch_overflow(k)
                        if k + 1 < NOVER:
                            overflow(k + 1, count)

                overflow(0, count)
                barrier(pool, "pool")
                for t in range(TT):
                    q = rows_of(t)
                    for x in range(2):
                        n = 2 * t + x
                        g.indirect_dma_start(yg[0:q, n, :], None, y_rows, rows_at(slot[0:q, x, t:t + 1])).then_inc(S(f"y_fetched{n}"), 16)
            barrier(pool, "pool")

        @block_.sync
        def _(sp):
            def ld(dst, src, name):
                return sp.dma_start(dst, src, allow_slow_non_contiguous=True).then_inc(S(name), 16)

            def load_slot(u):
                per = len(CHUNKS) + KD
                l, j = u // per, u % per
                if u >= NSLOT:
                    sp.wait_ge(filled, index[wlast[u - NSLOT]] + 1)
                if j < len(CHUNKS):
                    c0 = COL[CHUNKS[j][0]] + P * CHUNKS[j][1]
                    src = I["w_in"][l][:, c0:c0 + P]
                else:
                    m = j - len(CHUNKS)
                    src = I["w_out"][l][:, m * P:(m + 1) * P]
                ld(wslot[:, u % NSLOT, :, :], src.rearrange("(k p) c -> p k c", p=P), f"wslot{u % NSLOT}")

            x = I["x_prompt"][0]
            full4 = zflat[:, 0:4 * D].rearrange("p (t d) -> p t d", d=D)
            ld(tok(0)[0:N_META], I["meta_tokens"], "x_loaded")
            ld(tok(0)[N_META:P], x[0:P - N_META, :], "x_loaded")
            ld(full4[:, 1:4, :], x[P - N_META:4 * P - N_META, :].rearrange("(t p) d -> p t d", p=P), "x_loaded")
            ld(tok(4)[0:N_META], x[4 * P - N_META:SEQ, :], "x_loaded")
            ld(tok(4)[N_META:N_META + NS], I["x_sample"].rearrange("s t d -> (s t) d"), "x_loaded")
            ld(const[:, :], I["consts"], "const_loaded")
            sp.wait_ge(S("vec_zeroed"), 1)
            src = dict(q_norm="mla_q_norm", kv_norm="mla_kv_norm", b_a="gla_b_a", conv_w="ml_conv_w", conv_b="ml_conv_b",
                       ml_norm="ml_norm", ml_skip="ml_skip", ln1_g="ln1_g", ln1_b="ln1_b", ln2_g="ln2_g", ln2_b="ln2_b")
            for name, w in VEC:
                r = VROW[name]
                if name == "gla_norm":
                    for a in range(2):
                        ld(vecrows[r:r + DEPTH, 64 * a:64 * a + 64], I["gla_norm"], "vec_loaded")
                elif name == "conv_w":
                    ld(vecrows[r:r + DEPTH * w, :], I["ml_conv_w"].rearrange("l i (k p) -> (l i k) p", p=P), "vec_loaded")
                else:
                    ld(vecrows[r:r + DEPTH * w, :], I[src[name]].rearrange("l (k p) -> (l k) p", p=P), "vec_loaded")
            for name in ("ln_in_g", "ln_in_b"):
                r = VROW[name]
                ld(vecrows[r:r + KD, :], I[name].rearrange("(k p) -> k p", p=P), "vec_loaded")
            ld(bif[:, 0:DEPTH], I["ml_b_i"].rearrange("l h -> h l"), "vec_loaded")
            ld(bif[:, DEPTH:2 * DEPTH], I["ml_b_f"].rearrange("l h -> h l"), "vec_loaded")
            for u in range(NSLOT):
                load_slot(u)
            ld(y_rows[E * P:NTILE * P, :].rearrange("(i p) d -> p i d", p=P), over[:, 0:D].unsqueeze(1).to_broadcast([P, NOVER, D]), "rows_cleared")
            ld(slot_token.rearrange("(i p) a -> i (p a)", p=P), zero_ids, "slots_cleared")
            ld(routerw[:, :, :], I["router_w"].rearrange("(k p) e -> p k e", p=P), "router_loaded")
            ld(rbias[:, :], I["router_bias"].rearrange("(a e) -> a e", a=1).to_broadcast([P, E]), "router_loaded")

            per = len(CHUNKS) + KD
            sp.wait_ge(S("rows_cleared"), 16)
            for l in range(DEPTH):
                barrier(sp, "sp")
                w = I["w_in"][l].rearrange("(k p) c -> p k c", p=P)
                kr = COL["kr"]
                for d0, s0, n in ((0, kr, ROPE), (32, kr + 16, 16), (48, kr, 16), (64, COL["ga"], GR), (96, COL["mi"], 2 * MH)):
                    ld(wsm[:, :, d0:d0 + n], w[:, :, s0:s0 + n], "wsmall_loaded")
                ld(wa[64:64 + GR, :], I["gla_w_a"][l], "rec_loaded")
                for c in range(2):
                    for k in range(CONV - 1):
                        ld(mus[:, c, :, k], I["state_mlstm_conv"][l][:, k, c * P:(c + 1) * P].rearrange("s p -> p s"), "rec_loaded")
                ld(sgs, I["state_gla"][l].rearrange("s h k v -> (h k) s v"), "rec_loaded")
                for j in range(2):
                    ld(cns[:, j, :, 0:DH], I["state_mlstm_C"][l][:, 2 * j:2 * j + 2].rearrange("s h d v -> (h d) s v"), "rec_loaded")
                    ld(nst[:, j, :], I["state_mlstm_n"][l][:, 2 * j:2 * j + 2].rearrange("s h d -> (h d) s"), "rec_loaded")
                ld(msS[0:4, :], I["state_mlstm_m"][l].rearrange("s h -> h s"), "rec_loaded")
                sp.wait_ge(S("rec_zeroed"), l + 1)
                for qk, nm in enumerate(("ml_w_q", "ml_w_k")):
                    for hd in range(MH):
                        a = slice(64 * (hd % 2), 64 * (hd % 2) + 64)
                        ld(wqk[a, qk, hd // 2, a], I[nm][l, hd], "wqk_loaded")
                sp.wait_ge(S("small_ready"), l + 1)
                ld(ig, small[96:100, :], "rows_moved")
                ld(fg, small[100:104, :], "rows_moved")
                for j in range(NSLOT, len(CHUNKS) + NSLOT):
                    load_slot(l * per + j)
                sp.wait_ge(S("gla_state"), (NCH + 1) * (l + 1))
                sp.wait_ge(S("ml_state"), (NCH + 1) * (l + 1))
                uq = I["mla_w_uq"][l].rearrange("(k p) (h c) -> k p h c", p=P, h=H)
                for k in range(2):
                    for d0, s0, n, st in ((0, 0, NOPE, 64), (512, NOPE, ROPE, 32), (768, NOPE + 16, 16, 32), (784, NOPE, 16, 32)):
                        d = wuq[:, k, d0 - d0 % 32:(d0 - d0 % 32) + H * st].rearrange("p (h c) -> p h c", h=H)
                        ld(d[:, :, d0 % 32:d0 % 32 + n], uq[k][:, :, s0:s0 + n], "att_loaded")
                ukv = I["mla_w_ukv"][l].rearrange("r (h c) -> r h c", h=H)
                for x in range(2):
                    ld(wukv[:, 512 * x:512 * (x + 1)].rearrange("p (h c) -> p h c", h=H), ukv[:, :, 64 * x:64 * (x + 1)], "att_loaded")
                for r in range(ROWS_PAGE):
                    ld(ptab[r:P:ROWS_PAGE, :], I["page_table"].rearrange("s g -> g s"), "pages_table_loaded")
                n_out = 0
                for dst, srcv in (
                        (O["p_gla"][l, 0].rearrange("h k v -> (h k) v"), sg),
                        (O["s_gla"][l].rearrange("s h k v -> (h k) s v"), sgs),
                        (O["p_m"][l, 0].rearrange("(h a) -> h a", a=1), rowm[:, TP - 1:TP]),
                        (O["s_m"][l].rearrange("s h -> h s"), rowm[:, TP + TS - 1:T:TS])):
                    ld(dst, srcv, "states_out")
                    n_out += 1
                for j in range(2):
                    hs = slice(2 * j, 2 * j + 2)
                    fs = slice(j * P, (j + 1) * P)
                    for dst, srcv in (
                            (O["p_C"][l, 0, hs].rearrange("h d v -> (h d) v"), cn[:, j, 0:DH]),
                            (O["p_n"][l, 0, hs].rearrange("h (d a) -> (h d) a", a=1), cn[:, j, DH:DH + 1]),
                            (O["s_C"][l][:, hs].rearrange("s h d v -> (h d) s v"), cns[:, j, :, 0:DH]),
                            (O["s_n"][l][:, hs].rearrange("s h d -> (h d) s"), cns[:, j, :, DH]),
                            (O["p_conv"][l, 0][:, fs].rearrange("i p -> p i"), mup[:, j, TP:TP + CONV - 1]),
                            *((O["s_conv"][l][:, k, fs].rearrange("s p -> p s"), mus[:, j, :, TS + k]) for k in range(CONV - 1))):
                        ld(dst, srcv, "states_out")
                        n_out += 1
                sp.wait_ge(S("states_out"), 16 * n_out * (l + 1))
                barrier(sp, "sp")

                sp.wait_ge(S("ctok_ready"), l + 1)
                for nm, a, z in (("kv", 0, LAT), ("kr", LAT, LAT + ROPE)):
                    ld(O["p_" + nm][l, 0, 0:4 * P].rearrange("(t p) r -> p t r", p=P), ctok[:, 0:4, a:z], "cache_rows_out")
                    ld(O["p_" + nm][l, 0, 4 * P:TP], ctok[0:QT, 4, a:z], "cache_rows_out")
                    ld(O["s_" + nm][l].rearrange("(a b) t r -> (b t) a r", b=2), ctok[0:QT, 5:9, a:z], "cache_rows_out")
                barrier(sp, "sp")
                barrier(sp, "sp")
                sp.wait_ge(S("cache_rows_out"), 96 * (l + 1))
                barrier(sp, "sp")

                def load_expert(e):
                    if e >= 2:
                        sp.wait_ge(filled, index[("up", l, e - 2)] + 1)
                    for x, nm in enumerate(("moe_w_gate", "moe_w_up")):
                        ld(wgu[:, e % 2, :, x * F:(x + 1) * F], I[nm][l, e].rearrange("(k p) f -> p k f", p=P), f"wgu{e % 2}")
                    if e >= 2:
                        sp.wait_ge(filled, index[("dn", l, e - 2, 1)] + 1)
                    ld(wdn[:, e % 2, :, :], I["moe_w_down"][l, e].rearrange("(k p) d -> p k d", p=P), f"wdn{e % 2}")

                load_expert(0)
                load_expert(1)
                for j in range(NSLOT, KD):
                    load_slot(l * per + len(CHUNKS) + j)
                if l == DEPTH - 1:
                    for a, nm in enumerate(("ln2_g", "ln2_b")):
                        ld(lnrow[:, a, :], I[nm][l:l + 1, :].to_broadcast([P, D]), "ln_rows_loaded")
                sp.wait_ge(S("xt_half"), l + 1)
                sp.wait_ge(S("xt_other_half"), l + 1)
                ld(x_rows[0:4 * P, :].rearrange("(t p) d -> p t d", p=P), full4, "x_rows_written")
                ld(x_rows[4 * P:T, :], tok(4, LAST), "x_rows_written")
                for e in range(2, E):
                    load_expert(e)

                def load_overflow(k):
                    e = sp.value_load(dyn[0:1, k:k + 1], min_val=0, max_val=E - 1)
                    for x, nm in enumerate(("moe_w_gate", "moe_w_up")):
                        ld(wgu[:, 0, :, x * F:(x + 1) * F], I[nm][l][bass.ds(e, 1)].rearrange("a (k p) f -> p (a k) f", p=P), f"over_weights_{l}")
                    ld(wdn[:, 0, :, :], I["moe_w_down"][l][bass.ds(e, 1)].rearrange("a (k p) d -> p (a k) d", p=P), f"over_weights_{l}")

                sp.wait_ge(S("overflow_known"), l + 1)
                count = sp.value_load(dyn[0:1, NOVER:NOVER + 1], min_val=0, max_val=NOVER)
                with sp.If(count > 0):
                    sp.wait_ge(filled, index[("dn", l, E - 2, 1)] + 1)
                    load_overflow(0)
                barrier(sp, "sp")

                def overflow(k, count):
                    with sp.If(count > k):
                        if k:
                            sp.wait_ge(S(f"over_down_{l}"), k)
                            load_overflow(k)
                        if k + 1 < NOVER:
                            overflow(k + 1, count)

                overflow(0, count)
                barrier(sp, "sp")
                if l + 1 < DEPTH:
                    for j in range(NSLOT):
                        load_slot((l + 1) * per + j)
            y = O["y_prompt"][0]
            sp.wait_ge(S("y_ready"), 1)
            ld(y[0:P - N_META, :], tok(0)[N_META:P], "y_out")
            for t in range(1, 4):
                sp.wait_ge(S("y_ready"), t + 1)
                ld(y[t * P - N_META:(t + 1) * P - N_META, :], tok(t), "y_out")
            sp.wait_ge(S("y_ready"), TT)
            ld(y[4 * P - N_META:SEQ, :], tok(4)[0:N_META], "y_out")
            ld(O["y_sample"].rearrange("s t d -> (s t) d"), tok(4)[N_META:N_META + NS], "y_out")
            sp.wait_ge(S("y_out"), 16 * (TT + 1))
            barrier(sp, "sp")


_INS = ["x_prompt", "x_sample", "cache_kv_latent", "cache_k_rope", "state_gla", "state_mlstm_C", "state_mlstm_n",
        "state_mlstm_m", "state_mlstm_conv", "page_table", "meta_tokens", "ln_in_g", "ln_in_b", "w_in", "mla_q_norm",
        "mla_w_uq", "mla_kv_norm", "mla_w_ukv", "gla_w_a", "gla_b_a", "gla_norm", "ml_conv_w", "ml_conv_b", "ml_w_q", "ml_w_k",
        "ml_b_i", "ml_b_f", "ml_norm", "ml_skip", "w_out", "ln1_g", "ln1_b", "ln2_g", "ln2_b", "router_w", "router_bias",
        "moe_w_gate", "moe_w_up", "moe_w_down"]


def _states(b, rows):
    return [(DEPTH, b, rows, LAT), (DEPTH, b, rows, ROPE), (DEPTH, b, GH, GK, GV), (DEPTH, b, MH, DH, DH), (DEPTH, b, MH, DH),
            (DEPTH, b, MH), (DEPTH, b, CONV - 1, MH * DH)]


_STATE = ["kv", "kr", "gla", "C", "n", "m", "conv"]
_OUTS = [("y_prompt", (1, SEQ, D)), ("y_sample", (NSEQ, TS, D))]
_OUTS += [("p_" + n, s) for n, s in zip(_STATE, _states(1, TP))] + [("s_" + n, s) for n, s in zip(_STATE, _states(NSEQ, TS))]


def kernel(**inputs):
    import numpy as _np
    import concourse.bacc as _bacc
    from concourse import mybir as _mybir
    from concourse.bass_utils import run_bass_kernel_spmd as _run

    nc = _bacc.Bacc("TRN2", target_bir_lowering=False, num_devices=1)
    table, at = shape_constants()
    arrays, ins, outs = {"in_consts": table}, {}, {}
    ins["consts"] = nc.dram_tensor("in_consts", table.shape, _mybir.dt.float32, kind="ExternalInput").ap()
    for name in _INS:
        a = _np.ascontiguousarray(inputs[name])
        arrays["in_" + name] = a
        ins[name] = nc.dram_tensor("in_" + name, a.shape, _mybir.dt.from_np(a.dtype), kind="ExternalInput").ap()
    for name, shape in _OUTS:
        outs[name] = nc.dram_tensor("out_" + name, shape, _mybir.dt.float32, kind="ExternalOutput").ap()
    build(nc, ins, outs, at, table.shape[1])
    r = _run(nc, [arrays], core_ids=[0])
    return tuple(r.results[0]["out_" + name] for name, _ in _OUTS)
```
